# Optimizing a Trainium2 kernel written in Bass

```python
import jax, jax.numpy as jnp
from jax import lax
import numpy as np

D_MODEL = 1024
BATCH = 1
SEQ = 512
DEPTH = 1
DEC_BATCH = 8
DEC_SEQ = 4
PAST_LEN = 512
PAGE_SIZE = 128

HEAD_DIM = 64
ATTN_PATTERNS = ((128, 1), (512, 4), (2048, 16))
N_ATTN_GROUPS = len(ATTN_PATTERNS)
HEADS_PER_GROUP = 4
N_HEADS = N_ATTN_GROUPS * HEADS_PER_GROUP
ATTN_WIDTH = N_HEADS * HEAD_DIM
ATTN_MIX_WIDTH = HEADS_PER_GROUP * HEAD_DIM
ROT_DIM = HEAD_DIM // 4
ROPE_THETA = 500000.0
CONV_CH = D_MODEL // 2
CONV_WIDTH = 31
N_BRANCHES = 2
IN_WIDTH = 3 * ATTN_WIDTH + 2 * CONV_CH + N_BRANCHES * D_MODEL
N_EXPERT_GROUPS = 4
EXPERTS_PER_GROUP = 8
N_EXPERTS = N_EXPERT_GROUPS * EXPERTS_PER_GROUP
TOP_K = 2
D_EXPERT = D_MODEL // 2
MOE_BLOCK = 128
DN_ALPHA = (2 * DEPTH) ** 0.25
DN_BETA = (8 * DEPTH) ** -0.25
LN_EPS = 1e-5
SCALE = HEAD_DIM ** -0.5
NEG_INF = -1e30

kernel_name = "dilated_conv_hier_moe_decoder_step"

def layer_norm(x, g, b):
    xf = x.astype(jnp.float32)
    mu = jnp.mean(xf, -1, keepdims=True)
    var = jnp.mean(jnp.square(xf - mu), -1, keepdims=True)
    return ((xf - mu) * lax.rsqrt(var + LN_EPS) * g.astype(jnp.float32) + b.astype(jnp.float32)).astype(x.dtype)

def partial_rotary(x, pos):
    half = ROT_DIM // 2
    inv_freq = ROPE_THETA ** (-jnp.arange(half, dtype=jnp.float32) / half)
    ang = pos.astype(jnp.float32)[:, None] * inv_freq[None, :]
    cos, sin = jnp.cos(ang)[:, None, :], jnp.sin(ang)[:, None, :]
    xr = x[..., :ROT_DIM].astype(jnp.float32)
    x1, x2 = xr[..., :half], xr[..., half:]
    rot = jnp.concatenate([x1 * cos - x2 * sin, x2 * cos + x1 * sin], -1).astype(x.dtype)
    return jnp.concatenate([rot, x[..., ROT_DIM:]], -1)

def project_inputs(x, w_in, b_in, pos):
    z = x @ w_in + b_in
    sizes = [ATTN_WIDTH] * 3 + [CONV_CH, CONV_CH, N_BRANCHES * D_MODEL]
    q, k, v, ua, ub, gate_logits = jnp.split(z, np.cumsum(sizes)[:-1].tolist(), axis=-1)
    hs = x.shape[:-1] + (N_HEADS, HEAD_DIM)
    q = partial_rotary(q.reshape(hs), pos)
    k = partial_rotary(k.reshape(hs), pos)
    u = ua * jax.nn.sigmoid(ub)
    return q, k, v.reshape(hs), u, gate_logits

def masked_softmax_stats(s):
    m = jnp.max(s, -1, keepdims=True)
    p = jnp.exp(s - m)
    l = jnp.sum(p, -1, keepdims=True)
    return p / l, (m + jnp.log(l))[..., 0]

def dilated_group_prompt(q, k, v, dil, steps):
    B, S, H, E = q.shape
    L = S // dil
    nb = -(-L // steps)
    Lp = nb * steps

    def to_blocks(t):
        t = t.reshape(B, L, dil, H, E).transpose(0, 2, 1, 3, 4)
        t = jnp.pad(t, ((0, 0), (0, 0), (0, Lp - L), (0, 0), (0, 0)))
        return t.reshape(B, dil, nb, steps, H, E)

    qb, kb, vb = to_blocks(q), to_blocks(k), to_blocks(v)

    def with_prev(t):
        prev = jnp.pad(t[:, :, :-1], ((0, 0), (0, 0), (1, 0), (0, 0), (0, 0), (0, 0)))
        return jnp.concatenate([prev, t], axis=3)

    kw, vw = with_prev(kb), with_prev(vb)
    s = jnp.einsum('bdnqhe,bdnkhe->bdnhqk', qb, kw, preferred_element_type=jnp.float32) * SCALE
    qi = jnp.arange(steps)[:, None]
    kj = jnp.arange(2 * steps)[None, :]
    band = (kj >= qi) & (kj <= qi + steps)
    has_prev = (jnp.arange(nb) > 0)[:, None, None] | (kj >= steps)[None]
    mask = (band[None] & has_prev)[:, None]
    p, lse = masked_softmax_stats(jnp.where(mask, s, NEG_INF))
    o = jnp.einsum('bdnhqk,bdnkhe->bdnqhe', p, vw.astype(jnp.float32))
    o = o.reshape(B, dil, Lp, H, E)[:, :, :L].transpose(0, 2, 1, 3, 4).reshape(B, S, H, E)
    lse = jnp.swapaxes(lse, -1, -2).reshape(B, dil, Lp, H)[:, :, :L].transpose(0, 2, 1, 3).reshape(B, S, H)
    return o, lse

def dilated_group_sample(q, k, v, cache_kv, window, dil):
    steps = window // dil
    T = q.shape[1]
    Wb = cache_kv.shape[1]
    full = jnp.concatenate([cache_kv, jnp.stack([k, v], axis=2).astype(cache_kv.dtype)], axis=1)
    idx = Wb + jnp.arange(T)[:, None] - dil * jnp.arange(steps + 1)[None, :]
    valid = idx >= 0
    sel = full[:, jnp.maximum(idx, 0)]
    s = jnp.einsum('bthe,btkhe->bthk', q, sel[:, :, :, 0], preferred_element_type=jnp.float32) * SCALE
    p, lse = masked_softmax_stats(jnp.where(valid[:, None, :], s, NEG_INF))
    o = jnp.einsum('bthk,btkhe->bthe', p, sel[:, :, :, 1].astype(jnp.float32))
    keep = min(window, Wb + T)
    return o, lse, full[:, -keep:]

def combine_groups(outs, lses):
    o = jnp.stack(outs, axis=-3)
    lse = jnp.stack(lses, axis=-2)
    w = jax.nn.softmax(lse, axis=-2)
    mixed = jnp.sum(o * w[..., None], axis=-3)
    return mixed.reshape(mixed.shape[:-2] + (ATTN_MIX_WIDTH,))

def causal_depthwise(u_ext, w_dw, b_dw):
    out = lax.conv_general_dilated(u_ext, w_dw[:, None, :].astype(u_ext.dtype), (1,), 'VALID',
                                   dimension_numbers=('NWC', 'WIO', 'NWC'), feature_group_count=CONV_CH)
    return out + b_dw

def mix_prompt(x, w_in, b_in, w_dw, b_dw):
    S = x.shape[1]
    q, k, v, u, gate_logits = project_inputs(x, w_in, b_in, jnp.arange(S))
    outs, lses, kv_states = [], [], []
    for g, (window, dil) in enumerate(ATTN_PATTERNS):
        hs = slice(g * HEADS_PER_GROUP, (g + 1) * HEADS_PER_GROUP)
        o, lse = dilated_group_prompt(q[:, :, hs], k[:, :, hs], v[:, :, hs], dil, window // dil)
        outs.append(o)
        lses.append(lse)
        kv_states.append(jnp.stack([k[:, :, hs], v[:, :, hs]], axis=2)[:, -min(window, S):])
    attn = combine_groups(outs, lses).astype(x.dtype)
    conv = causal_depthwise(jnp.pad(u, ((0, 0), (CONV_WIDTH - 1, 0), (0, 0))), w_dw, b_dw)
    return attn, conv, gate_logits, kv_states, u[:, -(CONV_WIDTH - 1):]

def mix_sample(x, kv_caches, conv_state, w_in, b_in, w_dw, b_dw):
    T = x.shape[1]
    q, k, v, u, gate_logits = project_inputs(x, w_in, b_in, PAST_LEN + jnp.arange(T))
    outs, lses, kv_states = [], [], []
    for g, (window, dil) in enumerate(ATTN_PATTERNS):
        hs = slice(g * HEADS_PER_GROUP, (g + 1) * HEADS_PER_GROUP)
        o, lse, kv_new = dilated_group_sample(q[:, :, hs], k[:, :, hs], v[:, :, hs], kv_caches[g], window, dil)
        outs.append(o)
        lses.append(lse)
        kv_states.append(kv_new)
    attn = combine_groups(outs, lses).astype(x.dtype)
    u_ext = jnp.concatenate([conv_state.astype(u.dtype), u], axis=1)
    conv = causal_depthwise(u_ext, w_dw, b_dw)
    return attn, conv, gate_logits, kv_states, u_ext[:, -(CONV_WIDTH - 1):]

def hierarchical_moe(h, w_rg, b_rg, w_re, b_re, w_eg, w_eu, w_ed):
    xt = h.reshape(-1, D_MODEL)
    N = xt.shape[0]
    xf = xt.astype(jnp.float32)
    g_logits = xf @ w_rg.astype(jnp.float32) + b_rg.astype(jnp.float32)
    g_sel = jnp.argmax(g_logits, axis=-1)
    p_g = jnp.take_along_axis(jax.nn.softmax(g_logits, -1), g_sel[:, None], 1)
    e_logits = (xf @ w_re.astype(jnp.float32) + b_re.astype(jnp.float32)).reshape(N, N_EXPERT_GROUPS, EXPERTS_PER_GROUP)
    e_logits = jnp.take_along_axis(e_logits, g_sel[:, None, None], 1)[:, 0]
    top_v, top_i = lax.top_k(e_logits, TOP_K)
    gate = p_g * jax.nn.softmax(top_v, -1)
    expert = g_sel[:, None] * EXPERTS_PER_GROUP + top_i
    A = N * TOP_K
    e_flat = expert.reshape(A)
    order = jnp.argsort(e_flat)
    e_s = e_flat[order]
    tok_s = (jnp.arange(A) // TOP_K)[order]
    gate_s = gate.reshape(A)[order]
    counts = jnp.bincount(e_flat, length=N_EXPERTS)
    padded = ((counts + MOE_BLOCK - 1) // MOE_BLOCK) * MOE_BLOCK
    pad_end = jnp.cumsum(padded)
    pad_start = pad_end - padded
    start = jnp.cumsum(counts) - counts
    dest = pad_start[e_s] + jnp.arange(A) - start[e_s]
    n_blocks = -(-A // MOE_BLOCK) + N_EXPERTS
    rows = n_blocks * MOE_BLOCK
    buf = jnp.zeros((rows, D_MODEL), xt.dtype).at[dest].set(xt[tok_s])
    block_expert = jnp.minimum(jnp.searchsorted(pad_end, jnp.arange(n_blocks) * MOE_BLOCK, side='right'), N_EXPERTS - 1)

    def expert_block(args):
        xb, e = args
        return (jax.nn.silu(xb @ w_eg[e]) * (xb @ w_eu[e])) @ w_ed[e]

    yb = lax.map(expert_block, (buf.reshape(n_blocks, MOE_BLOCK, D_MODEL), block_expert)).reshape(rows, D_MODEL)
    y_rows = yb[dest] * gate_s[:, None].astype(yb.dtype)
    out = jnp.zeros((N, D_MODEL), yb.dtype).at[tok_s].add(y_rows)
    return out.reshape(h.shape)

def merge_and_channel_mix(x, attn, conv, gate_logits, conv_ln_g, conv_ln_b, w_conv_out, b_conv_out, w_attn_out,
                          w_o, ln1_g, ln1_b, w_rg, b_rg, w_re, b_re, w_eg, w_eu, w_ed, ln2_g, ln2_b):
    branch_c = jax.nn.silu(layer_norm(conv, conv_ln_g, conv_ln_b)) @ w_conv_out + b_conv_out
    branch_a = attn @ w_attn_out
    g_a, g_c = jnp.split(jax.nn.sigmoid(gate_logits), 2, axis=-1)
    y = (g_a * branch_a + g_c * branch_c) @ w_o
    h = layer_norm(DN_ALPHA * x + y, ln1_g, ln1_b)
    return layer_norm(DN_ALPHA * h + hierarchical_moe(h, w_rg, b_rg, w_re, b_re, w_eg, w_eu, w_ed), ln2_g, ln2_b)

def setup_inputs(seed: int = 0) -> dict:
    key = jax.random.key(seed)
    ks = jax.random.split(key, 32)

    def nrm(k, shape, scale=1.0):
        return scale * jax.random.normal(k, shape, jnp.float32)

    L = DEPTH
    wb = [min(w, PAST_LEN) for w, _ in ATTN_PATTERNS]
    kvs = (HEADS_PER_GROUP, HEAD_DIM)
    return {
        "x_prompt": nrm(ks[0], (BATCH, SEQ, D_MODEL)),
        "x_sample": nrm(ks[1], (DEC_BATCH, DEC_SEQ, D_MODEL)),
        "cache_kv_w128": nrm(ks[2], (L, DEC_BATCH, wb[0], 2) + kvs),
        "cache_kv_w512": nrm(ks[3], (L, DEC_BATCH, wb[1], 2) + kvs),
        "cache_kv_w2048": nrm(ks[4], (L, DEC_BATCH, wb[2], 2) + kvs),
        "state_conv": nrm(ks[5], (L, DEC_BATCH, CONV_WIDTH - 1, CONV_CH), 0.5),
        "w_in": nrm(ks[6], (L, D_MODEL, IN_WIDTH), D_MODEL ** -0.5),
        "b_in": nrm(ks[7], (L, IN_WIDTH), 0.01),
        "w_dw": nrm(ks[8], (L, CONV_WIDTH, CONV_CH), CONV_WIDTH ** -0.5),
        "b_dw": nrm(ks[9], (L, CONV_CH), 0.01),
        "conv_ln_g": 1.0 + nrm(ks[10], (L, CONV_CH), 0.01),
        "conv_ln_b": nrm(ks[11], (L, CONV_CH), 0.01),
        "w_conv_out": nrm(ks[12], (L, CONV_CH, D_MODEL), CONV_CH ** -0.5),
        "b_conv_out": nrm(ks[13], (L, D_MODEL), 0.01),
        "w_attn_out": nrm(ks[14], (L, ATTN_MIX_WIDTH, D_MODEL), ATTN_MIX_WIDTH ** -0.5),
        "w_o": nrm(ks[15], (L, D_MODEL, D_MODEL), DN_BETA * D_MODEL ** -0.5),
        "ln1_g": 1.0 + nrm(ks[16], (L, D_MODEL), 0.01),
        "ln1_b": nrm(ks[17], (L, D_MODEL), 0.01),
        "w_router_group": nrm(ks[18], (L, D_MODEL, N_EXPERT_GROUPS), D_MODEL ** -0.5),
        "b_router_group": nrm(ks[19], (L, N_EXPERT_GROUPS), 0.01),
        "w_router_expert": nrm(ks[20], (L, D_MODEL, N_EXPERTS), D_MODEL ** -0.5),
        "b_router_expert": nrm(ks[21], (L, N_EXPERTS), 0.01),
        "w_expert_gate": nrm(ks[22], (L, N_EXPERTS, D_MODEL, D_EXPERT), D_MODEL ** -0.5),
        "w_expert_up": nrm(ks[23], (L, N_EXPERTS, D_MODEL, D_EXPERT), D_MODEL ** -0.5),
        "w_expert_down": nrm(ks[24], (L, N_EXPERTS, D_EXPERT, D_MODEL), DN_BETA * D_EXPERT ** -0.5),
        "ln2_g": 1.0 + nrm(ks[25], (L, D_MODEL), 0.01),
        "ln2_b": nrm(ks[26], (L, D_MODEL), 0.01),
    }

def reference(x_prompt, x_sample, cache_kv_w128, cache_kv_w512, cache_kv_w2048, state_conv, w_in, b_in, w_dw,
              b_dw, conv_ln_g, conv_ln_b, w_conv_out, b_conv_out, w_attn_out, w_o, ln1_g, ln1_b, w_router_group,
              b_router_group, w_router_expert, b_router_expert, w_expert_gate, w_expert_up, w_expert_down,
              ln2_g, ln2_b):
    y_prompt, y_sample = x_prompt, x_sample
    kvp = [[], [], []]
    kvs = [[], [], []]
    convp, convs = [], []
    for l in range(DEPTH):
        tail = (conv_ln_g[l], conv_ln_b[l], w_conv_out[l], b_conv_out[l], w_attn_out[l], w_o[l], ln1_g[l], ln1_b[l],
                w_router_group[l], b_router_group[l], w_router_expert[l], b_router_expert[l], w_expert_gate[l],
                w_expert_up[l], w_expert_down[l], ln2_g[l], ln2_b[l])
        a, c, gl, kv_new, conv_new = mix_prompt(y_prompt, w_in[l], b_in[l], w_dw[l], b_dw[l])
        y_prompt = merge_and_channel_mix(y_prompt, a, c, gl, *tail)
        for g in range(N_ATTN_GROUPS):
            kvp[g].append(kv_new[g])
        convp.append(conv_new)
        caches = (cache_kv_w128[l], cache_kv_w512[l], cache_kv_w2048[l])
        a, c, gl, kv_new, conv_new = mix_sample(y_sample, caches, state_conv[l], w_in[l], b_in[l], w_dw[l], b_dw[l])
        y_sample = merge_and_channel_mix(y_sample, a, c, gl, *tail)
        for g in range(N_ATTN_GROUPS):
            kvs[g].append(kv_new[g])
        convs.append(conv_new)
    kv_w128_prompt = jnp.stack(kvp[0])
    kv_w512_prompt = jnp.stack(kvp[1])
    kv_w2048_prompt = jnp.stack(kvp[2])
    conv_prompt = jnp.stack(convp)
    kv_w128_sample = jnp.stack(kvs[0])
    kv_w512_sample = jnp.stack(kvs[1])
    kv_w2048_sample = jnp.stack(kvs[2])
    conv_sample = jnp.stack(convs)
    return (y_prompt, y_sample, kv_w128_prompt, kv_w512_prompt, kv_w2048_prompt, conv_prompt,
            kv_w128_sample, kv_w512_sample, kv_w2048_sample, conv_sample)


_drawn_inputs = setup_inputs


def setup_inputs(seed=0):
    import zlib

    import numpy as np

    out = dict(_drawn_inputs(seed))
    spreads = {}
    factors = {'b_in': 5.443,
     'b_dw': 5.793,
     'conv_ln_g': 8.0,
     'conv_ln_b': 8.0,
     'b_conv_out': 7.525,
     'ln1_g': 3.571,
     'b_router_group': 6.779,
     'b_router_expert': 8.0,
     'ln2_g': 5.565,
     'ln2_b': 5.604}
    for name, (base, spread) in spreads.items():
        noise = np.random.default_rng([zlib.crc32(name.encode()), seed]).standard_normal(out[name].shape)
        drawn = base * np.exp(spread * noise) if base else spread * noise
        out[name] = __import__('jax').numpy.asarray(drawn.astype(out[name].dtype))
    for name, factor in factors.items():
        out[name] = (out[name] * factor).astype(out[name].dtype)
    return out
```

```python
from contextlib import ExitStack

import numpy as np

import concourse.bass as bass
from concourse import mybir
from concourse.alu_op_type import AluOpType as ALU

F32 = mybir.dt.float32
BF16 = mybir.dt.bfloat16
I32 = mybir.dt.int32
ACT = mybir.ActivationFunctionType
AX_X = mybir.AxisListType.X

P = 128
D = 1024
KD = D // P
SEQ, NB, NT = 512, 8, 4
NS = NB * NT
N = SEQ + NS
HALF = N // 2
IN_W = 5376
MT = IN_W // P
Q0, K0, V0, UA0, UB0, G0 = 0, 6, 12, 18, 22, 26
CT = 4
CC = CT * P
TAPS = 31
PAD = TAPS - 1
HEADS, HD = 4, 64
WIN = (128, 512, 2048)
PAST = 512
ALPHA = 2 ** 0.25
EPS = 1e-5
SCALE = HD ** -0.5
NEG = -1e30
NGRP, NPER = 4, 8
NE = NGRP * NPER
FE = 512
KF = FE // P
BLK = 96
OVER = (2 * N) // BLK
NBLK = NE + OVER
LEVELS = (N - 1) // BLK
OOB = 1 << 20
TILES = [(t * P, min(P, N - t * P)) for t in range((N + P - 1) // P)]
NTT = len(TILES)
SKEYS = 3 * P + 3 * NS
PKEYS = SEQ + 2 * P


def constants():
    half = HD // 8
    pos = np.concatenate([np.arange(SEQ), np.tile(PAST + np.arange(NT), NB)]).astype(np.float32)
    inv = (np.float32(500000.0) ** (-np.arange(half, dtype=np.float32) / np.float32(half))).astype(np.float32)
    ang = (pos[None, :] * inv[:, None]).astype(np.float32)
    cos, sin = np.ones((P, N), np.float32), np.zeros((P, N), np.float32)
    rot = np.zeros((P, P), np.float32)
    for h in range(0, P, HD):
        for j in range(half):
            for i in (h + j, h + j + half):
                cos[i], sin[i] = np.cos(ang[j]), np.sin(ang[j])
            rot[h + j + half, h + j] = -1.0
            rot[h + j, h + j + half] = 1.0
    eye = np.eye(P, dtype=np.float32)
    before = np.triu(np.ones((P, P), np.float32), 1)
    rows = np.tile(np.concatenate([np.arange(BLK), np.arange(NBLK), np.arange(NE)]).astype(np.float32), (P, 1))
    p = np.arange(P)
    masks = []
    for r in range(4):
        t, key = 4 * p[:, None] + r, np.arange(SEQ)[None, :]
        masks.append((key <= t) & (key >= t - WIN[0]))
    masks.append(p[None, :] <= p[:, None])
    masks.append((p[None, :] <= p[:, None]) & ((p[:, None] - p[None, :]) % 4 == 0))
    pmask = np.where(np.concatenate(masks, 1), 0.0, NEG).astype(np.float32)
    b, t = (p // 8) % NB, (p // 2) % NT
    col, new = np.arange(P)[None, :], np.arange(NS)[None, :]
    own, nt = new // NT == b[:, None], new % NT
    smask = np.concatenate([col >= t[:, None], col >= 0 * t[:, None], col % 4 == t[:, None],
                            own & (nt <= t[:, None]), own & (nt == t[:, None]), own & (nt == t[:, None])], 1)
    smask = np.where(smask, 0.0, NEG).astype(np.float32)
    token = np.zeros((P, NTT, 2), np.float32)
    for i in range(NTT):
        for k in range(2):
            token[:, i, k] = 1 + k * N + i * P + p
    return np.concatenate([cos, sin, eye, rot, before, rows, token.reshape(P, -1), pmask, smask], 1)


C_COS, C_SIN = 0, N
C_EYE = 2 * N
C_ROWS = C_EYE + 3 * P
NROWS = BLK + NBLK + NE + 2 * NTT
C_PM = C_ROWS + NROWS
C_SM = C_PM + 4 * SEQ + 2 * P
C_END = C_SM + SKEYS


def build(nc, a, o):
    y_prompt, y_sample, kv0p, kv1p, kv2p, conv_p, kv0s, kv1s, kv2s, conv_s = o
    h_dram = nc.dram_tensor("h_rows", [N, D], F32, kind="Internal").ap()
    y_dram = nc.dram_tensor("expert_rows", [2 * N, D], F32, kind="Internal").ap()
    caches = [a["cache_kv_w128"][0], a["cache_kv_w512"][0], a["cache_kv_w2048"][0]]
    const = a["constants"]
    w_in = a["w_in"][0].rearrange("(k p) n -> p k n", p=P)
    wg_d = a["w_expert_gate"][0].rearrange("e (p k) f -> e p (k f)", k=KD)
    wu_d = a["w_expert_up"][0].rearrange("e (p k) f -> e p (k f)", k=KD)
    wd_d = a["w_expert_down"][0].rearrange("e (k p) d -> e p k d", p=P)
    x_p, x_s = a["x_prompt"][0], a["x_sample"].rearrange("b t d -> (b t) d")

    with ExitStack() as ctx:
        def sb(name, cols, dt=F32, parts=P):
            return ctx.enter_context(nc.sbuf_tensor(name, [parts, cols], dt))

        def sem(name):
            return ctx.enter_context(nc.semaphore(name))

        ea, eb = sb("region_a", 12288), sb("region_b", 12288)
        z2, xt_t = sb("z_conv_gates", (MT - V0 - 6) * N), sb("x_columns", KD * N)
        sc, vt_t = sb("scratch", 3256), sb("value_rows", 3072)
        wa_t, at_t = sb("w_attn", 2048), sb("attn_columns", 2 * N)
        ci = sb("const_small", 3 * P + NROWS)
        colb = sb("column_vectors", 62 + TAPS * CT)
        small = sb("small", 72)
        gidx, sidx = sb("gather_rows", NBLK, I32), sb("scatter_rows", NBLK, I32)
        over_i = sb("further_blocks", OVER + 1, I32)
        over_idx = sb("block_rows", 6, I32)
        ps = ctx.enter_context(nc.psum_tensor("ps", [P, 8, 512], F32))

        eye, rot, before = ci[:, 0:P], ci[:, P:2 * P], ci[:, 2 * P:3 * P]
        iota_r = ci[:, 3 * P:3 * P + BLK]
        iota_b = ci[:, 3 * P + BLK:3 * P + BLK + NBLK]
        iota_e = ci[:, 3 * P + BLK + NBLK:3 * P + BLK + NBLK + NE]
        token = ci[:, 3 * P + BLK + NBLK + NE:].rearrange("p (t k) -> p t k", k=2)
        bdw_c, clg_c, clb_c, bco_c = (colb[:, i:i + 8] for i in (42, 46, 50, 54))
        wdw_c = colb[:, 62:62 + TAPS * CT]

        zqkv = ea[:, 0:18 * N].rearrange("p (m n) -> p m n", n=N)
        pmask = ea[:, 18 * N:18 * N + 4 * SEQ + 2 * P]
        wring = eb[:, 0:6144].rearrange("p (s k n) -> p s k n", s=3, k=KD)
        kout12 = eb[:, 0:2048].rearrange("p (r c) -> p r c", r=4)
        kout0 = eb[:, 2048:2304]
        smask = eb[:, 2304:2304 + SKEYS]
        skv = eb[:, 2784:4320].rearrange("p (g two c) -> p g two c", g=3, two=2)
        qbd = eb[:, 4320:4704].rearrange("p (m b j) -> p m b j", m=6, j=2)
        st_sb, stn_sb = eb[:, 4704:5088], eb[:, 5088:5472]
        sp = eb[:, 5472:5472 + SKEYS]
        kc = eb[:, 6144:9216].rearrange("p (s t c) -> p s t c", s=2, t=6)
        vc = eb[:, 9216:12288].rearrange("p (s t c) -> p s t c", s=2, t=6)
        cos, sin = eb[:, 9216:9216 + N], eb[:, 9216 + N:9216 + 2 * N]
        wo = eb[:, 0:KD * D].rearrange("p (k n) -> p k n", k=KD)

        zr = z2[:, :].rearrange("p (m n) -> p m n", n=N)
        ua, ub = zr[:, 0:CT], zr[:, CT:2 * CT]
        xs = z2[:, 8 * N:8 * N + NTT * D].rearrange("p (t d) -> p t d", d=D)
        ga, gc = zr[:, 8:16], zr[:, 16:24]
        xt = xt_t[:, :].rearrange("p (k n) -> p k n", k=KD)
        wco = xt_t[:, 0:CT * D].rearrange("p (k n) -> p k n", k=CT)
        rows_a, rows_b = vt_t[0:62, 0:P], vt_t[0:TAPS * CT, P:2 * P]
        rtmp = vt_t[:, 2 * P:2 * P + 2 * N].rearrange("p (s n) -> p s n", s=2)
        cst = vt_t[0:4 * PAD, 1408:2432].rearrange("p (j c) -> p j c", j=2)
        vt = vt_t[:, :].rearrange("p (r c) -> p r c", r=4)
        uext = sc[:, 0:CT * (SEQ + PAD)].rearrange("p (c s) -> p c s", c=CT)
        sext = sc[:, CT * (SEQ + PAD):3256].rearrange("p (c b s) -> p c b s", c=CT, b=NB)
        ktr = sc[:, 0:3072].rearrange("p (s m k) -> p s m k", s=2, m=12)
        prob = sc[:, 0:2 * PKEYS].rearrange("p (s k) -> p s k", s=2)
        prt = sc[:, 2 * PKEYS:4 * PKEYS].rearrange("p (s m k) -> p s m k", s=2, m=6)
        wa = wa_t[:, :].rearrange("p (k n) -> p k n", k=2)
        at = at_t[:, :].rearrange("p (k n) -> p k n", k=2)

        acc, cen = ua, ub
        rstd_c = sc[:, 0:N]
        onesm = sb("ones_mean", P)[:, :]
        onesb = sb("ones_count", P, BF16)[:, :]
        beforeb = sb("before_count", P, BF16)[:, :]
        nmx_p, l_p = small[:, 0:16], small[:, 16:32]
        rinv = small[:, 32:36]
        pmx = small[:, 69:71]
        cst_u = ea[:, 18 * N + 4 * SEQ + 2 * P:18 * N + 4 * SEQ + 3 * P].rearrange("p (c n) -> p c n", c=CT)
        urow_p, urow_s = z2[:, 4 * N:4 * N + CC], z2[:, 4 * N + CC:4 * N + 2 * CC]
        atk = xt_t[:, 4096:4352]
        nmx_s, l_s, rinv_s = small[:, 36:37], small[:, 37:38], small[:, 38:39]

        wrv = z2[:, 16 * N + 3 * D:16 * N + 3 * D + KD * 36].rearrange("p (k n) -> p k n", k=KD)
        br = sb("b_router", 36)[:, :]
        hrow = z2[:, 0:2048].rearrange("p (s d) -> p s d", s=2)
        xrow = z2[:, 2048:4096].rearrange("p (s d) -> p s d", s=2)
        g1row, b1row = z2[:, 16 * N:16 * N + D], z2[:, 16 * N + D:16 * N + 2 * D]
        hcol = z2[:, 16 * N + 2 * D:16 * N + 3 * D].rearrange("p (k n) -> p k n", k=KD)
        stats = small[:, 40:64]
        mv = small[:, 64:66]
        sd, rs, nmr = small[:, 66:67], small[:, 67:68], small[:, 68:69]
        logits = sb("logits", NTT * 36)
        lg = logits[:, :].rearrange("p (t c) -> p t c", c=36)
        gates = sb("gate_weights", NTT * 2)
        mb = sb("choices", NTT * NE, BF16)[:, :].rearrange("p (t e) -> p t e", e=NE)
        at_col = [0]

        def route(*dims):
            n, c = int(np.prod(dims)), at_col[0]
            at_col[0] += n
            names = "abc"[:len(dims)]
            v = vt_t[:, c:c + n]
            return v if len(dims) == 1 else v.rearrange(f"p ({' '.join(names)}) -> p {' '.join(names)}",
                                                        **{names[i]: dims[i] for i in range(1, len(dims))})

        ohr, ohb = route(2 * NTT, BLK), route(2 * NTT, NBLK)
        oh, rank = route(2, NTT, NE), route(NTT, NE)
        emf, rt32, io32 = route(NTT * NE), route(NTT, NE), route(NTT, NE)
        em = emf.rearrange("p (t e) -> p t e", e=NE)
        em4 = emf.rearrange("p (t g e) -> p t g e", g=NGRP, e=NPER)
        rt_a4, rt_b4, rt_c4, rt_g3 = (route(NTT, NGRP) for _ in range(4))
        v12, e12 = route(2, NTT), route(2, NTT)
        m1, i1, rt_d = route(NTT), route(NTT), route(NTT)
        cnt, nov, ovst, tmp32, ovf = route(NE), route(NE), route(NE), route(NE), route(OVER + 1)
        ovend, tabf = route(2, NE), route(2, NBLK)
        rk, ek, ok, qk, q0 = (route(NTT, 2) for _ in range(5))

        wslot = [ea, eb]
        wgv = [w[:, 0:4096].rearrange("p (k f m) -> p k f m", k=KD, f=KF) for w in wslot]
        wuv = [w[:, 4096:8192].rearrange("p (k f m) -> p k f m", k=KD, f=KF) for w in wslot]
        wdv = [w[:, 8192:12288].rearrange("p (k d) -> p k d", k=KF) for w in wslot]
        xg = [xt_t[0:BLK, s * D:(s + 1) * D] for s in range(2)]
        yo = [xt_t[0:BLK, (2 + s) * D:(3 + s) * D] for s in range(2)]
        xgt = [sc[:, s * 768:(s + 1) * 768].rearrange("p (k c) -> p k c", k=KD) for s in range(2)]
        gact = sc[:, 1536:1920].rearrange("p (f c) -> p f c", f=KF)
        hact = sc[:, 1920:2304].rearrange("p (f c) -> p f c", f=KF)
        idx_t = over_idx

        x_loaded, rows_loaded, ci_loaded, trig_loaded = sem("x_loaded"), sem("rows_loaded"), sem("ci_loaded"), sem("trig_loaded")
        mask_loaded, state_loaded = sem("mask_loaded"), sem("state_loaded")
        win_loaded = [sem(f"win_loaded{s}") for s in range(3)]
        tile_mm, tile_free = sem("tile_mm"), sem("tile_free")
        pads_set = sem("pads_set")
        xt_ps, xt_sb = sem("xt_ps"), sem("xt_sb")
        colb_ps, colb_sb = sem("colb_ps"), sem("colb_sb")
        rot_ps, rot_used, rotated = sem("rot_ps"), sem("rot_used"), sem("rotated")
        state_ps, state_sb = sem("state_ps"), sem("state_sb")
        dve_chain, pool_steps, sp_steps = sem("dve_chain"), sem("pool_steps"), sem("sp_steps")
        sig_u, conv_step, u_set = sem("sig_u"), sem("conv_step"), sem("u_set")
        v_ps, v_sb, k_ps, k_sb, s_ps, s_sb = (sem(x) for x in ("v_ps", "v_sb", "k_ps", "k_sb", "s_ps", "s_sb"))
        u_ps, u_sb = sem("u_ps"), sem("u_sb")
        stored, copied, kout_stored = sem("stored"), sem("copied"), sem("kout_stored")
        kc_loaded = [sem(f"kc_loaded{s}") for s in range(2)]
        vc_loaded = [sem(f"vc_loaded{s}") for s in range(2)]
        kt_ps, kt_dve, kt_act, st_ps, st_done = (sem(x) for x in ("kt_ps", "kt_dve", "kt_act", "st_ps", "st_done"))
        qbd_set, sback_ps, sprob, spn, spt_ps, spt_sb, vs_used, so_ps, so_sb = (
            sem(x) for x in ("qbd_set", "sback_ps", "sprob", "spn", "spt_ps", "spt_sb", "vs_used", "so_ps", "so_sb"))
        smax = sem("smax")
        qk_ps, pmax, pexp, pt_ps, pt_dve, pt_act, pv_ps, otok, at_ps, at_sb = (
            sem(x) for x in ("qk_ps", "pmax", "pexp", "pt_ps", "pt_dve", "pt_act", "pv_ps", "otok", "at_ps", "at_sb"))
        mean_ps, cen_sb, sq_sb, var_ps, veps, csd, cnorm, cact = (
            sem(x) for x in ("mean_ps", "cen_sb", "sq_sb", "var_ps", "veps", "csd", "cnorm", "cact"))
        conv_done = sem("conv_done")
        wco_loaded, wa_loaded, wo_loaded = sem("wco_loaded"), sem("wa_loaded"), sem("wo_loaded")
        gates_act = sem("gates_act")
        br_ps, br_used, merged = sem("br_ps"), sem("br_used"), sem("merged")
        xrow_loaded = [sem(f"xrow_loaded{s}") for s in range(2)]
        rows1_loaded, wr_loaded = sem("rows1_loaded"), sem("wr_loaded")
        y_ps, y_used, hvar, hsd, hscale, hnorm, hmul, hdone = (
            sem(x) for x in ("y_ps", "y_used", "hvar", "hsd", "hscale", "hnorm", "hmul", "hdone"))
        h_stored = [sem(f"h_stored{s}") for s in range(2)]
        ht_ps, ht_sb, lg_ps, lg_sb = sem("ht_ps"), sem("ht_sb"), sem("lg_ps"), sem("lg_sb")
        rmax, rexp, mset, cnt_ps, sel_set, idx_ps, idx_set = (
            sem(x) for x in ("rmax", "rexp", "mset", "cnt_ps", "sel_set", "idx_ps", "idx_set"))
        rmax2, rexp2 = sem("rmax2"), sem("rexp2")
        e_loaded = [[sem(f"{n}_loaded{s}") for s in range(2)] for n in ("wg", "wu", "wd")]
        gathered = [sem(f"gathered{s}") for s in range(2)]
        scattered = [sem(f"scattered{s}") for s in range(2)]
        idx_set_e, xgt_ps, xgt_sb, gu_ps, gact_sb, hact_sb, dn_ps, yo_sb = (
            sem(x) for x in ("idx_copied", "xgt_ps", "xgt_sb", "gu_ps", "gact_sb", "hact_sb", "dn_ps", "yo_sb"))
        ov = {x: sem("ov_" + x) for x in ("load", "idx", "gat", "tps", "tsb", "gu", "ga", "ha", "dn", "yo", "sca")}
        over_done = sem("over_done")
        fin_loaded = [sem(f"fin_loaded{s}") for s in range(2)]
        rows2_loaded = sem("rows2_loaded")
        fmix, fvar, fsd, fscale, fnorm, fmul, fdone = (
            sem(x) for x in ("fmix", "fvar", "fsd", "fscale", "fnorm", "fmul", "fdone"))
        y_stored = [sem(f"y_stored{s}") for s in range(2)]
        qbd_zero, br_loaded = sem("qbd_zero"), sem("br_loaded")

        block = ctx.enter_context(nc.Block())
        fh = [z2[:, s * D:(s + 1) * D] for s in range(2)]
        fy1 = [z2[:, (2 + s) * D:(3 + s) * D] for s in range(2)]
        fy2 = [z2[:, (4 + s) * D:(5 + s) * D] for s in range(2)]
        g2row, b2row = z2[:, 6 * D:7 * D], z2[:, 7 * D:8 * D]

        @block.sync
        def _(sp_e):
            sp_e.dma_start(xs[:, 0:4, :], x_p.rearrange("(t p) d -> p t d", p=P)).then_inc(x_loaded, 16)
            sp_e.dma_start(xs[0:NS, 4, :], x_s).then_inc(x_loaded, 16)
            for s in range(3):
                sp_e.dma_start(wring[:, s], w_in[:, :, s * 256:(s + 1) * 256]).then_inc(win_loaded[s], 16)
            with sp_e.Fori(1, 7) as i:
                for s in range(3):
                    sp_e.wait_ge(tile_mm, 6 * i + 2 * s - 4)
                    sp_e.dma_start(wring[:, s], w_in[:, :, bass.ds(i * 768 + s * 256, 256)]).then_inc(win_loaded[s], 16)
            sp_e.wait_ge(tile_mm, MT)
            sp_e.dma_start(smask, const[:, C_SM:C_END]).then_inc(mask_loaded, 16)
            sp_e.dma_start(wco, a["w_conv_out"][0].rearrange("(k p) n -> p k n", p=P)).then_inc(wco_loaded, 16)
            sp_e.wait_ge(so_ps, 1)
            sp_e.wait_ge(kout_stored, 16 * 15)
            sp_e.dma_start(wo, a["w_o"][0].rearrange("(k p) n -> p k n", p=P)).then_inc(wo_loaded, 16)
            sp_e.wait_ge(at_sb, 4)
            for n, src in enumerate((wg_d, wu_d)):
                sp_e.dma_start(ea[:, n * 4096:(n + 1) * 4096], src[0]).then_inc(e_loaded[n][0], 16)
            sp_e.dma_start(wdv[0], wd_d[0]).then_inc(e_loaded[2][0], 16)
            for t in range(NTT):
                c0, n = TILES[t]
                if t == 0:
                    sp_e.wait_ge(merged, 8)
                    sp_e.dma_start(g1row, a["ln1_g"][0].partition_broadcast(P)).then_inc(rows1_loaded, 16)
                    sp_e.dma_start(b1row, a["ln1_b"][0].partition_broadcast(P)).then_inc(rows1_loaded, 16)
                    sp_e.dma_start(wrv[:, :, 0:4], a["w_router_group"][0].rearrange("(k p) n -> p k n", p=P)).then_inc(wr_loaded, 16)
                    sp_e.dma_start(wrv[:, :, 4:36], a["w_router_expert"][0].rearrange("(k p) n -> p k n", p=P)).then_inc(wr_loaded, 16)
                if t >= 2:
                    sp_e.wait_ge(y_used, t - 1)
                src = x_p[c0:c0 + n] if t < 4 else x_s
                sp_e.dma_start(xrow[0:n, t % 2, :], src).then_inc(xrow_loaded[t % 2], 16)
            sp_e.wait_ge(y_ps, NTT)
            for n, src in enumerate((wg_d, wu_d)):
                sp_e.dma_start(eb[:, n * 4096:(n + 1) * 4096], src[1]).then_inc(e_loaded[n][1], 16)
            sp_e.dma_start(wdv[1], wd_d[1]).then_inc(e_loaded[2][1], 16)
            with sp_e.Fori(1, NE // 2) as i:
                for s in range(2):
                    e = 2 * i + s
                    sp_e.wait_ge(gu_ps, KF * (2 * i + s - 1))
                    for n, src in enumerate((wg_d, wu_d)):
                        sp_e.dma_start(wslot[s][:, n * 4096:(n + 1) * 4096],
                                       src[bass.ds(e, 1)].rearrange("o p x -> p (o x)")).then_inc(e_loaded[n][s], 16)
                    sp_e.wait_ge(dn_ps, 2 * i + s - 1)
                    sp_e.dma_start(wdv[s], wd_d[bass.ds(e, 1)].rearrange("o p k d -> p (o k) d")).then_inc(e_loaded[2][s], 16)
            sp_e.wait_ge(idx_set, 1)
            sp_e.wait_ge(dn_ps, NE)
            count = sp_e.value_load(over_i[0:1, OVER:OVER + 1], min_val=0, max_val=OVER)
            with sp_e.If(count > 0):
                with sp_e.Fori(0, count) as i:
                    e = sp_e.value_load(over_i[0:1, bass.ds(i, 1)], min_val=0, max_val=NE - 1)
                    for n, src in enumerate((wg_d, wu_d)):
                        sp_e.dma_start(ea[:, n * 4096:(n + 1) * 4096],
                                       src[bass.ds(e, 1)].rearrange("o p x -> p (o x)")).then_inc(ov["load"], 16)
                    sp_e.dma_start(wdv[0], wd_d[bass.ds(e, 1)].rearrange("o p k d -> p (o k) d")).then_inc(ov["load"], 16)
                    sp_e.wait_ge(ov["sca"], 16 * i + 16)
                    sp_e.sem_inc(sp_steps, 1)
            sp_e.dma_start(g2row, a["ln2_g"][0].partition_broadcast(P)).then_inc(rows2_loaded, 16)
            sp_e.dma_start(b2row, a["ln2_b"][0].partition_broadcast(P)).then_inc(rows2_loaded, 16)
            sp_e.wait_ge(over_done, 1)
            for t in range(NTT):
                c0, n = TILES[t]
                s = t % 2
                if t >= 2:
                    sp_e.wait_ge(y_stored[s], 16 * (t // 2))
                sp_e.dma_start(fh[s][0:n], h_dram[c0:c0 + n]).then_inc(fin_loaded[s], 16)
                sp_e.dma_start(fy1[s][0:n], y_dram[c0:c0 + n]).then_inc(fin_loaded[s], 16)
                sp_e.dma_start(fy2[s][0:n], y_dram[N + c0:N + c0 + n]).then_inc(fin_loaded[s], 16)

        @block.tensor
        def _(pe):
            pe.wait_ge(ci_loaded, 16)
            pe.wait_ge(rows_loaded, 16 * 6)
            pe.transpose(ps[:, 3, 0:62], rows_a, eye[0:62, 0:62])
            pe.transpose(ps[:, 3, 64:64 + TAPS * CT], rows_b, eye[0:TAPS * CT, 0:TAPS * CT]).then_inc(colb_ps, 1)
            pe.wait_ge(x_loaded, 32)
            for t, (c0, n) in enumerate(TILES):
                if t >= 2:
                    pe.wait_ge(xt_sb, t - 1)
                for k in range(KD):
                    last = pe.transpose(ps[:, 4 + 2 * (t % 2) + k // 4, (k % 4) * P:(k % 4) * P + n],
                                        xs[0:n, t, k * P:(k + 1) * P], eye[0:n, 0:n])
                last.then_inc(xt_ps, 1)
            pe.wait_ge(xt_sb, NTT)

            def project(lo, hi):
                with pe.Fori(lo, hi) as i:
                    for s in range(3):
                        pe.wait_ge(win_loaded[s], 16 * i + 16)
                        for c in range(2):
                            pe.wait_ge(tile_free, 6 * i + 2 * s + c + 1)
                            for half in range(2):
                                for k in range(KD):
                                    last = pe.matmul(ps[:, 2 * c + half, 0:HALF], wring[:, s, k, c * P:(c + 1) * P],
                                                     xt[:, k, half * HALF:(half + 1) * HALF], start=k == 0, stop=k == KD - 1)
                            last.then_inc(tile_mm, 1)

            project(0, 3)
            for m in range(12):
                pe.wait_ge(tile_free, 2 + m + 1)
                if m >= 2:
                    pe.wait_ge(rot_used, m - 1)
                for half in range(2):
                    last = pe.matmul(ps[:, 4 + 2 * (m % 2) + half, 0:HALF], rot, zqkv[:, m, half * HALF:(half + 1) * HALF],
                                     start=True, stop=True)
                last.then_inc(rot_ps, 1)
            pe.wait_ge(state_loaded, 32)
            pe.wait_ge(rot_used, 12)
            for j in range(2):
                for c in range(CT):
                    last = pe.transpose(ps[:, 4 + j, c * P:c * P + 4 * PAD], cst[:, j, c * P:(c + 1) * P], eye[0:4 * PAD, 0:4 * PAD])
            last.then_inc(state_ps, 1)
            project(3, 7)

            pe.wait_ge(rotated, 12)
            pe.wait_ge(state_sb, 1)
            for m in range(6):
                if m >= 4:
                    pe.wait_ge(v_sb, m - 3)
                for r in range(4):
                    src = zqkv[:, V0 + m, r * P:(r + 1) * P] if m < 2 else zqkv[:, V0 + m, r:SEQ:4]
                    last = pe.transpose(ps[:, 4 + m % 4, r * P:(r + 1) * P], src, eye)
                last.then_inc(v_ps, 1)
            pe.wait_ge(tile_free, 2 + MT)
            for m in range(6):
                if m >= 4:
                    pe.wait_ge(k_sb, m - 3)
                for r in range(4):
                    if m < 2 and r < 3:
                        continue
                    src = zqkv[:, K0 + m, r * P:(r + 1) * P] if m < 2 else zqkv[:, K0 + m, r:SEQ:4]
                    last = pe.transpose(ps[:, m % 4, r * P:(r + 1) * P], src, eye)
                last.then_inc(k_ps, 1)
            pe.wait_ge(v_sb, 6)
            for m in range(12):
                last = pe.transpose(ps[0:NS, 4 + m // 4, (m % 4) * P:(m % 4) * P + P], zqkv[:, K0 + m, SEQ:N], eye)
            last.then_inc(s_ps, 1)
            pe.wait_ge(u_set, 1)
            for c in range(CT):
                pe.transpose(ps[0:PAD, 7, c * P:(c + 1) * P], uext[:, c, SEQ:SEQ + PAD], eye)
            pe.wait_ge(k_sb, 6)
            for c in range(CT):
                last = pe.transpose(ps[0:NS, 0, c * P:(c + 1) * P], cst_u[:, c, :], eye)
            last.then_inc(u_ps, 1)

            pe.wait_ge(u_sb, 1)
            pe.wait_ge(s_sb, 1)
            pe.wait_ge(qbd_set, 1)
            pe.wait_ge(conv_done, 1)

            def cached_scores(b):
                pe.wait_ge(kt_dve, b + 1)
                pe.wait_ge(kt_act, b + 1)
                for hp in range(2):
                    for tile in range(6):
                        g = (0, 1, 1, 1, 1, 2)[tile]
                        q = qbd[:, 2 * g + hp, b * NT:(b + 1) * NT, :].rearrange("p t j -> p (t j)")
                        c0 = g * P + hp * 64 + b * 8
                        if g == 1:
                            t = tile - 1
                            q, c0, w = q[:, 2 * t:2 * t + 2], c0 + 2 * t, 2
                        else:
                            w = 8
                        last = pe.matmul(ps[:, 6, c0:c0 + w], ktr[:, b % 2, tile * 2 + hp, :], q, start=True, stop=True)
                last.then_inc(st_ps, 1)

            for b in range(NB):
                pe.wait_ge(kc_loaded[b % 2], 48 * (b // 2 + 1))
                if b >= 2:
                    pe.wait_ge(kt_dve, b - 1)
                    pe.wait_ge(kt_act, b - 1)
                for tile in range(6):
                    for hp in range(2):
                        m = tile * 2 + hp
                        last = pe.transpose(ps[:, 3 * (b % 2) + m // 4, (m % 4) * P:(m % 4 + 1) * P],
                                            kc[:, b % 2, tile, hp * P:(hp + 1) * P], eye)
                last.then_inc(kt_ps, 1)
                if b >= 1:
                    cached_scores(b - 1)
            cached_scores(NB - 1)
            for m in range(6):
                last = pe.matmul(ps[0:NS, 7, m * 64:(m + 1) * 64], zqkv[:, K0 + m, SEQ:N],
                                 qbd[:, m, :, :].rearrange("p b j -> p (b j)"), start=True, stop=True)
            last.then_inc(st_ps, 1)
            pe.wait_ge(st_done, 2)
            for g in range(3):
                pe.transpose(ps[:, 0, g * P:(g + 1) * P], st_sb[:, g * P:(g + 1) * P], eye)
            for g in range(3):
                last = pe.transpose(ps[:, 0, 3 * P + g * NS:3 * P + (g + 1) * NS], stn_sb[0:NS, g * P:(g + 1) * P], eye[0:NS, 0:NS])
            last.then_inc(sback_ps, 1)
            pe.wait_ge(spn, 1)
            for g in range(3):
                pe.transpose(ps[:, 1, g * P:(g + 1) * P], sp[:, g * P:(g + 1) * P], eye)
            for g in range(3):
                last = pe.transpose(ps[0:NS, 2, g * P:(g + 1) * P], sp[:, 3 * P + g * NS:3 * P + (g + 1) * NS], eye)
            last.then_inc(spt_ps, 1)
            pe.wait_ge(spt_sb, 2)
            for hp in range(2):
                for g in range(3):
                    pe.matmul(ps[:, 4 + hp, 0:64], skv[0:NS, g, 1, hp * P:(hp + 1) * P],
                              stn_sb[0:NS, g * P + hp * 64:g * P + hp * 64 + 64], start=g == 0, stop=False,
                              skip_group_check=True)
            for b in range(NB):
                pe.wait_ge(vc_loaded[b % 2], 48 * (b // 2 + 1))
                for hp in range(2):
                    for tile in range(6):
                        g = (0, 1, 1, 1, 1, 2)[tile]
                        o0, w = (b * 8, 8) if g != 1 else (b * 8 + 2 * (tile - 1), 2)
                        last = pe.matmul(ps[:, 4 + hp, o0:o0 + w], vc[:, b % 2, tile, hp * P:(hp + 1) * P],
                                         st_sb[:, g * P + hp * 64 + o0:g * P + hp * 64 + o0 + w],
                                         start=False, stop=b == NB - 1, skip_group_check=True)
                last.then_inc(vs_used if b < NB - 1 else so_ps, 1)

            pe.wait_ge(so_sb, 1)

            def scores(i):
                r, h = divmod(i, HEADS)
                p0, hp, s = 64 * (h % 2), h // 2, i % 2
                if i >= 2:
                    pe.wait_ge(pmax, i - 1)
                for g in range(3):
                    q = zqkv[p0:p0 + 64, Q0 + 2 * g + hp, r:SEQ:4]
                    if g == 0:
                        pe.matmul(ps[:, 2 * s, :], q, zqkv[p0:p0 + 64, K0 + hp, 0:SEQ], start=True, stop=True)
                    else:
                        last = pe.matmul(ps[:, 2 * s + 1, (g - 1) * P:g * P], q,
                                         zqkv[p0:p0 + 64, K0 + 2 * g + hp, r:SEQ:4], start=True, stop=True)
                last.then_inc(qk_ps, 1)

            def turn(i):
                pe.wait_ge(pexp, i + 1)
                if i >= 1:
                    pe.wait_ge(pt_dve, i)
                    pe.wait_ge(pt_act, i)
                for c in range(6):
                    last = pe.transpose(ps[:, 4 + c // 4, (c % 4) * P:(c % 4 + 1) * P], prob[:, i % 2, c * P:(c + 1) * P], eye)
                last.then_inc(pt_ps, 1)

            def values(i):
                r, h = divmod(i, HEADS)
                pe.wait_ge(pt_dve, i + 1)
                pe.wait_ge(pt_act, i + 1)
                if h == 0 and r >= 2:
                    pe.wait_ge(at_sb, r - 1)
                for c in range(6):
                    kb, col = (c, h * HD) if c < 4 else (r, (c - 3) * 256 + h * HD)
                    last = pe.matmul(ps[:, 6 + r % 2, h * HD:(h + 1) * HD], prt[:, i % 2, c, :], vt[:, kb, col:col + HD],
                                     start=c == 0, stop=c == 5)
                last.then_inc(pv_ps, 1)

            def turn_out(r):
                pe.wait_ge(otok, r + 1)
                for hp in range(2):
                    last = pe.transpose(ps[:, 6 + r % 2, 256 + hp * P:256 + (hp + 1) * P], atk[:, hp * P:(hp + 1) * P], eye)
                last.then_inc(at_ps, 1)

            for i in range(16 + 2):
                if i < 16:
                    scores(i)
                if 1 <= i <= 16:
                    turn(i - 1)
                if i >= 2:
                    values(i - 2)
                    if (i - 2) % 4 == 0 and i - 2 >= 4:
                        turn_out((i - 2) // 4 - 1)
            turn_out(3)

            pe.wait_ge(pmax, 16)
            for half in range(2):
                for c in range(CT):
                    last = pe.matmul(ps[:, half, 0:HALF], onesm, acc[:, c, half * HALF:(half + 1) * HALF],
                                     start=c == 0, stop=c == CT - 1)
            last.then_inc(mean_ps, 1)
            pe.wait_ge(sq_sb, 1)
            for half in range(2):
                for c in range(CT):
                    last = pe.matmul(ps[:, 2 + half, 0:HALF], onesm, acc[:, c, half * HALF:(half + 1) * HALF],
                                     start=c == 0, stop=c == CT - 1)
            last.then_inc(var_ps, 1)
            pe.wait_ge(cact, CT)
            pe.wait_ge(at_sb, 4)
            pe.wait_ge(wco_loaded, 16)
            pe.wait_ge(wa_loaded, 16)
            for m in range(KD):
                s = 4 * (m % 2)
                if m >= 2:
                    pe.wait_ge(br_used, m - 1)
                for half in range(2):
                    cols = slice(half * HALF, (half + 1) * HALF)
                    for k in range(CT):
                        pe.matmul(ps[:, s + half, 0:HALF], wco[:, k, m * P:(m + 1) * P], acc[:, k, cols], start=k == 0, stop=k == CT - 1)
                    for k in range(2):
                        last = pe.matmul(ps[:, s + 2 + half, 0:HALF], wa[:, k, m * P:(m + 1) * P], at[:, k, cols], start=k == 0, stop=k == 1)
                last.then_inc(br_ps, 1)
            pe.wait_ge(merged, 8)
            pe.wait_ge(wo_loaded, 16)
            pe.wait_ge(wr_loaded, 32)

            def router(t):
                c0, n = TILES[t]
                pe.wait_ge(hdone, t + 1)
                if t >= 1:
                    pe.wait_ge(ht_sb, t)
                for k in range(KD):
                    last = pe.transpose(ps[:, 4 + k // 4, (k % 4) * P:(k % 4) * P + n], hrow[0:n, t % 2, k * P:(k + 1) * P], eye[0:n, 0:n])
                last.then_inc(ht_ps, 1)
                pe.wait_ge(ht_sb, t + 1)
                if t >= 2:
                    pe.wait_ge(lg_sb, t - 1)
                for k in range(KD):
                    last = pe.matmul(ps[0:n, 6 + t % 2, 0:36], hcol[:, k, 0:n], wrv[:, k, :], start=k == 0, stop=k == KD - 1)
                last.then_inc(lg_ps, 1)

            for t, (c0, n) in enumerate(TILES):
                if t >= 2:
                    pe.wait_ge(y_used, t - 1)
                for half in range(2):
                    for k in range(KD):
                        last = pe.matmul(ps[0:n, 2 * (t % 2) + half, :], ga[:, k, c0:c0 + n], wo[:, k, half * 512:(half + 1) * 512],
                                         start=k == 0, stop=k == KD - 1)
                last.then_inc(y_ps, 1)
                if t >= 1:
                    router(t - 1)
            router(NTT - 1)
            pe.wait_ge(mset, 1)
            for t, (c0, n) in enumerate(TILES):
                for u in range(t):
                    pe.matmul(ps[0:n, 0, t * NE:(t + 1) * NE], onesb[0:P, 0:n], mb[:, u, :], start=u == 0, stop=False)
                pe.matmul(ps[0:n, 0, t * NE:(t + 1) * NE], beforeb[0:n, 0:n], mb[0:n, t, :], start=t == 0, stop=True)
            for t, (c0, n) in enumerate(TILES):
                last = pe.matmul(ps[:, 1, 0:NE], onesb[0:n, :], mb[0:n, t, :], start=t == 0, stop=t == NTT - 1)
            last.then_inc(cnt_ps, 1)
            pe.wait_ge(sel_set, 1)
            for i in range(2 * NTT):
                n = TILES[i // 2][1]
                last = pe.matmul(ps[0:BLK, 2, 0:NBLK], ohr[0:n, i, :], ohb[0:n, i, :], start=i == 0, stop=i == 2 * NTT - 1)
            last.then_inc(idx_ps, 1)

            def turn_rows(src):
                for k in range(KD):
                    last = pe.transpose(ps[:, k // 4, (k % 4) * P:(k % 4) * P + BLK], src[:, k:D:KD], eye[0:BLK, 0:BLK])
                return last

            pe.wait_ge(idx_set, 1)
            pe.wait_ge(gathered[0], 16)
            turn_rows(xg[0]).then_inc(xgt_ps, 1)
            with pe.Fori(0, NE // 2) as i:
                for s in range(2):
                    pe.wait_ge(e_loaded[0][s], 16 * i + 16)
                    pe.wait_ge(e_loaded[1][s], 16 * i + 16)
                    pe.wait_ge(xgt_sb, 2 * i + s + 1)
                    for f in range(KF):
                        pe.wait_ge(hact_sb, (2 * i + s) * KF + f + 1)
                        for w, bank in ((wgv[s], 2 + f % 2), (wuv[s], 4 + f % 2)):
                            for k in range(KD):
                                last = pe.matmul(ps[:, bank, 0:BLK], w[:, k, f, :], xgt[s][:, k, :], start=k == 0, stop=k == KD - 1)
                        last.then_inc(gu_ps, 1)
                    pe.wait_ge(gathered[1 - s], 16 * (i + 1 + s) if s else 16 * i + 16)
                    pe.wait_ge(xgt_sb, 2 * i + s + 1)
                    turn_rows(xg[1 - s]).then_inc(xgt_ps, 1)
                    pe.wait_ge(e_loaded[2][s], 16 * i + 16)
                    pe.wait_ge(hact_sb, (2 * i + s) * KF + KF + 2)
                    pe.wait_ge(yo_sb, 2 * i + s + 1)
                    for half in range(2):
                        for k in range(KF):
                            last = pe.matmul(ps[0:BLK, 6 + half, :], hact[:, k, :], wdv[s][:, k, half * 512:(half + 1) * 512],
                                             start=k == 0, stop=k == KF - 1)
                    last.then_inc(dn_ps, 1)
            count = pe.value_load(over_i[0:1, OVER:OVER + 1], min_val=0, max_val=OVER)
            with pe.If(count > 0):
                pe.wait_ge(yo_sb, NE + 1)
                pe.wait_ge(xgt_sb, NE + 1)
                with pe.Fori(0, count) as i:
                    pe.wait_ge(ov["gat"], 16 * i + 16)
                    pe.wait_ge(ov["load"], 48 * i + 48)
                    turn_rows(xg[0]).then_inc(ov["tps"], 1)
                    pe.wait_ge(ov["tsb"], i + 1)
                    for f in range(KF):
                        for w, bank in ((wgv[0], 2), (wuv[0], 4)):
                            for k in range(KD):
                                last = pe.matmul(ps[:, bank, 0:BLK], w[:, k, f, :], xgt[0][:, k, :], start=k == 0, stop=k == KD - 1)
                        last.then_inc(ov["gu"], 1)
                        pe.wait_ge(ov["ha"], KF * i + f + 1)
                    for half in range(2):
                        for k in range(KF):
                            last = pe.matmul(ps[0:BLK, 6 + half, :], hact[:, k, :], wdv[0][:, k, half * 512:(half + 1) * 512],
                                             start=k == 0, stop=k == KF - 1)
                    last.then_inc(ov["dn"], 1)

        @block.scalar
        def _(ac):
            ac.dma_start(ci[:, :], const[:, C_EYE:C_PM]).then_inc(ci_loaded, 16)
            ac.dma_start(vt_t[0:42, 0:P], a["b_in"][0].rearrange("(m c) -> m c", c=P)).then_inc(rows_loaded, 16)
            for name, r0, r1 in (("b_dw", 42, 46), ("conv_ln_g", 46, 50), ("conv_ln_b", 50, 54), ("b_conv_out", 54, 62)):
                ac.dma_start(vt_t[r0:r1, 0:P], a[name][0].rearrange("(m c) -> m c", c=P)).then_inc(rows_loaded, 16)
            ac.dma_start(rows_b, a["w_dw"][0].rearrange("t (m c) -> (t m) c", c=P)).then_inc(rows_loaded, 16)
            ac.dma_start(eb[:, 9216:9216 + 2 * N], const[:, C_COS:C_COS + 2 * N]).then_inc(trig_loaded, 16)
            for j in range(2):
                ac.dma_start(cst[:, j, :], a["state_conv"][0, 4 * j:4 * j + 4].rearrange("b s c -> (b s) c")).then_inc(state_loaded, 16)
            ac.dma_start(pmask, const[:, C_PM:C_SM]).then_inc(mask_loaded, 16)
            ac.dma_start(wa, a["w_attn_out"][0].rearrange("(k p) n -> p k n", p=P)).then_inc(wa_loaded, 16)
            ac.dma_start(br[:, 0:4], a["b_router_group"][0].partition_broadcast(P)).then_inc(br_loaded, 16)
            ac.dma_start(br[:, 4:36], a["b_router_expert"][0].partition_broadcast(P)).then_inc(br_loaded, 16)
            ac.wait_ge(colb_sb, 2)
            ac.sem_inc(tile_free, 2)

            def evacuate(lo, hi, dst, first, func):
                with ac.Fori(lo, hi) as i:
                    for j in range(6):
                        c = j % 2
                        ac.wait_ge(tile_mm, 6 * i + j + 1)
                        ac.activation(dst[:, bass.ds((6 * i + j - first) * N, N)].rearrange("p (h n) -> p h n", h=2),
                                      ps[:, 2 * c:2 * c + 2, 0:HALF], func, bias=colb[:, bass.ds(6 * i + j, 1)]).then_inc(tile_free, 1)

            evacuate(0, 3, ea, 0, ACT.Identity)
            evacuate(3, 5, z2, 18, ACT.Identity)
            ac.wait_ge(tile_free, 2 + 30)
            ac.activation(z2[:, 4 * N:12 * N], z2[:, 4 * N:12 * N], ACT.Sigmoid).then_inc(sig_u, 1)
            evacuate(5, 7, z2, 18, ACT.Sigmoid)

            for m in range(6):
                ac.wait_ge(k_ps, m + 1)
                if m < 2:
                    ac.copy(kout0[:, m * P:(m + 1) * P], ps[:, m % 4, 3 * P:4 * P]).then_inc(k_sb, 1)
                else:
                    ac.copy(kout12[:, :, (m - 2) * P:(m - 1) * P],
                            ps[:, m % 4, :].rearrange("p (r c) -> p r c", r=4)).then_inc(k_sb, 1)
            ac.wait_ge(s_ps, 1)
            for two in range(2):
                for g in range(3):
                    m = 6 * two + 2 * g
                    last = ac.copy(skv[0:NS, g, two, :], ps[0:NS, 4 + m // 4, (m % 4) * P:(m % 4) * P + 256])
            last.then_inc(s_sb, 1)
            ac.wait_ge(u_ps, 1)
            ac.copy(urow_p[0:PAD, :], ps[0:PAD, 7, :])
            ac.copy(urow_s[0:NS, :], ps[0:NS, 0, :]).then_inc(u_sb, 1)
            for b in range(NB):
                ac.wait_ge(kt_ps, b + 1)
                if b >= 2:
                    ac.wait_ge(st_ps, b - 1)
                ac.copy(ktr[:, b % 2, 8:12, :], ps[:, 3 * (b % 2) + 2, :].rearrange("p (m k) -> p m k", m=4)).then_inc(kt_act, 1)
            ac.wait_ge(smax, 1)
            ac.activation(sp, sp, ACT.Exp, bias=nmx_s, scale=SCALE, accum_out=l_s).then_inc(sprob, 1)
            for i in range(16 + 1):
                if i < 16:
                    ac.wait_ge(pmax, i + 1)
                    ac.activation(prob[:, i % 2, :], prob[:, i % 2, :], ACT.Exp, bias=nmx_p[:, i:i + 1], scale=SCALE,
                                  accum_out=l_p[:, i:i + 1]).then_inc(pexp, 1)
                if i >= 1:
                    j = i - 1
                    ac.wait_ge(pt_ps, j + 1)
                    if j >= 2:
                        ac.wait_ge(pv_ps, j - 1)
                    ac.copy(prt[:, j % 2, 4:6, :], ps[:, 5, 0:256].rearrange("p (m k) -> p m k", m=2)).then_inc(pt_act, 1)
            ac.wait_ge(cen_sb, 2)
            ac.activation(acc, cen, ACT.Square).then_inc(sq_sb, 1)
            ac.wait_ge(veps, 1)
            ac.activation(rstd_c, rstd_c, ACT.Sqrt).then_inc(csd, 1)
            ac.wait_ge(cnorm, 1)
            for c in range(CT):
                ac.activation(acc[:, c, :], cen[:, c, :], ACT.Silu, bias=clb_c[:, c:c + 1], scale=clg_c[:, c:c + 1]).then_inc(cact, 1)
            for t, (c0, n) in enumerate(TILES):
                s = t % 2
                ac.wait_ge(hvar, t + 1)
                ac.activation(sd[0:n], rs[0:n], ACT.Sqrt).then_inc(hsd, 1)
                ac.wait_ge(hscale, t + 1)
                ac.activation(hrow[0:n, s, :], hrow[0:n, s, :], ACT.Identity, bias=nmr[0:n], scale=rs[0:n]).then_inc(hnorm, 1)
                if t >= 1:
                    c1, n1 = TILES[t - 1]
                    ac.wait_ge(ht_ps, t)
                    if t >= 2:
                        ac.wait_ge(lg_ps, t - 1)
                    ac.copy(hcol[:, :, 0:n1], ps[:, 4:6, :].rearrange("p b (k c) -> p (b k) c", k=4)[:, :, 0:n1]).then_inc(ht_sb, 1)
            ac.wait_ge(ht_ps, NTT)
            ac.wait_ge(lg_ps, NTT - 1)
            ac.copy(hcol[:, :, 0:NS], ps[:, 4:6, :].rearrange("p b (k c) -> p (b k) c", k=4)[:, :, 0:NS]).then_inc(ht_sb, 1)
            ac.wait_ge(rmax, 1)
            ac.activation(rt_g3, rt_g3, ACT.Exp).then_inc(rexp, 1)
            ac.wait_ge(rmax2, 1)
            ac.activation(rt_d, rt_d, ACT.Exp).then_inc(rexp2, 1)
            ac.sem_inc(yo_sb, 1)
            def expert_pair(i):
                for s in range(2):
                    for f in range(KF):
                        ac.wait_ge(gu_ps, (2 * i + s) * KF + f + 1)
                        ac.wait_ge(hact_sb, (2 * i + s) * KF + f + 1)
                        ac.activation(gact[:, f, :], ps[:, 2 + f % 2, 0:BLK], ACT.Silu).then_inc(gact_sb, 1)
                    ac.wait_ge(dn_ps, 2 * i + s + 1)
                    if not isinstance(i, int):
                        ac.wait_ge(scattered[s], 16 * i)
                    ac.copy(yo[s].rearrange("p (h n) -> p h n", h=2), ps[0:BLK, 6:8, :]).then_inc(yo_sb, 1)

            expert_pair(0)
            with ac.Fori(1, NE // 2) as i:
                expert_pair(i)
            ac.wait_ge(idx_set, 1)
            count = ac.value_load(over_i[0:1, OVER:OVER + 1], min_val=0, max_val=OVER)
            with ac.If(count > 0):
                with ac.Fori(0, count) as i:
                    for f in range(KF):
                        ac.wait_ge(ov["gu"], KF * i + f + 1)
                        ac.activation(gact[:, f, :], ps[:, 2, 0:BLK], ACT.Silu).then_inc(ov["ga"], 1)
                    ac.wait_ge(ov["dn"], i + 1)
                    ac.copy(yo[0].rearrange("p (h n) -> p h n", h=2), ps[0:BLK, 6:8, :]).then_inc(ov["yo"], 1)
            for t, (c0, n) in enumerate(TILES):
                s = t % 2
                ac.wait_ge(fvar, t + 1)
                ac.activation(sd[0:n], rs[0:n], ACT.Sqrt).then_inc(fsd, 1)
                ac.wait_ge(fscale, t + 1)
                ac.activation(fh[s][0:n], fh[s][0:n], ACT.Identity, bias=nmr[0:n], scale=rs[0:n]).then_inc(fnorm, 1)

        @block.vector
        def _(ve):
            chain = [0]

            def link(ins):
                chain[0] += 1
                ins.then_inc(dve_chain, 1)
                ve.wait_ge(dve_chain, chain[0])

            ve.wait_ge(colb_ps, 1)
            ve.tensor_copy(colb[:, 0:62], ps[:, 3, 0:62]).then_inc(colb_sb, 1)
            ve.tensor_copy(wdw_c, ps[:, 3, 64:64 + TAPS * CT]).then_inc(colb_sb, 1)
            for t, (c0, n) in enumerate(TILES):
                ve.wait_ge(xt_ps, t + 1)
                src = ps[:, 4 + 2 * (t % 2):6 + 2 * (t % 2), :].rearrange("p b (k c) -> p (b k) c", k=4)
                ve.tensor_copy(xt[:, :, c0:c0 + n], src[:, :, 0:n]).then_inc(xt_sb, 1)
            ve.wait_ge(trig_loaded, 16)
            for m in range(12):
                ve.wait_ge(rot_ps, m + 1)
                ve.tensor_tensor(rtmp[:, m % 2, :].rearrange("p (h n) -> p h n", h=2), ps[:, 4 + 2 * (m % 2):6 + 2 * (m % 2), 0:HALF],
                                 sin.rearrange("p (h n) -> p h n", h=2), ALU.mult).then_inc(rot_used, 1)
                link(ve.tensor_tensor(zqkv[:, m, :], zqkv[:, m, :], cos, ALU.mult))
                ve.wait_ge(rot_used, m + 1)
                ve.tensor_tensor(zqkv[:, m, :], zqkv[:, m, :], rtmp[:, m % 2, :], ALU.add).then_inc(rotated, 1)
            ve.wait_ge(pads_set, 1)
            ve.wait_ge(state_ps, 1)
            for j in range(2):
                for c in range(CT):
                    last = ve.tensor_copy(sext[:, c, 4 * j:4 * j + 4, 0:PAD],
                                          ps[:, 4 + j, c * P:c * P + 4 * PAD].rearrange("p (b s) -> p b s", b=4))
            last.then_inc(state_sb, 1)
            ve.wait_ge(sig_u, 1)
            ve.tensor_tensor(uext[:, :, PAD:PAD + SEQ], ua[:, :, 0:SEQ], ub[:, :, 0:SEQ], ALU.mult)
            for c in range(CT):
                ve.tensor_tensor(sext[:, c, :, PAD:PAD + NT], ua[:, c, SEQ:N].rearrange("p (b t) -> p b t", t=NT),
                                 ub[:, c, SEQ:N].rearrange("p (b t) -> p b t", t=NT), ALU.mult)
            link(ve.tensor_tensor(cst_u, ua[:, :, SEQ:N], ub[:, :, SEQ:N], ALU.mult))
            ve.nop().then_inc(u_set, 1)

            def conv_parts():
                for c in range(CT):
                    yield c, acc[:, c, 0:SEQ], lambda k, c=c: uext[:, c, bass.ds(k, SEQ)] if not isinstance(k, int) else uext[:, c, k:k + SEQ]
                for c in range(CT):
                    yield (c, acc[:, c, SEQ:N].rearrange("p (b t) -> p b t", t=NT),
                           lambda k, c=c: sext[:, c, :, bass.ds(k, NT)] if not isinstance(k, int) else sext[:, c, :, k:k + NT])

            for c, dst, win in conv_parts():
                ve.tensor_scalar(dst, win(0), wdw_c[:, c:c + 1], bdw_c[:, c:c + 1], ALU.mult, ALU.add).then_inc(conv_step, 1)
            with ve.Fori(1, TAPS) as k:
                for j, (c, dst, win) in enumerate(conv_parts()):
                    ve.wait_ge(conv_step, 8 * k + j - 7)
                    ve.scalar_tensor_tensor(dst, win(k), wdw_c[:, bass.ds(k * CT + c, 1)], dst, ALU.mult, ALU.add).then_inc(conv_step, 1)
            ve.wait_ge(conv_step, 8 * TAPS)
            ve.nop().then_inc(conv_done, 1)
            for m in range(6):
                ve.wait_ge(v_ps, m + 1)
                ve.tensor_copy(vt[:, :, m * P:(m + 1) * P], ps[:, 4 + m % 4, :].rearrange("p (r c) -> p r c", r=4)).then_inc(v_sb, 1)
            ve.wait_ge(qbd_zero, 1)
            for hh in range(2):
                rows = slice(64 * hh, 64 * hh + 64)
                last = ve.tensor_copy(qbd[rows, :, :, hh], zqkv[rows, Q0:Q0 + 6, SEQ:N])
            last.then_inc(qbd_set, 1)
            ve.wait_ge(u_ps, 1)
            for b in range(NB):
                ve.wait_ge(kt_ps, b + 1)
                if b >= 2:
                    ve.wait_ge(st_ps, b - 1)
                ve.tensor_copy(ktr[:, b % 2, 0:8, :], ps[:, 3 * (b % 2):3 * (b % 2) + 2, :].rearrange("p b (m k) -> p (b m) k", m=4)).then_inc(kt_dve, 1)
            ve.wait_ge(st_ps, NB + 1)
            ve.tensor_copy(st_sb, ps[:, 6, 0:3 * P]).then_inc(st_done, 1)
            ve.tensor_copy(stn_sb[0:NS, :], ps[0:NS, 7, 0:3 * P]).then_inc(st_done, 1)
            ve.wait_ge(sback_ps, 1)
            ve.wait_ge(mask_loaded, 32)
            link(ve.tensor_tensor_reduce(sp, ps[:, 0, 0:SKEYS], smask, 1.0, -3e38, ALU.add, ALU.max, nmx_s))
            ve.tensor_scalar(nmx_s, nmx_s, -SCALE, None, ALU.mult).then_inc(smax, 1)
            ve.wait_ge(sprob, 1)
            link(ve.reciprocal(rinv_s, l_s))
            ve.tensor_scalar(sp, sp, rinv_s, None, ALU.mult).then_inc(spn, 1)
            ve.wait_ge(spt_ps, 1)
            ve.tensor_copy(st_sb, ps[:, 1, 0:3 * P]).then_inc(spt_sb, 1)
            ve.tensor_copy(stn_sb[0:NS, :], ps[0:NS, 2, 0:3 * P]).then_inc(spt_sb, 1)
            ve.wait_ge(so_ps, 1)
            for hh in range(2):
                rows = slice(64 * hh, 64 * hh + 64)
                last = ve.tensor_copy(at[rows, :, SEQ:N], ps[rows, 4:6, 0:64].rearrange("p h (b j) -> p h b j", j=2)[:, :, :, hh])
            last.then_inc(so_sb, 1)

            def mask_max(i):
                r, s = i // 4, i % 2
                ve.wait_ge(qk_ps, i + 1)
                if i >= 2:
                    ve.wait_ge(pt_ps, i - 1)
                sv = ps[:, 2 * s:2 * s + 2, :].rearrange("p b k -> p (b k)")
                link(ve.tensor_tensor_reduce(prob[:, s, 0:SEQ], sv[:, 0:SEQ], pmask[:, r * SEQ:(r + 1) * SEQ], 1.0, -3e38,
                                             ALU.add, ALU.max, pmx[:, 0:1]))
                link(ve.tensor_tensor_reduce(prob[:, s, SEQ:PKEYS], sv[:, SEQ:PKEYS], pmask[:, 4 * SEQ:4 * SEQ + 2 * P], 1.0, pmx[:, 0:1],
                                             ALU.add, ALU.max, pmx[:, 1:2]))
                ve.tensor_scalar(nmx_p[:, i:i + 1], pmx[:, 1:2], -SCALE, None, ALU.mult).then_inc(pmax, 1)

            for i in range(16 + 1):
                if i < 16:
                    mask_max(i)
                if i >= 1:
                    j = i - 1
                    r, h = divmod(j, 4)
                    ve.wait_ge(pt_ps, j + 1)
                    if j >= 2:
                        ve.wait_ge(pv_ps, j - 1)
                    ve.tensor_copy(prt[:, j % 2, 0:4, :], ps[:, 4, :].rearrange("p (m k) -> p m k", m=4)).then_inc(pt_dve, 1)
                if i in (6, 10, 14, 16):
                    q = {6: 0, 10: 1, 14: 2, 16: 3}[i]
                    if q < 3:
                        ve.wait_ge(pv_ps, 4 * q + 4)
                        link(ve.reciprocal(rinv, l_p[:, 4 * q:4 * q + 4]))
                        ve.tensor_tensor(atk[:, :].rearrange("p (h e) -> p h e", h=4),
                                         ps[:, 6 + q % 2, 0:256].rearrange("p (h e) -> p h e", h=4),
                                         rinv.unsqueeze(2).to_broadcast([P, 4, HD]), ALU.mult).then_inc(otok, 1)
                if i in (8, 12):
                    q = i // 4 - 2
                    ve.wait_ge(at_ps, q + 1)
                    ve.tensor_copy(at[:, :, q:SEQ:4], ps[:, 6 + q % 2, 256:512].rearrange("p (m k) -> p m k", m=2)).then_inc(at_sb, 1)
            ve.wait_ge(at_ps, 3)
            ve.tensor_copy(at[:, :, 2:SEQ:4], ps[:, 6, 256:512].rearrange("p (m k) -> p m k", m=2)).then_inc(at_sb, 1)
            ve.wait_ge(pv_ps, 16)
            link(ve.reciprocal(rinv, l_p[:, 12:16]))
            ve.tensor_tensor(atk[:, :].rearrange("p (h e) -> p h e", h=4),
                             ps[:, 7, 0:256].rearrange("p (h e) -> p h e", h=4),
                             rinv.unsqueeze(2).to_broadcast([P, 4, HD]), ALU.mult).then_inc(otok, 1)
            ve.wait_ge(at_ps, 4)
            ve.tensor_copy(at[:, :, 3:SEQ:4], ps[:, 7, 256:512].rearrange("p (m k) -> p m k", m=2)).then_inc(at_sb, 1)

            ve.wait_ge(mean_ps, 1)
            ve.wait_ge(stored, 16 * 8)
            for half in range(2):
                cols = slice(half * HALF, (half + 1) * HALF)
                ve.tensor_tensor(cen[:, :, cols], acc[:, :, cols], ps[:, half, 0:HALF].unsqueeze(1).broadcast_to([P, CT, HALF]),
                                 ALU.subtract).then_inc(cen_sb, 1)
            ve.wait_ge(var_ps, 1)
            ve.tensor_scalar(rstd_c.rearrange("p (h n) -> p h n", h=2), ps[:, 2:4, 0:HALF], EPS, None, ALU.add).then_inc(veps, 1)
            ve.wait_ge(csd, 1)
            link(ve.reciprocal(rstd_c, rstd_c))
            ve.wait_ge(cen_sb, 2)
            ve.tensor_tensor(cen, cen, rstd_c.unsqueeze(1).broadcast_to([P, CT, N]), ALU.mult).then_inc(cnorm, 1)
            ve.wait_ge(tile_free, 2 + MT)
            for m in range(KD):
                s = 4 * (m % 2)
                ve.wait_ge(br_ps, m + 1)
                v2 = lambda t: t.rearrange("p (h n) -> p h n", h=2)
                ve.scalar_tensor_tensor(v2(gc[:, m, :]), ps[:, s:s + 2, 0:HALF], bco_c[:, m:m + 1], v2(gc[:, m, :]), ALU.add, ALU.mult)
                ve.tensor_tensor(v2(ga[:, m, :]), ps[:, s + 2:s + 4, 0:HALF], v2(ga[:, m, :]), ALU.mult).then_inc(br_used, 1)
            ve.wait_ge(rows1_loaded, 32)
            ve.wait_ge(br_loaded, 32)
            for t, (c0, n) in enumerate(TILES):
                s = t % 2
                ve.wait_ge(y_ps, t + 1)
                ve.wait_ge(xrow_loaded[s], 16 * (t // 2 + 1))
                if t >= 2:
                    ve.wait_ge(h_stored[s], 16 * (t // 2))
                    ve.wait_ge(ht_ps, t - 1)
                hs = hrow[0:n, s, :]
                ve.scalar_tensor_tensor(hs.rearrange("p (h n) -> p h n", h=2), xrow[0:n, s, :].rearrange("p (h n) -> p h n", h=2), ALPHA,
                                        ps[0:n, 2 * s:2 * s + 2, :], ALU.mult, ALU.add).then_inc(y_used, 1)
                ve.wait_ge(y_used, t + 1)
                for half in range(2):
                    st = ve.bn_stats(stats[0:n, 6 * half:6 * half + 6], hrow[0:n, s, half * 512:(half + 1) * 512])
                link(st)
                link(ve.bn_aggr(mv[0:n], stats[0:n, 0:12]))
                ve.tensor_scalar(rs[0:n], mv[0:n, 1:2], EPS, None, ALU.add).then_inc(hvar, 1)
                ve.wait_ge(hsd, t + 1)
                link(ve.reciprocal(rs[0:n], sd[0:n]))
                ve.scalar_tensor_tensor(nmr[0:n], mv[0:n, 0:1], -1.0, rs[0:n], ALU.mult, ALU.mult).then_inc(hscale, 1)
                ve.wait_ge(hnorm, t + 1)
                link(ve.tensor_tensor(hs, hs, g1row[0:n], ALU.mult))
                ve.tensor_tensor(hs, hs, b1row[0:n], ALU.add).then_inc(hdone, 1)
                if t >= 1:
                    c1, n1 = TILES[t - 1]
                    ve.wait_ge(lg_ps, t)
                    ve.tensor_tensor(lg[0:n1, t - 1, :], ps[0:n1, 6 + (t - 1) % 2, 0:36], br[0:n1], ALU.add).then_inc(lg_sb, 1)
            ve.wait_ge(lg_ps, NTT)
            ve.tensor_tensor(lg[0:NS, 4, :], ps[0:NS, 6, 0:36], br[0:NS], ALU.add).then_inc(lg_sb, 1)
            ve.wait_ge(lg_sb, NTT)

            def bc(x, shape):
                return x.to_broadcast(shape)

            S4, S32 = [P, NTT, NGRP], [P, NTT, NE]
            L4, L32 = lg[:, :, 0:4], lg[:, :, 4:36]
            ve.wait_ge(stored, 16 * 8)
            link(ve.memset(rank, 0.0))
            link(ve.tensor_reduce(m1, L4, AX_X, ALU.max))
            link(ve.tensor_tensor(rt_a4, L4, bc(m1.unsqueeze(2), S4), ALU.is_equal))
            link(ve.tensor_scalar(rt_b4, iota_e[:, 0:4].unsqueeze(1).broadcast_to(S4), -64.0, None, ALU.add))
            link(ve.tensor_tensor(rt_c4, rt_b4, rt_a4, ALU.mult))
            link(ve.tensor_reduce(i1, rt_c4, AX_X, ALU.min))
            link(ve.tensor_tensor(rt_a4, rt_b4, bc(i1.unsqueeze(2), S4), ALU.is_equal))
            ve.tensor_tensor(rt_g3, L4, bc(m1.unsqueeze(2), S4), ALU.subtract).then_inc(rmax, 1)
            link(ve.tensor_scalar(rt_b4, rt_a4, -1.0, 1e30, ALU.add, ALU.mult))
            link(ve.tensor_tensor(em4, L32.rearrange("p t (g e) -> p t g e", g=NGRP),
                                  bc(rt_b4.unsqueeze(3), [P, NTT, NGRP, NPER]), ALU.add))
            link(ve.tensor_scalar(io32, iota_e.unsqueeze(1).broadcast_to(S32), -64.0, None, ALU.add))
            for k in range(2):
                link(ve.tensor_reduce(v12[:, k, :], em, AX_X, ALU.max))
                link(ve.tensor_tensor(rt32, em, bc(v12[:, k, :].unsqueeze(2), S32), ALU.is_equal))
                link(ve.tensor_tensor(rt32, rt32, io32, ALU.mult))
                link(ve.tensor_reduce(e12[:, k, :], rt32, AX_X, ALU.min))
                link(ve.tensor_tensor(oh[:, k], io32, bc(e12[:, k, :].unsqueeze(2), S32), ALU.is_equal))
                if k == 0:
                    link(ve.scalar_tensor_tensor(em, oh[:, 0], -3e38, em, ALU.mult, ALU.add))
            link(ve.tensor_tensor(mb, oh[:, 0], oh[:, 1], ALU.add))
            ve.nop().then_inc(mset, 1)
            ve.tensor_tensor(rt_d, v12[:, 1, :], v12[:, 0, :], ALU.subtract).then_inc(rmax2, 1)
            ve.wait_ge(rexp, 1)
            link(ve.tensor_reduce(i1, rt_g3, AX_X, ALU.add))
            ve.wait_ge(rexp2, 1)
            link(ve.scalar_tensor_tensor(m1, rt_d, 1.0, i1, ALU.add, ALU.mult))
            gw = gates[:, :].rearrange("p (k t) -> p k t", k=2)
            link(ve.reciprocal(gw[:, 0, :], m1))
            link(ve.tensor_tensor(gw[:, 1, :], gw[:, 0, :], rt_d, ALU.mult))
            ve.wait_ge(cnt_ps, 1)
            link(ve.tensor_copy(cnt, ps[:, 1, 0:NE]))
            link(ve.tensor_scalar(nov, cnt, float(BLK), None, ALU.is_gt))
            for j in range(2, LEVELS + 1):
                link(ve.scalar_tensor_tensor(nov, cnt, float(j * BLK), nov, ALU.is_gt, ALU.add))
            link(ve.tensor_copy(ovend[:, 0, :], nov))
            cur = 0
            for sh in (1, 2, 4, 8, 16):
                link(ve.tensor_copy(ovend[:, 1 - cur, 0:sh], ovend[:, cur, 0:sh]))
                link(ve.tensor_tensor(ovend[:, 1 - cur, sh:NE], ovend[:, cur, sh:NE], ovend[:, cur, 0:NE - sh], ALU.add))
                cur = 1 - cur
            oe = ovend[:, cur, :]
            link(ve.tensor_tensor(ovst, oe, nov, ALU.subtract))
            for b in range(OVER):
                link(ve.tensor_scalar(tmp32, oe, float(b), None, ALU.is_le))
                link(ve.tensor_reduce(ovf[:, b:b + 1], tmp32, AX_X, ALU.add))
            link(ve.tensor_scalar(ovf[:, 0:OVER], ovf[:, 0:OVER], float(NE - 1), None, ALU.min))
            link(ve.tensor_copy(ovf[:, OVER:OVER + 1], oe[:, NE - 1:NE]))
            link(ve.tensor_copy(over_i[:, :], ovf))
            link(ve.tensor_copy(rank[:, 0:4, :], ps[:, 0, 0:4 * NE].rearrange("p (t e) -> p t e", e=NE)))
            link(ve.tensor_copy(rank[0:NS, 4, :], ps[0:NS, 0, 4 * NE:5 * NE]))
            for k in range(2):
                link(ve.tensor_tensor(rt32, oh[:, k], rank, ALU.mult))
                link(ve.tensor_reduce(rk[:, :, k], rt32, AX_X, ALU.add))
                link(ve.tensor_tensor(rt32, oh[:, k], iota_e.unsqueeze(1).broadcast_to(S32), ALU.mult))
                link(ve.tensor_reduce(ek[:, :, k], rt32, AX_X, ALU.add))
                link(ve.tensor_tensor(rt32, oh[:, k], ovst.unsqueeze(1).broadcast_to(S32), ALU.mult))
                link(ve.tensor_reduce(ok[:, :, k], rt32, AX_X, ALU.add))
            link(ve.tensor_scalar(qk, rk, float(BLK), None, ALU.is_ge))
            link(ve.tensor_copy(q0, qk))
            for j in range(2, LEVELS + 1):
                link(ve.scalar_tensor_tensor(qk, rk, float(j * BLK), qk, ALU.is_ge, ALU.add))
            link(ve.scalar_tensor_tensor(ok, qk, float(NE - 1), ok, ALU.add, ALU.add))
            link(ve.tensor_tensor(ok, ok, ek, ALU.subtract))
            link(ve.tensor_tensor(ok, ok, q0, ALU.mult))
            link(ve.tensor_tensor(ok, ok, ek, ALU.add))
            link(ve.scalar_tensor_tensor(rk, qk, -float(BLK), rk, ALU.mult, ALU.add))
            fl = lambda x: x.rearrange("p t k -> p (t k)")
            R3, B3 = [P, 2 * NTT, BLK], [P, 2 * NTT, NBLK]
            link(ve.tensor_tensor(ohr, iota_r.unsqueeze(1).broadcast_to(R3), fl(rk).unsqueeze(2).to_broadcast(R3), ALU.is_equal))
            link(ve.tensor_tensor(ohb, iota_b.unsqueeze(1).broadcast_to(B3), fl(ok).unsqueeze(2).to_broadcast(B3), ALU.is_equal))
            link(ve.tensor_tensor(ohb, ohb, fl(token).unsqueeze(2).to_broadcast(B3), ALU.mult))
            ve.nop().then_inc(sel_set, 1)
            ve.wait_ge(idx_ps, 1)
            tv, te = tabf[0:BLK, 0, :], tabf[0:BLK, 1, :]
            link(ve.tensor_scalar(tv, ps[0:BLK, 2, 0:NBLK], -1.0, None, ALU.add))
            link(ve.tensor_scalar(te, tv, 0.0, float(OOB), ALU.is_lt, ALU.mult))
            link(ve.tensor_tensor(te, te, tv, ALU.add))
            link(ve.tensor_copy(sidx[0:BLK, :], te))
            link(ve.tensor_scalar(te, tv, float(N), -float(N), ALU.is_ge, ALU.mult))
            link(ve.tensor_tensor(tv, tv, te, ALU.add))
            link(ve.tensor_scalar(tv, tv, 0.0, None, ALU.max))
            link(ve.tensor_copy(gidx[0:BLK, :], tv))
            ve.nop().then_inc(idx_set, 1)

            def rows_out(s):
                src = ps[:, 0:2, :].rearrange("p b (k c) -> p (b k) c", k=4)[:, :, 0:BLK]
                return ve.tensor_copy(xgt[s], src)

            ve.wait_ge(xgt_ps, 1)
            rows_out(0).then_inc(xgt_sb, 1)
            ve.nop().then_inc(hact_sb, 2)

            def expert_pair(i):
                for s in range(2):
                    if not isinstance(i, int) or s > 0:
                        ve.wait_ge(dn_ps, 2 * i + s)
                    for f in range(KF):
                        ve.wait_ge(gact_sb, (2 * i + s) * KF + f + 1)
                        ve.tensor_tensor(hact[:, f, :], ps[:, 4 + f % 2, 0:BLK], gact[:, f, :], ALU.mult).then_inc(hact_sb, 1)
                    ve.wait_ge(xgt_ps, 2 * i + s + 2)
                    rows_out(1 - s).then_inc(xgt_sb, 1)

            expert_pair(0)
            with ve.Fori(1, NE // 2) as i:
                expert_pair(i)
            count = ve.value_load(over_i[0:1, OVER:OVER + 1], min_val=0, max_val=OVER)
            with ve.If(count > 0):
                with ve.Fori(0, count) as i:
                    ve.wait_ge(ov["tps"], i + 1)
                    rows_out(0).then_inc(ov["tsb"], 1)
                    for f in range(KF):
                        ve.wait_ge(ov["ga"], KF * i + f + 1)
                        ve.tensor_tensor(hact[:, f, :], ps[:, 4, 0:BLK], gact[:, f, :], ALU.mult).then_inc(ov["ha"], 1)

            ve.wait_ge(rows2_loaded, 32)
            for t, (c0, n) in enumerate(TILES):
                s = t % 2
                ve.wait_ge(fin_loaded[s], 48 * (t // 2 + 1))
                hs, y1, y2 = fh[s][0:n], fy1[s][0:n], fy2[s][0:n]
                link(ve.tensor_scalar(y1, y1, gw[0:n, 0, t:t + 1], None, ALU.mult))
                link(ve.scalar_tensor_tensor(y1, y2, gw[0:n, 1, t:t + 1], y1, ALU.mult, ALU.add))
                link(ve.scalar_tensor_tensor(hs, hs, ALPHA, y1, ALU.mult, ALU.add))
                for half in range(2):
                    st = ve.bn_stats(stats[0:n, 6 * half:6 * half + 6], fh[s][0:n, half * 512:(half + 1) * 512])
                link(st)
                link(ve.bn_aggr(mv[0:n], stats[0:n, 0:12]))
                ve.tensor_scalar(rs[0:n], mv[0:n, 1:2], EPS, None, ALU.add).then_inc(fvar, 1)
                ve.wait_ge(fsd, t + 1)
                link(ve.reciprocal(rs[0:n], sd[0:n]))
                ve.scalar_tensor_tensor(nmr[0:n], mv[0:n, 0:1], -1.0, rs[0:n], ALU.mult, ALU.mult).then_inc(fscale, 1)
                ve.wait_ge(fnorm, t + 1)
                link(ve.tensor_tensor(hs, hs, g2row[0:n], ALU.mult))
                ve.tensor_tensor(hs, hs, b2row[0:n], ALU.add).then_inc(fdone, 1)

        @block.gpsimd
        def _(po):
            po.memset(onesm[:, :], 1.0 / CC)
            po.memset(uext[:, :, 0:PAD], 0.0).then_inc(pads_set, 1)
            po.memset(onesb[:, :], 1.0)
            po.memset(logits[:, :], 0.0)
            po.wait_ge(ci_loaded, 16)
            po.tensor_copy(beforeb[:, :], before).then_inc(pads_set, 1)
            po.wait_ge(tile_mm, 2)
            for b in range(NB):
                for g, dst in enumerate((kv0s, kv1s, kv2s)):
                    w = caches[g].shape[1]
                    keep = dst.shape[2] - NT
                    src = caches[g][b, w - keep:w].rearrange("s two h e -> (s two h e)").rearrange("(c f) -> c f", c=32)
                    po.dma_start(dst[0, b, 0:keep].rearrange("s two h e -> (s two h e)").rearrange("(c f) -> c f", c=32), src).then_inc(copied, 16)
                po.dma_start(conv_s[0, b, 0:PAD - NT].rearrange("s c -> (s c)").rearrange("(c f) -> c f", c=16),
                             a["state_conv"][0, b, NT:PAD].rearrange("s c -> (s c)").rearrange("(c f) -> c f", c=16)).then_inc(copied, 16)

            def load_cache(dst, b, two, done):
                c = caches
                po.dma_start(dst[:, 0, :], c[0][b, :, two].rearrange("s h e -> s (h e)")).then_inc(done, 16)
                po.dma_start(dst[:, 1:5, :], c[1][b, :, two].rearrange("(p t) h e -> p t (h e)", t=4)).then_inc(done, 16)
                po.dma_start(dst[:, 5, :], c[2][b, :, two].rearrange("(a t) h e -> a t (h e)", t=16)[:, 0:4, :]).then_inc(done, 16)

            for b in range(2):
                load_cache(kc[:, b], b, 0, kc_loaded[b])
            po.wait_ge(rotated, 12)
            for b in range(2):
                load_cache(vc[:, b], b, 1, vc_loaded[b])
            po.wait_ge(tile_mm, MT)
            po.memset(eb[:, 4320:4704], 0.0).then_inc(qbd_zero, 1)
            po.wait_ge(k_sb, 6)
            po.wait_ge(v_sb, 6)
            po.dma_start(kv0p[0, 0, :, 0].rearrange("s h e -> s (h e)"), kout0).then_inc(kout_stored, 16)
            po.dma_start(kv0p[0, 0, :, 1].rearrange("s h e -> s (h e)"), vt[:, 3, 0:256]).then_inc(stored, 16)
            for g, dst in ((1, kv1p), (2, kv2p)):
                rows = dst[0, 0].rearrange("(p r) two h e -> p r two (h e)", r=4)
                po.dma_start(rows[:, :, 0, :], kout12[:, :, (g - 1) * 256:g * 256]).then_inc(kout_stored, 16)
                po.dma_start(rows[:, :, 1, :], vt[:, :, g * 256:(g + 1) * 256]).then_inc(stored, 16)
            po.wait_ge(s_sb, 1)
            for g, dst in enumerate((kv0s, kv1s, kv2s)):
                w = dst.shape[2]
                for t in range(NT):
                    po.dma_start(dst[0, :, w - NT + t].rearrange("b two h e -> b (two h e)"),
                                 skv[t:NS:NT, g].rearrange("p two c -> p (two c)")).then_inc(kout_stored, 16)
            po.wait_ge(u_sb, 1)
            po.dma_start(conv_p[0, 0], urow_p[0:PAD, :]).then_inc(stored, 16)
            for t in range(NT):
                po.dma_start(conv_s[0, :, PAD - NT + t], urow_s[t:NS:NT, :]).then_inc(stored, 16)
            for b in range(2, NB):
                po.wait_ge(kt_ps, b - 1)
                load_cache(kc[:, b % 2], b, 0, kc_loaded[b % 2])
            for b in range(2, NB):
                po.wait_ge(vs_used, b - 1)
                load_cache(vc[:, b % 2], b, 1, vc_loaded[b % 2])
            for m in range(KD):
                po.wait_ge(br_used, m + 1)
                po.tensor_tensor(ga[:, m, :], ga[:, m, :], gc[:, m, :], ALU.add).then_inc(merged, 1)
            for t, (c0, n) in enumerate(TILES):
                po.wait_ge(hdone, t + 1)
                po.dma_start(h_dram[c0:c0 + n], hrow[0:n, t % 2, :]).then_inc(h_stored[t % 2], 16)
            po.wait_ge(idx_set, 1)
            po.wait_ge(h_stored[0], 48)
            po.wait_ge(h_stored[1], 32)

            def gather(s, col, done, copied_sem, value):
                po.tensor_copy(idx_t[0:BLK, s:s + 1], gidx[0:BLK, col]).then_inc(copied_sem, 1)
                po.wait_ge(copied_sem, value)
                po.sem_inc(pool_steps, 1)
                po.indirect_dma_start(out=xg[s], out_offset=None, in_=h_dram,
                                      in_offset=bass.IndirectOffsetOnAxis(ap=idx_t[0:BLK, s:s + 1], axis=0)).then_inc(done, 16)

            def scatter(s, col, done, copied_sem, value):
                po.tensor_copy(idx_t[0:BLK, 2 + s:3 + s], sidx[0:BLK, col]).then_inc(copied_sem, 1)
                po.wait_ge(copied_sem, value)
                po.sem_inc(pool_steps, 1)
                po.indirect_dma_start(out=y_dram, out_offset=bass.IndirectOffsetOnAxis(ap=idx_t[0:BLK, 2 + s:3 + s], axis=0),
                                      in_=yo[s], in_offset=None, bounds_check=2 * N - 1, oob_is_err=False).then_inc(done, 16)

            for s in range(2):
                gather(s, slice(s, s + 1), gathered[s], idx_set_e, s + 1)
            with po.Fori(0, NE // 2) as i:
                for s in range(2):
                    po.wait_ge(xgt_ps, 2 * i + s + 1)
                    gather(s, bass.ds(2 * i + s + 2, 1), gathered[s], idx_set_e, 4 * i + 2 * s + 3)
                    po.wait_ge(yo_sb, 2 * i + s + 2)
                    scatter(s, bass.ds(2 * i + s, 1), scattered[s], idx_set_e, 4 * i + 2 * s + 4)
            for s in range(2):
                po.wait_ge(gathered[s], 16 * (NE // 2 + 1))
                po.wait_ge(scattered[s], 16 * (NE // 2))
            po.wait_ge(xgt_ps, NE + 1)
            count = po.value_load(over_i[0:1, OVER:OVER + 1], min_val=0, max_val=OVER)
            with po.If(count > 0):
                with po.Fori(0, count) as i:
                    gather(0, bass.ds(i + NE, 1), ov["gat"], ov["idx"], 2 * i + 1)
                    po.wait_ge(ov["yo"], i + 1)
                    scatter(0, bass.ds(i + NE, 1), ov["sca"], ov["idx"], 2 * i + 2)
                    po.wait_ge(ov["sca"], 16 * i + 16)
                    po.sem_inc(pool_steps, 1)
            po.nop().then_inc(over_done, 1)
            for t, (c0, n) in enumerate(TILES):
                po.wait_ge(fdone, t + 1)
                dst = y_prompt[0, c0:c0 + n] if t < 4 else y_sample.rearrange("b t d -> (b t) d")
                po.dma_start(dst, fh[t % 2][0:n]).then_inc(y_stored[t % 2], 16)
            po.wait_ge(y_stored[0], 48)
            po.wait_ge(y_stored[1], 32)
            po.wait_ge(copied, 16 * 4 * NB)
            po.wait_ge(stored, 16 * 8)
            po.wait_ge(kout_stored, 16 * 15)


INPUTS = ['x_prompt', 'x_sample', 'cache_kv_w128', 'cache_kv_w512', 'cache_kv_w2048', 'state_conv', 'w_in', 'b_in', 'w_dw',
          'b_dw', 'conv_ln_g', 'conv_ln_b', 'w_conv_out', 'b_conv_out', 'w_attn_out', 'w_o', 'ln1_g', 'ln1_b',
          'w_router_group', 'b_router_group', 'w_router_expert', 'b_router_expert', 'w_expert_gate', 'w_expert_up',
          'w_expert_down', 'ln2_g', 'ln2_b']
OUTPUTS = [(1, SEQ, D), (NB, NT, D), (1, 1, 128, 2, 4, 64), (1, 1, 512, 2, 4, 64), (1, 1, 512, 2, 4, 64), (1, 1, PAD, CC),
           (1, NB, 128, 2, 4, 64), (1, NB, 512, 2, 4, 64), (1, NB, 516, 2, 4, 64), (1, NB, PAD, CC)]


def kernel(**inputs):
    from concourse import bacc
    from concourse.bass_utils import run_bass_kernel_spmd

    nc = bacc.Bacc("TRN2", target_bir_lowering=False, num_devices=1)
    arrays, args = {}, {}
    for name in INPUTS:
        arrays["in_" + name] = np.ascontiguousarray(inputs[name])
        args[name] = nc.dram_tensor("in_" + name, arrays["in_" + name].shape, F32, kind="ExternalInput").ap()
    arrays["in_constants"] = constants()
    args["constants"] = nc.dram_tensor("in_constants", arrays["in_constants"].shape, F32, kind="ExternalInput").ap()
    outs = [nc.dram_tensor(f"out_{i}", shape, F32, kind="ExternalOutput").ap() for i, shape in enumerate(OUTPUTS)]
    build(nc, args, outs)
    r = run_bass_kernel_spmd(nc, [arrays], core_ids=[0])
    return tuple(r.results[0][f"out_{i}"] for i in range(len(OUTPUTS)))
```

```python
from contextlib import ExitStack

import numpy as np

import concourse.bass as bass
from concourse import mybir
from concourse.alu_op_type import AluOpType as ALU

F32 = mybir.dt.float32
BF16 = mybir.dt.bfloat16
I32 = mybir.dt.int32
ACT = mybir.ActivationFunctionType
AX_X = mybir.AxisListType.X

P = 128
D = 1024
KD = D // P
SEQ, NB, NT = 512, 8, 4
NS = NB * NT
N = SEQ + NS
HALF = N // 2
IN_W = 5376
MT = IN_W // P
Q0, K0, V0, UA0, UB0, G0 = 0, 6, 12, 18, 22, 26
CT = 4
CC = CT * P
TAPS = 31
PAD = TAPS - 1
HEADS, HD = 4, 64
WIN = (128, 512, 2048)
PAST = 512
ALPHA = 2 ** 0.25
EPS = 1e-5
SCALE = HD ** -0.5
NEG = -1e30
NGRP, NPER = 4, 8
NE = NGRP * NPER
FE = 512
KF = FE // P
BLK = 96
OVER = (2 * N) // BLK
NBLK = NE + OVER
LEVELS = (N - 1) // BLK
SLOTS = 3
ROUNDS = NE // SLOTS
OOB = 1 << 20
TILES = [(t * P, min(P, N - t * P)) for t in range((N + P - 1) // P)]
NTT = len(TILES)
SKEYS = 3 * P + 3 * NS
PKEYS = SEQ + 2 * P


def constants():
    half = HD // 8
    pos = np.concatenate([np.arange(SEQ), np.tile(PAST + np.arange(NT), NB)]).astype(np.float32)
    inv = (np.float32(500000.0) ** (-np.arange(half, dtype=np.float32) / np.float32(half))).astype(np.float32)
    ang = (pos[None, :] * inv[:, None]).astype(np.float32)
    cos, sin = np.ones((P, N), np.float32), np.zeros((P, N), np.float32)
    rot = np.zeros((P, P), np.float32)
    for h in range(0, P, HD):
        for j in range(half):
            for i in (h + j, h + j + half):
                cos[i], sin[i] = np.cos(ang[j]), np.sin(ang[j])
            rot[h + j + half, h + j] = -1.0
            rot[h + j, h + j + half] = 1.0
    eye = np.eye(P, dtype=np.float32)
    before = np.triu(np.ones((P, P), np.float32), 1)
    rows = np.tile(np.concatenate([np.arange(BLK), np.arange(NBLK), np.arange(NE)]).astype(np.float32), (P, 1))
    p = np.arange(P)
    masks = []
    for r in range(4):
        t, key = 4 * p[:, None] + r, np.arange(SEQ)[None, :]
        masks.append((key <= t) & (key >= t - WIN[0]))
    masks.append(p[None, :] <= p[:, None])
    masks.append((p[None, :] <= p[:, None]) & ((p[:, None] - p[None, :]) % 4 == 0))
    pmask = np.where(np.concatenate(masks, 1), 0.0, NEG).astype(np.float32)
    b, t = (p // 8) % NB, (p // 2) % NT
    col, new = np.arange(P)[None, :], np.arange(NS)[None, :]
    own, nt = new // NT == b[:, None], new % NT
    smask = np.concatenate([col >= t[:, None], col >= 0 * t[:, None], col % 4 == t[:, None],
                            own & (nt <= t[:, None]), own & (nt == t[:, None]), own & (nt == t[:, None])], 1)
    smask = np.where(smask, 0.0, NEG).astype(np.float32)
    token = np.zeros((P, NTT, 2), np.float32)
    for i in range(NTT):
        for k in range(2):
            token[:, i, k] = 1 + k * N + i * P + p
    return np.concatenate([cos, sin, eye, rot, before, rows, token.reshape(P, -1), pmask, smask], 1)


C_COS, C_SIN = 0, N
C_EYE = 2 * N
C_ROWS = C_EYE + 3 * P
NROWS = BLK + NBLK + NE + 2 * NTT
C_PM = C_ROWS + NROWS
C_SM = C_PM + 4 * SEQ + 2 * P
C_END = C_SM + SKEYS


def build(nc, a, o):
    y_prompt, y_sample, kv0p, kv1p, kv2p, conv_p, kv0s, kv1s, kv2s, conv_s = o
    h_dram = nc.dram_tensor("h_rows", [N, D], F32, kind="Internal").ap()
    y_dram = nc.dram_tensor("expert_rows", [2 * N, D], F32, kind="Internal").ap()
    caches = [a["cache_kv_w128"][0], a["cache_kv_w512"][0], a["cache_kv_w2048"][0]]
    const = a["constants"]
    w_in = a["w_in"][0].rearrange("(k p) n -> p k n", p=P)
    wg_d = a["w_expert_gate"][0].rearrange("e (p k) f -> e p (k f)", k=KD)
    wu_d = a["w_expert_up"][0].rearrange("e (p k) f -> e p (k f)", k=KD)
    wd_d = a["w_expert_down"][0].rearrange("e (k p) d -> e p k d", p=P)
    x_p, x_s = a["x_prompt"][0], a["x_sample"].rearrange("b t d -> (b t) d")

    with ExitStack() as ctx:
        def sb(name, cols, dt=F32, parts=P):
            return ctx.enter_context(nc.sbuf_tensor(name, [parts, cols], dt))

        def sem(name):
            return ctx.enter_context(nc.semaphore(name))

        ea, eb = sb("region_a", 12288), sb("region_b", 12288)
        z2, xt_t = sb("z_conv_gates", (MT - V0 - 6) * N), sb("x_columns", KD * N)
        sc, vt_t = sb("scratch", 3256), sb("value_rows", 3072)
        wa_t, at_t = sb("w_attn", 2048), sb("attn_columns", 2 * N)
        ci = sb("const_small", 3 * P + NROWS)
        colb = sb("column_vectors", 62 + TAPS * CT)
        small = sb("small", 80)
        gidx, sidx = sb("gather_rows", NBLK, I32), sb("scatter_rows", NBLK, I32)
        over_i = sb("further_blocks", OVER + 1, I32)
        over_idx = sb("block_rows", 2 * SLOTS, I32)
        ps = ctx.enter_context(nc.psum_tensor("ps", [P, 8, 512], F32))

        eye, rot, before = ci[:, 0:P], ci[:, P:2 * P], ci[:, 2 * P:3 * P]
        iota_r = ci[:, 3 * P:3 * P + BLK]
        iota_b = ci[:, 3 * P + BLK:3 * P + BLK + NBLK]
        iota_e = ci[:, 3 * P + BLK + NBLK:3 * P + BLK + NBLK + NE]
        token = ci[:, 3 * P + BLK + NBLK + NE:].rearrange("p (t k) -> p t k", k=2)
        bdw_c, clg_c, clb_c, bco_c = (colb[:, i:i + 8] for i in (42, 46, 50, 54))
        wdw_c = colb[:, 62:62 + TAPS * CT]

        zqkv = ea[:, 0:18 * N].rearrange("p (m n) -> p m n", n=N)
        pmask = ea[:, 18 * N:18 * N + 4 * SEQ + 2 * P]
        wring = eb[:, 0:6144].rearrange("p (s k n) -> p s k n", s=3, k=KD)
        kout12 = eb[:, 0:2048].rearrange("p (r c) -> p r c", r=4)
        kout0 = eb[:, 2048:2304]
        smask = eb[:, 2304:2304 + SKEYS]
        skv = eb[:, 2784:4320].rearrange("p (g two c) -> p g two c", g=3, two=2)
        qbd = eb[:, 4320:4704].rearrange("p (m b j) -> p m b j", m=6, j=2)
        st_sb, stn_sb = eb[:, 4704:5088], eb[:, 5088:5472]
        sp = eb[:, 5472:5472 + SKEYS]
        kc = eb[:, 6144:9216].rearrange("p (s t c) -> p s t c", s=2, t=6)
        vc = eb[:, 9216:12288].rearrange("p (s t c) -> p s t c", s=2, t=6)
        cos, sin = eb[:, 9216:9216 + N], eb[:, 9216 + N:9216 + 2 * N]
        wo = eb[:, 0:KD * D].rearrange("p (k n) -> p k n", k=KD)

        zr = z2[:, :].rearrange("p (m n) -> p m n", n=N)
        ua, ub = zr[:, 0:CT], zr[:, CT:2 * CT]
        xs = z2[:, 8 * N:8 * N + NTT * D].rearrange("p (t d) -> p t d", d=D)
        ga, gc = zr[:, 8:16], zr[:, 16:24]
        xt = xt_t[:, :].rearrange("p (k n) -> p k n", k=KD)
        wco = xt_t[:, 0:CT * D].rearrange("p (k n) -> p k n", k=CT)
        rows_a, rows_b = vt_t[0:62, 0:P], vt_t[0:TAPS * CT, P:2 * P]
        rtmp = vt_t[:, 2 * P:2 * P + 2 * N].rearrange("p (s n) -> p s n", s=2)
        cst = vt_t[0:4 * PAD, 1408:2432].rearrange("p (j c) -> p j c", j=2)
        vt = vt_t[:, :].rearrange("p (r c) -> p r c", r=4)
        uext = sc[:, 0:CT * (SEQ + PAD)].rearrange("p (c s) -> p c s", c=CT)
        sext = sc[:, CT * (SEQ + PAD):3256].rearrange("p (c b s) -> p c b s", c=CT, b=NB)
        ktr = sc[:, 0:3072].rearrange("p (s m k) -> p s m k", s=2, m=12)
        prob = sc[:, 0:2 * PKEYS].rearrange("p (s k) -> p s k", s=2)
        prt = sc[:, 2 * PKEYS:4 * PKEYS].rearrange("p (s m k) -> p s m k", s=2, m=6)
        wa = wa_t[:, :].rearrange("p (k n) -> p k n", k=2)
        at = at_t[:, :].rearrange("p (k n) -> p k n", k=2)

        acc, cen = ua, ub
        rstd_c = sc[:, 0:N]
        onesm = sb("ones_mean", P)[:, :]
        onesb = sb("ones_count", P, BF16)[:, :]
        beforeb = sb("before_count", P, BF16)[:, :]
        nmx_p, l_p = small[:, 0:16], small[:, 16:32]
        rinv = small[:, 32:36]
        pmx = small[:, 76:78]
        cst_u = ea[:, 18 * N + 4 * SEQ + 2 * P:18 * N + 4 * SEQ + 3 * P].rearrange("p (c n) -> p c n", c=CT)
        urow_p, urow_s = z2[:, 4 * N:4 * N + CC], z2[:, 4 * N + CC:4 * N + 2 * CC]
        atk = xt_t[:, 4096:4352]
        nmx_s, l_s, rinv_s = small[:, 36:37], small[:, 37:38], small[:, 38:39]

        wrv = z2[:, 16 * N + 3 * D:16 * N + 3 * D + KD * 36].rearrange("p (k n) -> p k n", k=KD)
        br = sb("b_router", 36)[:, :]
        hrow = z2[:, 0:2048].rearrange("p (s d) -> p s d", s=2)
        xrow = z2[:, 2048:4096].rearrange("p (s d) -> p s d", s=2)
        g1row, b1row = z2[:, 16 * N:16 * N + D], z2[:, 16 * N + D:16 * N + 2 * D]
        hcol = z2[:, 16 * N + 2 * D:16 * N + 3 * D].rearrange("p (k n) -> p k n", k=KD)
        def ln_cols(first, width=1):
            return [small[:, 40 + 18 * q + first:40 + 18 * q + first + width] for q in range(2)]

        stats, mv, var_e, sd, rs, nmr = ln_cols(0, 12), ln_cols(12, 2), ln_cols(14), ln_cols(15), ln_cols(16), ln_cols(17)
        logits = sb("logits", NTT * 36)
        lg = logits[:, :].rearrange("p (t c) -> p t c", c=36)
        gates = sb("gate_weights", NTT * 2)
        gw = gates[:, :].rearrange("p (k t) -> p k t", k=2)
        mb = sb("choices", NTT * NE, BF16)[:, :].rearrange("p (t e) -> p t e", e=NE)
        at_col = [0]

        def route(*dims):
            n, c = int(np.prod(dims)), at_col[0]
            at_col[0] += n
            names = "abc"[:len(dims)]
            v = vt_t[:, c:c + n]
            return v if len(dims) == 1 else v.rearrange(f"p ({' '.join(names)}) -> p {' '.join(names)}",
                                                        **{names[i]: dims[i] for i in range(1, len(dims))})

        ohr, ohb = route(2 * NTT, BLK), route(2 * NTT, NBLK)
        oh, rank = route(2, NTT, NE), route(NTT, NE)
        emf, rt32, io32 = route(NTT * NE), route(NTT, NE), route(NTT, NE)
        em = emf.rearrange("p (t e) -> p t e", e=NE)
        em4 = emf.rearrange("p (t g e) -> p t g e", g=NGRP, e=NPER)
        rt_a4, rt_b4, rt_c4, rt_g3 = (route(NTT, NGRP) for _ in range(4))
        v12, e12 = route(2, NTT), route(2, NTT)
        m1, i1, rt_d = route(NTT), route(NTT), route(NTT)
        cnt, nov, ovst, tmp32, ovf = route(NE), route(NE), route(NE), route(NE), route(OVER + 1)
        ovend, tabf = route(2, NE), route(2, NBLK)
        rk, ek, ok, qk, q0 = (route(NTT, 2) for _ in range(5))

        wslot = [ea, eb, z2]
        wgv = [w[:, 0:4096].rearrange("p (k f m) -> p k f m", k=KD, f=KF) for w in wslot]
        wuv = [w[:, 4096:8192].rearrange("p (k f m) -> p k f m", k=KD, f=KF) for w in wslot]
        wdv = [w[:, 8192:12288].rearrange("p (k d) -> p k d", k=KF) for w in wslot]
        xg = [xt_t[0:BLK, s * D:(s + 1) * D] for s in range(SLOTS)]
        yo = [vt_t[0:BLK, s * D:(s + 1) * D] for s in range(SLOTS)]
        xgt = [sc[:, s * 768:(s + 1) * 768].rearrange("p (k c) -> p k c", k=KD) for s in range(SLOTS)]
        gact = sc[:, 2304:2688].rearrange("p (f c) -> p f c", f=KF)
        hact = sc[:, 2688:3072].rearrange("p (f c) -> p f c", f=KF)
        idx_t = over_idx

        x_loaded, rows_loaded, ci_loaded, trig_loaded = sem("x_loaded"), sem("rows_loaded"), sem("ci_loaded"), sem("trig_loaded")
        mask_loaded, state_loaded = sem("mask_loaded"), sem("state_loaded")
        win_loaded = [sem(f"win_loaded{s}") for s in range(3)]
        tile_mm, tile_free = sem("tile_mm"), sem("tile_free")
        pads_set = sem("pads_set")
        xt_ps, xt_sb = sem("xt_ps"), sem("xt_sb")
        colb_ps, colb_sb = sem("colb_ps"), sem("colb_sb")
        rot_ps, rot_used, rotated = sem("rot_ps"), sem("rot_used"), sem("rotated")
        state_ps, state_sb = sem("state_ps"), sem("state_sb")
        dve_chain, pool_steps, sp_steps = sem("dve_chain"), sem("pool_steps"), sem("sp_steps")
        sig_u, conv_step, u_set = sem("sig_u"), sem("conv_step"), sem("u_set")
        v_ps, v_sb, k_ps, k_sb, s_ps, s_sb = (sem(x) for x in ("v_ps", "v_sb", "k_ps", "k_sb", "s_ps", "s_sb"))
        u_ps, u_sb = sem("u_ps"), sem("u_sb")
        stored, copied, kout_stored = sem("stored"), sem("copied"), sem("kout_stored")
        kc_loaded = [sem(f"kc_loaded{s}") for s in range(2)]
        vc_loaded = [sem(f"vc_loaded{s}") for s in range(2)]
        kt_ps, kt_dve, kt_act, st_ps, st_done = (sem(x) for x in ("kt_ps", "kt_dve", "kt_act", "st_ps", "st_done"))
        qbd_set, sback_ps, sprob, spn, spt_ps, spt_sb, vs_used, so_ps, so_sb = (
            sem(x) for x in ("qbd_set", "sback_ps", "sprob", "spn", "spt_ps", "spt_sb", "vs_used", "so_ps", "so_sb"))
        smax = sem("smax")
        qk_ps, pmax, pexp, pt_ps, pt_dve, pt_act, pv_ps, otok, at_ps, at_sb = (
            sem(x) for x in ("qk_ps", "pmax", "pexp", "pt_ps", "pt_dve", "pt_act", "pv_ps", "otok", "at_ps", "at_sb"))
        mean_ps, cen_sb, sq_sb, var_ps, veps, csd, cnorm, cact = (
            sem(x) for x in ("mean_ps", "cen_sb", "sq_sb", "var_ps", "veps", "csd", "cnorm", "cact"))
        conv_done = sem("conv_done")
        wco_loaded, wa_loaded, wo_loaded = sem("wco_loaded"), sem("wa_loaded"), sem("wo_loaded")
        br_ps, br_used, merged = sem("br_ps"), sem("br_used"), sem("merged")
        xrow_loaded = [sem(f"xrow_loaded{s}") for s in range(2)]
        rows1_loaded, wr_loaded = sem("rows1_loaded"), sem("wr_loaded")
        y_ps, y_used, hvar, hsd, hscale, hnorm, hdone = (
            sem(x) for x in ("y_ps", "y_used", "hvar", "hsd", "hscale", "hnorm", "hdone"))
        h_stored = [sem(f"h_stored{s}") for s in range(2)]
        ht_ps, ht_sb, lg_ps, lg_sb = sem("ht_ps"), sem("ht_sb"), sem("lg_ps"), sem("lg_sb")
        rmax, rexp, mset, cnt_ps, sel_set, idx_ps, idx_set = (
            sem(x) for x in ("rmax", "rexp", "mset", "cnt_ps", "sel_set", "idx_ps", "idx_set"))
        e_loaded = [[sem(f"{n}_loaded{s}") for s in range(SLOTS)] for n in ("wg", "wu", "wd")]
        gathered = [sem(f"gathered{s}") for s in range(SLOTS)]
        scattered = [sem(f"scattered{s}") for s in range(SLOTS)]
        idx_set_e, xgt_ps, xgt_sb, gu_ps, gact_sb, hact_sb, dn_ps, yo_sb = (
            sem(x) for x in ("idx_copied", "xgt_ps", "xgt_sb", "gu_ps", "gact_sb", "hact_sb", "dn_ps", "yo_sb"))
        ov = {x: sem("ov_" + x) for x in ("load", "idx", "gat", "tps", "tsb", "gu", "ga", "ha", "dn", "yo", "sca")}
        over_done = sem("over_done")
        fin_loaded = [sem(f"fin_loaded{s}") for s in range(2)]
        rows2_loaded = sem("rows2_loaded")
        fmix, fmul, fdone = (sem(x) for x in ("fmix", "fmul", "fdone"))
        fweigh, xg_zero, y_stored = sem("fweigh"), sem("xg_zero"), sem("y_stored")
        qbd_zero, br_loaded = sem("qbd_zero"), sem("br_loaded")

        block = ctx.enter_context(nc.Block())
        fh = [z2[:, t * D:(t + 1) * D] for t in range(NTT)]
        fy1 = [z2[:, (NTT + s) * D:(NTT + 1 + s) * D] for s in range(2)]
        fy2 = [z2[:, (NTT + 2 + s) * D:(NTT + 3 + s) * D] for s in range(2)]
        g2row, b2row = z2[:, (NTT + 4) * D:(NTT + 5) * D], z2[:, (NTT + 5) * D:(NTT + 6) * D]

        @block.sync
        def _(sp_e):
            sp_e.dma_start(xs[:, 0:4, :], x_p.rearrange("(t p) d -> p t d", p=P)).then_inc(x_loaded, 16)
            sp_e.dma_start(xs[0:NS, 4, :], x_s).then_inc(x_loaded, 16)
            for s in range(3):
                sp_e.dma_start(wring[:, s], w_in[:, :, s * 256:(s + 1) * 256]).then_inc(win_loaded[s], 16)
            with sp_e.Fori(1, 7) as i:
                for s in range(3):
                    sp_e.wait_ge(tile_mm, 6 * i + 2 * s - 4)
                    sp_e.dma_start(wring[:, s], w_in[:, :, bass.ds(i * 768 + s * 256, 256)]).then_inc(win_loaded[s], 16)
            sp_e.wait_ge(tile_mm, MT)
            sp_e.dma_start(smask, const[:, C_SM:C_END]).then_inc(mask_loaded, 16)
            sp_e.dma_start(wco, a["w_conv_out"][0].rearrange("(k p) n -> p k n", p=P)).then_inc(wco_loaded, 16)
            sp_e.wait_ge(so_ps, 1)
            sp_e.wait_ge(kout_stored, 16 * 15)
            sp_e.dma_start(wo, a["w_o"][0].rearrange("(k p) n -> p k n", p=P)).then_inc(wo_loaded, 16)
            sp_e.wait_ge(at_sb, 4)
            for n, src in enumerate((wg_d, wu_d)):
                sp_e.dma_start(ea[:, n * 4096:(n + 1) * 4096], src[0]).then_inc(e_loaded[n][0], 16)
            sp_e.dma_start(wdv[0], wd_d[0]).then_inc(e_loaded[2][0], 16)
            for t in range(NTT):
                c0, n = TILES[t]
                if t == 0:
                    sp_e.wait_ge(merged, 8)
                    sp_e.dma_start(g1row, a["ln1_g"][0].partition_broadcast(P)).then_inc(rows1_loaded, 16)
                    sp_e.dma_start(b1row, a["ln1_b"][0].partition_broadcast(P)).then_inc(rows1_loaded, 16)
                    sp_e.dma_start(wrv[:, :, 0:4], a["w_router_group"][0].rearrange("(k p) n -> p k n", p=P)).then_inc(wr_loaded, 16)
                    sp_e.dma_start(wrv[:, :, 4:36], a["w_router_expert"][0].rearrange("(k p) n -> p k n", p=P)).then_inc(wr_loaded, 16)
                if t >= 2:
                    sp_e.wait_ge(y_used, t - 1)
                src = x_p[c0:c0 + n] if t < 4 else x_s
                sp_e.dma_start(xrow[0:n, t % 2, :], src).then_inc(xrow_loaded[t % 2], 16)
            def load_expert(e, s):
                for n, src in enumerate((wg_d, wu_d)):
                    sp_e.dma_start(wslot[s][:, n * 4096:(n + 1) * 4096],
                                   src[bass.ds(e, 1)].rearrange("o p x -> p (o x)")).then_inc(e_loaded[n][s], 16)

            def load_down(e, s):
                sp_e.dma_start(wdv[s], wd_d[bass.ds(e, 1)].rearrange("o p k d -> p (o k) d")).then_inc(e_loaded[2][s], 16)

            sp_e.wait_ge(y_ps, NTT)
            load_expert(1, 1)
            load_down(1, 1)
            sp_e.wait_ge(lg_ps, NTT)
            sp_e.wait_ge(h_stored[0], 48)
            sp_e.wait_ge(h_stored[1], 32)
            load_expert(2, 2)
            load_down(2, 2)

            def reload(i, s):
                e = SLOTS * i + s
                sp_e.wait_ge(gu_ps, KF * (e - SLOTS + 1))
                load_expert(e, s)
                sp_e.wait_ge(dn_ps, e - SLOTS + 1)
                load_down(e, s)

            with sp_e.Fori(1, ROUNDS) as i:
                for s in range(SLOTS):
                    reload(i, s)
            for s in range(NE % SLOTS):
                reload(ROUNDS, s)
            sp_e.wait_ge(dn_ps, NE - NE % SLOTS)
            for t, (c0, n) in enumerate(TILES):
                sp_e.dma_start(fh[t][0:n], h_dram[c0:c0 + n]).then_inc(rows2_loaded, 16)
            sp_e.dma_start(g2row, a["ln2_g"][0].partition_broadcast(P)).then_inc(rows2_loaded, 16)
            sp_e.dma_start(b2row, a["ln2_b"][0].partition_broadcast(P)).then_inc(rows2_loaded, 16)
            sp_e.wait_ge(idx_set, 1)
            sp_e.wait_ge(dn_ps, NE)
            count = sp_e.value_load(over_i[0:1, OVER:OVER + 1], min_val=0, max_val=OVER)
            with sp_e.If(count > 0):
                with sp_e.Fori(0, count) as i:
                    e = sp_e.value_load(over_i[0:1, bass.ds(i, 1)], min_val=0, max_val=NE - 1)
                    for n, src in enumerate((wg_d, wu_d)):
                        sp_e.dma_start(ea[:, n * 4096:(n + 1) * 4096],
                                       src[bass.ds(e, 1)].rearrange("o p x -> p (o x)")).then_inc(ov["load"], 16)
                    sp_e.dma_start(wdv[0], wd_d[bass.ds(e, 1)].rearrange("o p k d -> p (o k) d")).then_inc(ov["load"], 16)
                    sp_e.wait_ge(ov["sca"], 16 * i + 16)
                    sp_e.sem_inc(sp_steps, 1)
            sp_e.wait_ge(over_done, 1)

            def load_results(t):
                c0, n = TILES[t]
                s = t % 2
                if t >= 2:
                    sp_e.wait_ge(fmix, t - 1)
                sp_e.dma_start(fy1[s][0:n], y_dram[c0:c0 + n]).then_inc(fin_loaded[s], 16)
                sp_e.dma_start(fy2[s][0:n], y_dram[N + c0:N + c0 + n]).then_inc(fin_loaded[s], 16)

            load_results(0)
            load_results(1)
            for t, (c0, n) in enumerate(TILES):
                if t + 2 < NTT:
                    load_results(t + 2)
                sp_e.wait_ge(fdone, t + 1)
                dst = y_prompt[0, c0:c0 + n] if t < 4 else y_sample.rearrange("b t d -> (b t) d")
                sp_e.dma_start(dst, fh[t][0:n]).then_inc(y_stored, 16)
            sp_e.wait_ge(y_stored, 16 * NTT)

        @block.tensor
        def _(pe):
            pe.wait_ge(ci_loaded, 16)
            pe.wait_ge(rows_loaded, 16 * 6)
            pe.transpose(ps[:, 3, 0:62], rows_a, eye[0:62, 0:62])
            pe.transpose(ps[:, 3, 64:64 + TAPS * CT], rows_b, eye[0:TAPS * CT, 0:TAPS * CT]).then_inc(colb_ps, 1)
            pe.wait_ge(x_loaded, 32)
            for t, (c0, n) in enumerate(TILES):
                if t >= 2:
                    pe.wait_ge(xt_sb, t - 1)
                for k in range(KD):
                    last = pe.transpose(ps[:, 4 + 2 * (t % 2) + k // 4, (k % 4) * P:(k % 4) * P + n],
                                        xs[0:n, t, k * P:(k + 1) * P], eye[0:n, 0:n])
                last.then_inc(xt_ps, 1)
            pe.wait_ge(xt_sb, NTT)

            def project(lo, hi):
                with pe.Fori(lo, hi) as i:
                    for s in range(3):
                        pe.wait_ge(win_loaded[s], 16 * i + 16)
                        for c in range(2):
                            pe.wait_ge(tile_free, 6 * i + 2 * s + c + 1)
                            for half in range(2):
                                for k in range(KD):
                                    last = pe.matmul(ps[:, 2 * c + half, 0:HALF], wring[:, s, k, c * P:(c + 1) * P],
                                                     xt[:, k, half * HALF:(half + 1) * HALF], start=k == 0, stop=k == KD - 1)
                            last.then_inc(tile_mm, 1)

            project(0, 3)
            for m in range(12):
                pe.wait_ge(tile_free, 2 + m + 1)
                if m >= 2:
                    pe.wait_ge(rot_used, m - 1)
                for half in range(2):
                    last = pe.matmul(ps[:, 4 + 2 * (m % 2) + half, 0:HALF], rot, zqkv[:, m, half * HALF:(half + 1) * HALF],
                                     start=True, stop=True)
                last.then_inc(rot_ps, 1)
            pe.wait_ge(state_loaded, 32)
            pe.wait_ge(rot_used, 12)
            for j in range(2):
                for c in range(CT):
                    last = pe.transpose(ps[:, 4 + j, c * P:c * P + 4 * PAD], cst[:, j, c * P:(c + 1) * P], eye[0:4 * PAD, 0:4 * PAD])
            last.then_inc(state_ps, 1)
            project(3, 7)

            pe.wait_ge(rotated, 12)
            pe.wait_ge(state_sb, 1)
            for m in range(6):
                if m >= 4:
                    pe.wait_ge(v_sb, m - 3)
                for r in range(4):
                    src = zqkv[:, V0 + m, r * P:(r + 1) * P] if m < 2 else zqkv[:, V0 + m, r:SEQ:4]
                    last = pe.transpose(ps[:, 4 + m % 4, r * P:(r + 1) * P], src, eye)
                last.then_inc(v_ps, 1)
            pe.wait_ge(tile_free, 2 + MT)
            for m in range(6):
                if m >= 4:
                    pe.wait_ge(k_sb, m - 3)
                for r in range(4):
                    if m < 2 and r < 3:
                        continue
                    src = zqkv[:, K0 + m, r * P:(r + 1) * P] if m < 2 else zqkv[:, K0 + m, r:SEQ:4]
                    last = pe.transpose(ps[:, m % 4, r * P:(r + 1) * P], src, eye)
                last.then_inc(k_ps, 1)
            pe.wait_ge(v_sb, 6)
            for m in range(12):
                last = pe.transpose(ps[0:NS, 4 + m // 4, (m % 4) * P:(m % 4) * P + P], zqkv[:, K0 + m, SEQ:N], eye)
            last.then_inc(s_ps, 1)
            pe.wait_ge(u_set, 1)
            for c in range(CT):
                pe.transpose(ps[0:PAD, 7, c * P:(c + 1) * P], uext[:, c, SEQ:SEQ + PAD], eye)
            pe.wait_ge(k_sb, 6)
            for c in range(CT):
                last = pe.transpose(ps[0:NS, 0, c * P:(c + 1) * P], cst_u[:, c, :], eye)
            last.then_inc(u_ps, 1)

            pe.wait_ge(u_sb, 1)
            pe.wait_ge(s_sb, 1)
            pe.wait_ge(qbd_set, 1)
            pe.wait_ge(conv_done, 1)

            def cached_scores(b):
                pe.wait_ge(kt_dve, b + 1)
                pe.wait_ge(kt_act, b + 1)
                for hp in range(2):
                    for tile in range(6):
                        g = (0, 1, 1, 1, 1, 2)[tile]
                        q = qbd[:, 2 * g + hp, b * NT:(b + 1) * NT, :].rearrange("p t j -> p (t j)")
                        c0 = g * P + hp * 64 + b * 8
                        if g == 1:
                            t = tile - 1
                            q, c0, w = q[:, 2 * t:2 * t + 2], c0 + 2 * t, 2
                        else:
                            w = 8
                        last = pe.matmul(ps[:, 6, c0:c0 + w], ktr[:, b % 2, tile * 2 + hp, :], q, start=True, stop=True)
                last.then_inc(st_ps, 1)

            for b in range(NB):
                pe.wait_ge(kc_loaded[b % 2], 48 * (b // 2 + 1))
                if b >= 2:
                    pe.wait_ge(kt_dve, b - 1)
                    pe.wait_ge(kt_act, b - 1)
                for tile in range(6):
                    for hp in range(2):
                        m = tile * 2 + hp
                        last = pe.transpose(ps[:, 3 * (b % 2) + m // 4, (m % 4) * P:(m % 4 + 1) * P],
                                            kc[:, b % 2, tile, hp * P:(hp + 1) * P], eye)
                last.then_inc(kt_ps, 1)
                if b >= 1:
                    cached_scores(b - 1)
            cached_scores(NB - 1)
            for m in range(6):
                last = pe.matmul(ps[0:NS, 7, m * 64:(m + 1) * 64], zqkv[:, K0 + m, SEQ:N],
                                 qbd[:, m, :, :].rearrange("p b j -> p (b j)"), start=True, stop=True)
            last.then_inc(st_ps, 1)
            pe.wait_ge(st_done, 2)
            for g in range(3):
                pe.transpose(ps[:, 0, g * P:(g + 1) * P], st_sb[:, g * P:(g + 1) * P], eye)
            for g in range(3):
                last = pe.transpose(ps[:, 0, 3 * P + g * NS:3 * P + (g + 1) * NS], stn_sb[0:NS, g * P:(g + 1) * P], eye[0:NS, 0:NS])
            last.then_inc(sback_ps, 1)
            pe.wait_ge(spn, 1)
            for g in range(3):
                pe.transpose(ps[:, 1, g * P:(g + 1) * P], sp[:, g * P:(g + 1) * P], eye)
            for g in range(3):
                last = pe.transpose(ps[0:NS, 2, g * P:(g + 1) * P], sp[:, 3 * P + g * NS:3 * P + (g + 1) * NS], eye)
            last.then_inc(spt_ps, 1)
            pe.wait_ge(spt_sb, 2)
            for hp in range(2):
                for g in range(3):
                    pe.matmul(ps[:, 4 + hp, 0:64], skv[0:NS, g, 1, hp * P:(hp + 1) * P],
                              stn_sb[0:NS, g * P + hp * 64:g * P + hp * 64 + 64], start=g == 0, stop=False,
                              skip_group_check=True)
            for b in range(NB):
                pe.wait_ge(vc_loaded[b % 2], 48 * (b // 2 + 1))
                for hp in range(2):
                    for tile in range(6):
                        g = (0, 1, 1, 1, 1, 2)[tile]
                        o0, w = (b * 8, 8) if g != 1 else (b * 8 + 2 * (tile - 1), 2)
                        last = pe.matmul(ps[:, 4 + hp, o0:o0 + w], vc[:, b % 2, tile, hp * P:(hp + 1) * P],
                                         st_sb[:, g * P + hp * 64 + o0:g * P + hp * 64 + o0 + w],
                                         start=False, stop=b == NB - 1, skip_group_check=True)
                last.then_inc(vs_used if b < NB - 1 else so_ps, 1)

            pe.wait_ge(so_sb, 1)

            def scores(i):
                r, h = divmod(i, HEADS)
                p0, hp, s = 64 * (h % 2), h // 2, i % 2
                if i >= 2:
                    pe.wait_ge(pmax, i - 1)
                for g in range(3):
                    q = zqkv[p0:p0 + 64, Q0 + 2 * g + hp, r:SEQ:4]
                    if g == 0:
                        pe.matmul(ps[:, 2 * s, :], q, zqkv[p0:p0 + 64, K0 + hp, 0:SEQ], start=True, stop=True)
                    else:
                        last = pe.matmul(ps[:, 2 * s + 1, (g - 1) * P:g * P], q,
                                         zqkv[p0:p0 + 64, K0 + 2 * g + hp, r:SEQ:4], start=True, stop=True)
                last.then_inc(qk_ps, 1)

            def turn(i):
                pe.wait_ge(pexp, i + 1)
                if i >= 1:
                    pe.wait_ge(pt_dve, i)
                    pe.wait_ge(pt_act, i)
                for c in range(6):
                    last = pe.transpose(ps[:, 4 + c // 4, (c % 4) * P:(c % 4 + 1) * P], prob[:, i % 2, c * P:(c + 1) * P], eye)
                last.then_inc(pt_ps, 1)

            def values(i):
                r, h = divmod(i, HEADS)
                pe.wait_ge(pt_dve, i + 1)
                pe.wait_ge(pt_act, i + 1)
                if h == 0 and r >= 2:
                    pe.wait_ge(at_sb, r - 1)
                for c in range(6):
                    kb, col = (c, h * HD) if c < 4 else (r, (c - 3) * 256 + h * HD)
                    last = pe.matmul(ps[:, 6 + r % 2, h * HD:(h + 1) * HD], prt[:, i % 2, c, :], vt[:, kb, col:col + HD],
                                     start=c == 0, stop=c == 5)
                last.then_inc(pv_ps, 1)

            def turn_out(r):
                pe.wait_ge(otok, r + 1)
                for hp in range(2):
                    last = pe.transpose(ps[:, 6 + r % 2, 256 + hp * P:256 + (hp + 1) * P], atk[:, hp * P:(hp + 1) * P], eye)
                last.then_inc(at_ps, 1)

            for i in range(16 + 2):
                if i < 16:
                    scores(i)
                if 1 <= i <= 16:
                    turn(i - 1)
                if i >= 2:
                    values(i - 2)
                    if (i - 2) % 4 == 0 and i - 2 >= 4:
                        turn_out((i - 2) // 4 - 1)
            turn_out(3)

            pe.wait_ge(pmax, 16)
            for half in range(2):
                for c in range(CT):
                    last = pe.matmul(ps[:, half, 0:HALF], onesm, acc[:, c, half * HALF:(half + 1) * HALF],
                                     start=c == 0, stop=c == CT - 1)
            last.then_inc(mean_ps, 1)
            pe.wait_ge(sq_sb, 1)
            for half in range(2):
                for c in range(CT):
                    last = pe.matmul(ps[:, 2 + half, 0:HALF], onesm, acc[:, c, half * HALF:(half + 1) * HALF],
                                     start=c == 0, stop=c == CT - 1)
            last.then_inc(var_ps, 1)
            pe.wait_ge(cact, CT)
            pe.wait_ge(at_sb, 4)
            pe.wait_ge(wco_loaded, 16)
            pe.wait_ge(wa_loaded, 16)
            for m in range(KD):
                s = 4 * (m % 2)
                if m >= 2:
                    pe.wait_ge(br_used, m - 1)
                for half in range(2):
                    cols = slice(half * HALF, (half + 1) * HALF)
                    for k in range(CT):
                        pe.matmul(ps[:, s + half, 0:HALF], wco[:, k, m * P:(m + 1) * P], acc[:, k, cols], start=k == 0, stop=k == CT - 1)
                    for k in range(2):
                        last = pe.matmul(ps[:, s + 2 + half, 0:HALF], wa[:, k, m * P:(m + 1) * P], at[:, k, cols], start=k == 0, stop=k == 1)
                last.then_inc(br_ps, 1)
            pe.wait_ge(merged, 8)
            pe.wait_ge(wo_loaded, 16)
            pe.wait_ge(wr_loaded, 32)

            def router(t):
                c0, n = TILES[t]
                pe.wait_ge(hdone, t + 1)
                if t >= 1:
                    pe.wait_ge(ht_sb, t)
                for k in range(KD):
                    last = pe.transpose(ps[:, 4 + k // 4, (k % 4) * P:(k % 4) * P + n], hrow[0:n, t % 2, k * P:(k + 1) * P], eye[0:n, 0:n])
                last.then_inc(ht_ps, 1)
                pe.wait_ge(ht_sb, t + 1)
                if t >= 2:
                    pe.wait_ge(lg_sb, t - 1)
                for k in range(KD):
                    last = pe.matmul(ps[0:n, 6 + t % 2, 0:36], hcol[:, k, 0:n], wrv[:, k, :], start=k == 0, stop=k == KD - 1)
                last.then_inc(lg_ps, 1)

            for t, (c0, n) in enumerate(TILES):
                if t >= 2:
                    pe.wait_ge(y_used, t - 1)
                for half in range(2):
                    for k in range(KD):
                        last = pe.matmul(ps[0:n, 2 * (t % 2) + half, :], ga[:, k, c0:c0 + n], wo[:, k, half * 512:(half + 1) * 512],
                                         start=k == 0, stop=k == KD - 1)
                last.then_inc(y_ps, 1)
                if t >= 1:
                    router(t - 1)
            router(NTT - 1)
            pe.wait_ge(mset, 1)
            for t, (c0, n) in enumerate(TILES):
                for u in range(t):
                    pe.matmul(ps[0:n, 0, t * NE:(t + 1) * NE], onesb[0:P, 0:n], mb[:, u, :], start=u == 0, stop=False)
                pe.matmul(ps[0:n, 0, t * NE:(t + 1) * NE], beforeb[0:n, 0:n], mb[0:n, t, :], start=t == 0, stop=True)
            for t, (c0, n) in enumerate(TILES):
                last = pe.matmul(ps[:, 1, 0:NE], onesb[0:n, :], mb[0:n, t, :], start=t == 0, stop=t == NTT - 1)
            last.then_inc(cnt_ps, 1)
            pe.wait_ge(sel_set, 1)
            for i in range(2 * NTT):
                n = TILES[i // 2][1]
                last = pe.matmul(ps[0:BLK, 2, 0:NBLK], ohr[0:n, i, :], ohb[0:n, i, :], start=i == 0, stop=i == 2 * NTT - 1)
            last.then_inc(idx_ps, 1)

            def turn_rows(src):
                for k in range(KD):
                    last = pe.transpose(ps[:, k // 4, (k % 4) * P:(k % 4) * P + BLK], src[:, k:D:KD], eye[0:BLK, 0:BLK])
                return last

            pe.wait_ge(idx_set, 1)
            pe.wait_ge(gathered[0], 16)
            turn_rows(xg[0]).then_inc(xgt_ps, 1)

            def expert(i, s):
                e, nxt = SLOTS * i + s, (s + 1) % SLOTS
                pe.wait_ge(e_loaded[0][s], 16 * i + 16)
                pe.wait_ge(e_loaded[1][s], 16 * i + 16)
                pe.wait_ge(xgt_sb, e + 1)
                for f in range(KF):
                    pe.wait_ge(hact_sb, e * KF + f + 1)
                    for w, bank in ((wgv[s], 2 + f % 2), (wuv[s], 4 + f % 2)):
                        for k in range(KD):
                            last = pe.matmul(ps[:, bank, 0:BLK], w[:, k, f, :], xgt[s][:, k, :], start=k == 0, stop=k == KD - 1)
                    last.then_inc(gu_ps, 1)
                if not (isinstance(i, int) and e == NE - 1):
                    pe.wait_ge(gathered[nxt], 16 * i + 16 + 16 * (nxt == 0))
                    turn_rows(xg[nxt]).then_inc(xgt_ps, 1)
                pe.wait_ge(e_loaded[2][s], 16 * i + 16)
                pe.wait_ge(hact_sb, e * KF + KF + 2)
                pe.wait_ge(yo_sb, e + 1)
                for half in range(2):
                    for k in range(KF):
                        last = pe.matmul(ps[0:BLK, 6 + half, :], hact[:, k, :], wdv[s][:, k, half * 512:(half + 1) * 512],
                                         start=k == 0, stop=k == KF - 1)
                last.then_inc(dn_ps, 1)

            with pe.Fori(0, ROUNDS) as i:
                for s in range(SLOTS):
                    expert(i, s)
            for s in range(NE % SLOTS):
                expert(ROUNDS, s)
            count = pe.value_load(over_i[0:1, OVER:OVER + 1], min_val=0, max_val=OVER)
            with pe.If(count > 0):
                pe.wait_ge(yo_sb, NE + 1)
                pe.wait_ge(xgt_sb, NE)
                with pe.Fori(0, count) as i:
                    pe.wait_ge(ov["gat"], 16 * i + 16)
                    pe.wait_ge(ov["load"], 48 * i + 48)
                    turn_rows(xg[0]).then_inc(ov["tps"], 1)
                    pe.wait_ge(ov["tsb"], i + 1)
                    for f in range(KF):
                        for w, bank in ((wgv[0], 2), (wuv[0], 4)):
                            for k in range(KD):
                                last = pe.matmul(ps[:, bank, 0:BLK], w[:, k, f, :], xgt[0][:, k, :], start=k == 0, stop=k == KD - 1)
                        last.then_inc(ov["gu"], 1)
                        pe.wait_ge(ov["ha"], KF * i + f + 1)
                    for half in range(2):
                        for k in range(KF):
                            last = pe.matmul(ps[0:BLK, 6 + half, :], hact[:, k, :], wdv[0][:, k, half * 512:(half + 1) * 512],
                                             start=k == 0, stop=k == KF - 1)
                    last.then_inc(ov["dn"], 1)

        @block.scalar
        def _(ac):
            ac.dma_start(ci[:, :], const[:, C_EYE:C_PM]).then_inc(ci_loaded, 16)
            ac.dma_start(vt_t[0:42, 0:P], a["b_in"][0].rearrange("(m c) -> m c", c=P)).then_inc(rows_loaded, 16)
            for name, r0, r1 in (("b_dw", 42, 46), ("conv_ln_g", 46, 50), ("conv_ln_b", 50, 54), ("b_conv_out", 54, 62)):
                ac.dma_start(vt_t[r0:r1, 0:P], a[name][0].rearrange("(m c) -> m c", c=P)).then_inc(rows_loaded, 16)
            ac.dma_start(rows_b, a["w_dw"][0].rearrange("t (m c) -> (t m) c", c=P)).then_inc(rows_loaded, 16)
            ac.dma_start(eb[:, 9216:9216 + 2 * N], const[:, C_COS:C_COS + 2 * N]).then_inc(trig_loaded, 16)
            for j in range(2):
                ac.dma_start(cst[:, j, :], a["state_conv"][0, 4 * j:4 * j + 4].rearrange("b s c -> (b s) c")).then_inc(state_loaded, 16)
            ac.dma_start(pmask, const[:, C_PM:C_SM]).then_inc(mask_loaded, 16)
            ac.dma_start(wa, a["w_attn_out"][0].rearrange("(k p) n -> p k n", p=P)).then_inc(wa_loaded, 16)
            ac.dma_start(br[:, 0:4], a["b_router_group"][0].partition_broadcast(P)).then_inc(br_loaded, 16)
            ac.dma_start(br[:, 4:36], a["b_router_expert"][0].partition_broadcast(P)).then_inc(br_loaded, 16)
            ac.wait_ge(colb_sb, 2)
            ac.sem_inc(tile_free, 2)

            def evacuate(lo, hi, dst, first, func):
                with ac.Fori(lo, hi) as i:
                    for j in range(6):
                        c = j % 2
                        ac.wait_ge(tile_mm, 6 * i + j + 1)
                        ac.activation(dst[:, bass.ds((6 * i + j - first) * N, N)].rearrange("p (h n) -> p h n", h=2),
                                      ps[:, 2 * c:2 * c + 2, 0:HALF], func, bias=colb[:, bass.ds(6 * i + j, 1)]).then_inc(tile_free, 1)

            evacuate(0, 3, ea, 0, ACT.Identity)
            evacuate(3, 5, z2, 18, ACT.Identity)
            ac.wait_ge(tile_free, 2 + 30)
            ac.activation(z2[:, 4 * N:12 * N], z2[:, 4 * N:12 * N], ACT.Sigmoid).then_inc(sig_u, 1)
            evacuate(5, 7, z2, 18, ACT.Sigmoid)

            for m in range(6):
                ac.wait_ge(k_ps, m + 1)
                if m < 2:
                    ac.copy(kout0[:, m * P:(m + 1) * P], ps[:, m % 4, 3 * P:4 * P]).then_inc(k_sb, 1)
                else:
                    ac.copy(kout12[:, :, (m - 2) * P:(m - 1) * P],
                            ps[:, m % 4, :].rearrange("p (r c) -> p r c", r=4)).then_inc(k_sb, 1)
            ac.wait_ge(s_ps, 1)
            for two in range(2):
                for g in range(3):
                    m = 6 * two + 2 * g
                    last = ac.copy(skv[0:NS, g, two, :], ps[0:NS, 4 + m // 4, (m % 4) * P:(m % 4) * P + 256])
            last.then_inc(s_sb, 1)
            ac.wait_ge(u_ps, 1)
            ac.copy(urow_p[0:PAD, :], ps[0:PAD, 7, :])
            ac.copy(urow_s[0:NS, :], ps[0:NS, 0, :]).then_inc(u_sb, 1)
            for b in range(NB):
                ac.wait_ge(kt_ps, b + 1)
                if b >= 2:
                    ac.wait_ge(st_ps, b - 1)
                ac.copy(ktr[:, b % 2, 8:12, :], ps[:, 3 * (b % 2) + 2, :].rearrange("p (m k) -> p m k", m=4)).then_inc(kt_act, 1)
            ac.wait_ge(smax, 1)
            ac.activation(sp, sp, ACT.Exp, bias=nmx_s, scale=SCALE, accum_out=l_s).then_inc(sprob, 1)
            for i in range(16 + 1):
                if i < 16:
                    ac.wait_ge(pmax, i + 1)
                    ac.activation(prob[:, i % 2, :], prob[:, i % 2, :], ACT.Exp, bias=nmx_p[:, i:i + 1], scale=SCALE,
                                  accum_out=l_p[:, i:i + 1]).then_inc(pexp, 1)
                if i >= 1:
                    j = i - 1
                    ac.wait_ge(pt_ps, j + 1)
                    if j >= 2:
                        ac.wait_ge(pv_ps, j - 1)
                    ac.copy(prt[:, j % 2, 4:6, :], ps[:, 5, 0:256].rearrange("p (m k) -> p m k", m=2)).then_inc(pt_act, 1)
            ac.wait_ge(cen_sb, 2)
            ac.activation(acc, cen, ACT.Square).then_inc(sq_sb, 1)
            ac.wait_ge(veps, 1)
            ac.activation(rstd_c, rstd_c, ACT.Sqrt).then_inc(csd, 1)
            ac.wait_ge(cnorm, 1)
            for c in range(CT):
                ac.activation(acc[:, c, :], cen[:, c, :], ACT.Silu, bias=clb_c[:, c:c + 1], scale=clg_c[:, c:c + 1]).then_inc(cact, 1)
            def columns_out(t):
                c1, n1 = TILES[t]
                ac.wait_ge(ht_ps, t + 1)
                if t >= 1:
                    ac.wait_ge(lg_ps, t)
                ac.copy(hcol[:, :, 0:n1], ps[:, 4:6, :].rearrange("p b (k c) -> p (b k) c", k=4)[:, :, 0:n1]).then_inc(ht_sb, 1)

            for t, (c0, n) in enumerate(TILES):
                s = t % 2
                ac.wait_ge(hvar, t + 1)
                ac.activation(sd[s][0:n], var_e[s][0:n], ACT.Sqrt).then_inc(hsd, 1)
                ac.wait_ge(hscale, t + 1)
                ac.activation(hrow[0:n, s, :], hrow[0:n, s, :], ACT.Identity, bias=nmr[s][0:n], scale=rs[s][0:n]).then_inc(hnorm, 1)
                columns_out(t)
            ac.wait_ge(rmax, 1)
            ac.activation(rt_g3, rt_g3, ACT.Exp).then_inc(rexp, 1)
            ac.wait_ge(rmax, 2)
            ac.activation(rt_d, rt_d, ACT.Exp).then_inc(rexp, 1)
            ac.sem_inc(yo_sb, 1)

            def expert(i, s):
                e = SLOTS * i + s
                for f in range(KF):
                    ac.wait_ge(gu_ps, e * KF + f + 1)
                    ac.wait_ge(hact_sb, e * KF + f + 1)
                    ac.activation(gact[:, f, :], ps[:, 2 + f % 2, 0:BLK], ACT.Silu).then_inc(gact_sb, 1)
                ac.wait_ge(dn_ps, e + 1)
                if not isinstance(i, int) or i > 0:
                    ac.wait_ge(scattered[s], 16 * i)
                ac.copy(yo[s].rearrange("p (h n) -> p h n", h=2), ps[0:BLK, 6:8, :]).then_inc(yo_sb, 1)

            for s in range(SLOTS):
                expert(0, s)
            with ac.Fori(1, ROUNDS) as i:
                for s in range(SLOTS):
                    expert(i, s)
            for s in range(NE % SLOTS):
                expert(ROUNDS, s)
            ac.wait_ge(idx_set, 1)
            count = ac.value_load(over_i[0:1, OVER:OVER + 1], min_val=0, max_val=OVER)
            with ac.If(count > 0):
                with ac.Fori(0, count) as i:
                    for f in range(KF):
                        ac.wait_ge(ov["gu"], KF * i + f + 1)
                        ac.activation(gact[:, f, :], ps[:, 2, 0:BLK], ACT.Silu).then_inc(ov["ga"], 1)
                    ac.wait_ge(ov["dn"], i + 1)
                    ac.copy(yo[0].rearrange("p (h n) -> p h n", h=2), ps[0:BLK, 6:8, :]).then_inc(ov["yo"], 1)
            def weigh(t):
                n = TILES[t][1]
                ac.wait_ge(fin_loaded[t % 2], 32 * (t // 2 + 1))
                ac.activation(fy1[t % 2][0:n], fy1[t % 2][0:n], ACT.Identity, scale=gw[0:n, 0, t:t + 1]).then_inc(fweigh, 1)

            weigh(0)
            for t, (c0, n) in enumerate(TILES):
                s = t % 2
                if t + 1 < NTT:
                    weigh(t + 1)
                if t == 0:
                    ac.wait_ge(rows2_loaded, 16 * 7)
                ac.wait_ge(hvar, NTT + t + 1)
                ac.activation(sd[s][0:n], var_e[s][0:n], ACT.Sqrt).then_inc(hsd, 1)
                ac.wait_ge(hscale, NTT + t + 1)
                ac.activation(fh[t][0:n], fh[t][0:n], ACT.Identity, bias=nmr[s][0:n], scale=rs[s][0:n]).then_inc(hnorm, 1)

        @block.vector
        def _(ve):
            chain = [0]

            def link(ins):
                chain[0] += 1
                ins.then_inc(dve_chain, 1)
                ve.wait_ge(dve_chain, chain[0])

            ve.wait_ge(colb_ps, 1)
            ve.tensor_copy(colb[:, 0:62], ps[:, 3, 0:62]).then_inc(colb_sb, 1)
            ve.tensor_copy(wdw_c, ps[:, 3, 64:64 + TAPS * CT]).then_inc(colb_sb, 1)
            for t, (c0, n) in enumerate(TILES):
                ve.wait_ge(xt_ps, t + 1)
                src = ps[:, 4 + 2 * (t % 2):6 + 2 * (t % 2), :].rearrange("p b (k c) -> p (b k) c", k=4)
                ve.tensor_copy(xt[:, :, c0:c0 + n], src[:, :, 0:n]).then_inc(xt_sb, 1)
            ve.wait_ge(trig_loaded, 16)
            for m in range(12):
                ve.wait_ge(rot_ps, m + 1)
                ve.tensor_tensor(rtmp[:, m % 2, :].rearrange("p (h n) -> p h n", h=2), ps[:, 4 + 2 * (m % 2):6 + 2 * (m % 2), 0:HALF],
                                 sin.rearrange("p (h n) -> p h n", h=2), ALU.mult).then_inc(rot_used, 1)
                link(ve.tensor_tensor(zqkv[:, m, :], zqkv[:, m, :], cos, ALU.mult))
                ve.wait_ge(rot_used, m + 1)
                ve.tensor_tensor(zqkv[:, m, :], zqkv[:, m, :], rtmp[:, m % 2, :], ALU.add).then_inc(rotated, 1)
            ve.wait_ge(pads_set, 1)
            ve.wait_ge(state_ps, 1)
            for j in range(2):
                for c in range(CT):
                    last = ve.tensor_copy(sext[:, c, 4 * j:4 * j + 4, 0:PAD],
                                          ps[:, 4 + j, c * P:c * P + 4 * PAD].rearrange("p (b s) -> p b s", b=4))
            last.then_inc(state_sb, 1)
            ve.wait_ge(sig_u, 1)
            ve.tensor_tensor(uext[:, :, PAD:PAD + SEQ], ua[:, :, 0:SEQ], ub[:, :, 0:SEQ], ALU.mult)
            for c in range(CT):
                ve.tensor_tensor(sext[:, c, :, PAD:PAD + NT], ua[:, c, SEQ:N].rearrange("p (b t) -> p b t", t=NT),
                                 ub[:, c, SEQ:N].rearrange("p (b t) -> p b t", t=NT), ALU.mult)
            link(ve.tensor_tensor(cst_u, ua[:, :, SEQ:N], ub[:, :, SEQ:N], ALU.mult))
            ve.nop().then_inc(u_set, 1)

            def conv_parts():
                for c in range(CT):
                    yield c, acc[:, c, 0:SEQ], lambda k, c=c: uext[:, c, bass.ds(k, SEQ)] if not isinstance(k, int) else uext[:, c, k:k + SEQ]
                for c in range(CT):
                    yield (c, acc[:, c, SEQ:N].rearrange("p (b t) -> p b t", t=NT),
                           lambda k, c=c: sext[:, c, :, bass.ds(k, NT)] if not isinstance(k, int) else sext[:, c, :, k:k + NT])

            for c, dst, win in conv_parts():
                ve.tensor_scalar(dst, win(0), wdw_c[:, c:c + 1], bdw_c[:, c:c + 1], ALU.mult, ALU.add).then_inc(conv_step, 1)
            with ve.Fori(1, TAPS) as k:
                for j, (c, dst, win) in enumerate(conv_parts()):
                    ve.wait_ge(conv_step, 8 * k + j - 7)
                    ve.scalar_tensor_tensor(dst, win(k), wdw_c[:, bass.ds(k * CT + c, 1)], dst, ALU.mult, ALU.add).then_inc(conv_step, 1)
            ve.wait_ge(conv_step, 8 * TAPS)
            ve.nop().then_inc(conv_done, 1)
            for m in range(6):
                ve.wait_ge(v_ps, m + 1)
                ve.tensor_copy(vt[:, :, m * P:(m + 1) * P], ps[:, 4 + m % 4, :].rearrange("p (r c) -> p r c", r=4)).then_inc(v_sb, 1)
            ve.wait_ge(qbd_zero, 1)
            for hh in range(2):
                rows = slice(64 * hh, 64 * hh + 64)
                last = ve.tensor_copy(qbd[rows, :, :, hh], zqkv[rows, Q0:Q0 + 6, SEQ:N])
            last.then_inc(qbd_set, 1)
            ve.wait_ge(u_ps, 1)
            for b in range(NB):
                ve.wait_ge(kt_ps, b + 1)
                if b >= 2:
                    ve.wait_ge(st_ps, b - 1)
                ve.tensor_copy(ktr[:, b % 2, 0:8, :], ps[:, 3 * (b % 2):3 * (b % 2) + 2, :].rearrange("p b (m k) -> p (b m) k", m=4)).then_inc(kt_dve, 1)
            ve.wait_ge(st_ps, NB + 1)
            ve.tensor_copy(st_sb, ps[:, 6, 0:3 * P]).then_inc(st_done, 1)
            ve.tensor_copy(stn_sb[0:NS, :], ps[0:NS, 7, 0:3 * P]).then_inc(st_done, 1)
            ve.wait_ge(sback_ps, 1)
            ve.wait_ge(mask_loaded, 32)
            link(ve.tensor_tensor_reduce(sp, ps[:, 0, 0:SKEYS], smask, 1.0, -3e38, ALU.add, ALU.max, nmx_s))
            ve.tensor_scalar(nmx_s, nmx_s, -SCALE, None, ALU.mult).then_inc(smax, 1)
            ve.wait_ge(sprob, 1)
            link(ve.reciprocal(rinv_s, l_s))
            ve.tensor_scalar(sp, sp, rinv_s, None, ALU.mult).then_inc(spn, 1)
            ve.wait_ge(spt_ps, 1)
            ve.tensor_copy(st_sb, ps[:, 1, 0:3 * P]).then_inc(spt_sb, 1)
            ve.tensor_copy(stn_sb[0:NS, :], ps[0:NS, 2, 0:3 * P]).then_inc(spt_sb, 1)
            ve.wait_ge(so_ps, 1)
            for hh in range(2):
                rows = slice(64 * hh, 64 * hh + 64)
                last = ve.tensor_copy(at[rows, :, SEQ:N], ps[rows, 4:6, 0:64].rearrange("p h (b j) -> p h b j", j=2)[:, :, :, hh])
            last.then_inc(so_sb, 1)

            def mask_max(i):
                r, s = i // 4, i % 2
                ve.wait_ge(qk_ps, i + 1)
                if i >= 2:
                    ve.wait_ge(pt_ps, i - 1)
                sv = ps[:, 2 * s:2 * s + 2, :].rearrange("p b k -> p (b k)")
                link(ve.tensor_tensor_reduce(prob[:, s, 0:SEQ], sv[:, 0:SEQ], pmask[:, r * SEQ:(r + 1) * SEQ], 1.0, -3e38,
                                             ALU.add, ALU.max, pmx[:, 0:1]))
                link(ve.tensor_tensor_reduce(prob[:, s, SEQ:PKEYS], sv[:, SEQ:PKEYS], pmask[:, 4 * SEQ:4 * SEQ + 2 * P], 1.0, pmx[:, 0:1],
                                             ALU.add, ALU.max, pmx[:, 1:2]))
                ve.tensor_scalar(nmx_p[:, i:i + 1], pmx[:, 1:2], -SCALE, None, ALU.mult).then_inc(pmax, 1)

            for i in range(16 + 1):
                if i < 16:
                    mask_max(i)
                if i >= 1:
                    j = i - 1
                    r, h = divmod(j, 4)
                    ve.wait_ge(pt_ps, j + 1)
                    if j >= 2:
                        ve.wait_ge(pv_ps, j - 1)
                    ve.tensor_copy(prt[:, j % 2, 0:4, :], ps[:, 4, :].rearrange("p (m k) -> p m k", m=4)).then_inc(pt_dve, 1)
                if i in (6, 10, 14, 16):
                    q = {6: 0, 10: 1, 14: 2, 16: 3}[i]
                    if q < 3:
                        ve.wait_ge(pv_ps, 4 * q + 4)
                        link(ve.reciprocal(rinv, l_p[:, 4 * q:4 * q + 4]))
                        ve.tensor_tensor(atk[:, :].rearrange("p (h e) -> p h e", h=4),
                                         ps[:, 6 + q % 2, 0:256].rearrange("p (h e) -> p h e", h=4),
                                         rinv.unsqueeze(2).to_broadcast([P, 4, HD]), ALU.mult).then_inc(otok, 1)
                if i in (8, 12):
                    q = i // 4 - 2
                    ve.wait_ge(at_ps, q + 1)
                    ve.tensor_copy(at[:, :, q:SEQ:4], ps[:, 6 + q % 2, 256:512].rearrange("p (m k) -> p m k", m=2)).then_inc(at_sb, 1)
            ve.wait_ge(at_ps, 3)
            ve.tensor_copy(at[:, :, 2:SEQ:4], ps[:, 6, 256:512].rearrange("p (m k) -> p m k", m=2)).then_inc(at_sb, 1)
            ve.wait_ge(pv_ps, 16)
            link(ve.reciprocal(rinv, l_p[:, 12:16]))
            ve.tensor_tensor(atk[:, :].rearrange("p (h e) -> p h e", h=4),
                             ps[:, 7, 0:256].rearrange("p (h e) -> p h e", h=4),
                             rinv.unsqueeze(2).to_broadcast([P, 4, HD]), ALU.mult).then_inc(otok, 1)
            ve.wait_ge(at_ps, 4)
            ve.tensor_copy(at[:, :, 3:SEQ:4], ps[:, 7, 256:512].rearrange("p (m k) -> p m k", m=2)).then_inc(at_sb, 1)

            ve.wait_ge(mean_ps, 1)
            ve.wait_ge(stored, 16 * 8)
            for half in range(2):
                cols = slice(half * HALF, (half + 1) * HALF)
                ve.tensor_tensor(cen[:, :, cols], acc[:, :, cols], ps[:, half, 0:HALF].unsqueeze(1).broadcast_to([P, CT, HALF]),
                                 ALU.subtract).then_inc(cen_sb, 1)
            ve.wait_ge(var_ps, 1)
            ve.tensor_scalar(rstd_c.rearrange("p (h n) -> p h n", h=2), ps[:, 2:4, 0:HALF], EPS, None, ALU.add).then_inc(veps, 1)
            ve.wait_ge(csd, 1)
            link(ve.reciprocal(rstd_c, rstd_c))
            ve.wait_ge(cen_sb, 2)
            ve.tensor_tensor(cen, cen, rstd_c.unsqueeze(1).broadcast_to([P, CT, N]), ALU.mult).then_inc(cnorm, 1)
            ve.wait_ge(tile_free, 2 + MT)
            for m in range(KD):
                s = 4 * (m % 2)
                ve.wait_ge(br_ps, m + 1)
                v2 = lambda t: t.rearrange("p (h n) -> p h n", h=2)
                ve.scalar_tensor_tensor(v2(gc[:, m, :]), ps[:, s:s + 2, 0:HALF], bco_c[:, m:m + 1], v2(gc[:, m, :]), ALU.add, ALU.mult)
                ve.tensor_tensor(v2(ga[:, m, :]), ps[:, s + 2:s + 4, 0:HALF], v2(ga[:, m, :]), ALU.mult).then_inc(br_used, 1)
            def statistics(rows, s, n, done):
                for half in range(2):
                    st = ve.bn_stats(stats[s][0:n, 6 * half:6 * half + 6], rows[:, half * 512:(half + 1) * 512])
                link(st)
                link(ve.bn_aggr(mv[s][0:n], stats[s][0:n, :]))
                ve.tensor_scalar(var_e[s][0:n], mv[s][0:n, 1:2], EPS, None, ALU.add).then_inc(done, 1)

            def scaling(s, n, done):
                link(ve.reciprocal(rs[s][0:n], sd[s][0:n]))
                ve.scalar_tensor_tensor(nmr[s][0:n], mv[s][0:n, 0:1], -1.0, rs[s][0:n], ALU.mult, ALU.mult).then_inc(done, 1)

            ve.wait_ge(rows1_loaded, 32)
            ve.wait_ge(br_loaded, 32)
            for t, (c0, n) in enumerate(TILES):
                s = t % 2
                ve.wait_ge(y_ps, t + 1)
                ve.wait_ge(xrow_loaded[s], 16 * (t // 2 + 1))
                if t >= 2:
                    ve.wait_ge(h_stored[s], 16 * (t // 2))
                    ve.wait_ge(ht_ps, t - 1)
                hs = hrow[0:n, s, :]
                ve.scalar_tensor_tensor(hs.rearrange("p (h n) -> p h n", h=2), xrow[0:n, s, :].rearrange("p (h n) -> p h n", h=2), ALPHA,
                                        ps[0:n, 2 * s:2 * s + 2, :], ALU.mult, ALU.add).then_inc(y_used, 1)
                ve.wait_ge(y_used, t + 1)
                statistics(hrow[0:n, s, :], s, n, hvar)
                ve.wait_ge(hsd, t + 1)
                scaling(s, n, hscale)
                ve.wait_ge(hnorm, t + 1)
                link(ve.tensor_tensor(hs, hs, g1row[0:n], ALU.mult))
                ve.tensor_tensor(hs, hs, b1row[0:n], ALU.add).then_inc(hdone, 1)
                if t >= 1:
                    c1, n1 = TILES[t - 1]
                    ve.wait_ge(lg_ps, t)
                    ve.tensor_tensor(lg[0:n1, t - 1, :], ps[0:n1, 6 + (t - 1) % 2, 0:36], br[0:n1], ALU.add).then_inc(lg_sb, 1)
            ve.wait_ge(lg_ps, NTT)
            ve.tensor_tensor(lg[0:NS, 4, :], ps[0:NS, 6, 0:36], br[0:NS], ALU.add).then_inc(lg_sb, 1)
            ve.wait_ge(lg_sb, NTT)

            def bc(x, shape):
                return x.to_broadcast(shape)

            S4, S32 = [P, NTT, NGRP], [P, NTT, NE]
            L4, L32 = lg[:, :, 0:4], lg[:, :, 4:36]
            ve.wait_ge(stored, 16 * 8)
            link(ve.memset(rank, 0.0))
            link(ve.tensor_reduce(m1, L4, AX_X, ALU.max))
            link(ve.tensor_tensor(rt_a4, L4, bc(m1.unsqueeze(2), S4), ALU.is_equal))
            link(ve.tensor_scalar(rt_b4, iota_e[:, 0:4].unsqueeze(1).broadcast_to(S4), -64.0, None, ALU.add))
            link(ve.tensor_tensor(rt_c4, rt_b4, rt_a4, ALU.mult))
            link(ve.tensor_reduce(i1, rt_c4, AX_X, ALU.min))
            link(ve.tensor_tensor(rt_a4, rt_b4, bc(i1.unsqueeze(2), S4), ALU.is_equal))
            ve.tensor_tensor(rt_g3, L4, bc(m1.unsqueeze(2), S4), ALU.subtract).then_inc(rmax, 1)
            link(ve.tensor_scalar(rt_b4, rt_a4, -1.0, 1e30, ALU.add, ALU.mult))
            link(ve.tensor_tensor(em4, L32.rearrange("p t (g e) -> p t g e", g=NGRP),
                                  bc(rt_b4.unsqueeze(3), [P, NTT, NGRP, NPER]), ALU.add))
            link(ve.tensor_scalar(io32, iota_e.unsqueeze(1).broadcast_to(S32), -64.0, None, ALU.add))
            for k in range(2):
                link(ve.tensor_reduce(v12[:, k, :], em, AX_X, ALU.max))
                link(ve.tensor_tensor(rt32, em, bc(v12[:, k, :].unsqueeze(2), S32), ALU.is_equal))
                link(ve.tensor_tensor(rt32, rt32, io32, ALU.mult))
                link(ve.tensor_reduce(e12[:, k, :], rt32, AX_X, ALU.min))
                link(ve.tensor_tensor(oh[:, k], io32, bc(e12[:, k, :].unsqueeze(2), S32), ALU.is_equal))
                if k == 0:
                    link(ve.scalar_tensor_tensor(em, oh[:, 0], -3e38, em, ALU.mult, ALU.add))
            link(ve.tensor_tensor(mb, oh[:, 0], oh[:, 1], ALU.add))
            ve.nop().then_inc(mset, 1)
            ve.tensor_tensor(rt_d, v12[:, 1, :], v12[:, 0, :], ALU.subtract).then_inc(rmax, 1)
            ve.wait_ge(rexp, 1)
            link(ve.tensor_reduce(i1, rt_g3, AX_X, ALU.add))
            ve.wait_ge(rexp, 2)
            link(ve.scalar_tensor_tensor(m1, rt_d, 1.0, i1, ALU.add, ALU.mult))
            link(ve.reciprocal(gw[:, 0, :], m1))
            link(ve.tensor_tensor(gw[:, 1, :], gw[:, 0, :], rt_d, ALU.mult))
            ve.wait_ge(cnt_ps, 1)
            link(ve.tensor_copy(cnt, ps[:, 1, 0:NE]))
            link(ve.tensor_scalar(nov, cnt, float(BLK), None, ALU.is_gt))
            for j in range(2, LEVELS + 1):
                link(ve.scalar_tensor_tensor(nov, cnt, float(j * BLK), nov, ALU.is_gt, ALU.add))
            link(ve.tensor_copy(ovend[:, 0, :], nov))
            cur = 0
            for sh in (1, 2, 4, 8, 16):
                link(ve.tensor_copy(ovend[:, 1 - cur, 0:sh], ovend[:, cur, 0:sh]))
                link(ve.tensor_tensor(ovend[:, 1 - cur, sh:NE], ovend[:, cur, sh:NE], ovend[:, cur, 0:NE - sh], ALU.add))
                cur = 1 - cur
            oe = ovend[:, cur, :]
            link(ve.tensor_tensor(ovst, oe, nov, ALU.subtract))
            for b in range(OVER):
                link(ve.tensor_scalar(tmp32, oe, float(b), None, ALU.is_le))
                link(ve.tensor_reduce(ovf[:, b:b + 1], tmp32, AX_X, ALU.add))
            link(ve.tensor_scalar(ovf[:, 0:OVER], ovf[:, 0:OVER], float(NE - 1), None, ALU.min))
            link(ve.tensor_copy(ovf[:, OVER:OVER + 1], oe[:, NE - 1:NE]))
            link(ve.tensor_copy(over_i[:, :], ovf))
            link(ve.tensor_copy(rank[:, 0:4, :], ps[:, 0, 0:4 * NE].rearrange("p (t e) -> p t e", e=NE)))
            link(ve.tensor_copy(rank[0:NS, 4, :], ps[0:NS, 0, 4 * NE:5 * NE]))
            for k in range(2):
                link(ve.tensor_tensor(rt32, oh[:, k], rank, ALU.mult))
                link(ve.tensor_reduce(rk[:, :, k], rt32, AX_X, ALU.add))
                link(ve.tensor_tensor(rt32, oh[:, k], iota_e.unsqueeze(1).broadcast_to(S32), ALU.mult))
                link(ve.tensor_reduce(ek[:, :, k], rt32, AX_X, ALU.add))
                link(ve.tensor_tensor(rt32, oh[:, k], ovst.unsqueeze(1).broadcast_to(S32), ALU.mult))
                link(ve.tensor_reduce(ok[:, :, k], rt32, AX_X, ALU.add))
            link(ve.tensor_scalar(qk, rk, float(BLK), None, ALU.is_ge))
            link(ve.tensor_copy(q0, qk))
            for j in range(2, LEVELS + 1):
                link(ve.scalar_tensor_tensor(qk, rk, float(j * BLK), qk, ALU.is_ge, ALU.add))
            link(ve.scalar_tensor_tensor(ok, qk, float(NE - 1), ok, ALU.add, ALU.add))
            link(ve.tensor_tensor(ok, ok, ek, ALU.subtract))
            link(ve.tensor_tensor(ok, ok, q0, ALU.mult))
            link(ve.tensor_tensor(ok, ok, ek, ALU.add))
            link(ve.scalar_tensor_tensor(rk, qk, -float(BLK), rk, ALU.mult, ALU.add))
            fl = lambda x: x.rearrange("p t k -> p (t k)")
            R3, B3 = [P, 2 * NTT, BLK], [P, 2 * NTT, NBLK]
            link(ve.tensor_tensor(ohr, iota_r.unsqueeze(1).broadcast_to(R3), fl(rk).unsqueeze(2).to_broadcast(R3), ALU.is_equal))
            link(ve.tensor_tensor(ohb, iota_b.unsqueeze(1).broadcast_to(B3), fl(ok).unsqueeze(2).to_broadcast(B3), ALU.is_equal))
            link(ve.tensor_tensor(ohb, ohb, fl(token).unsqueeze(2).to_broadcast(B3), ALU.mult))
            ve.nop().then_inc(sel_set, 1)
            ve.wait_ge(idx_ps, 1)
            tv, te = tabf[0:BLK, 0, :], tabf[0:BLK, 1, :]
            link(ve.tensor_scalar(tv, ps[0:BLK, 2, 0:NBLK], -1.0, None, ALU.add))
            link(ve.tensor_scalar(te, tv, 0.0, float(OOB), ALU.is_lt, ALU.mult))
            link(ve.tensor_tensor(te, te, tv, ALU.add))
            ve.tensor_copy(sidx[0:BLK, :], te)
            link(ve.tensor_scalar(tv, tv, float(N), -float(N), ALU.is_ge, ALU.mult))
            link(ve.tensor_tensor(tv, tv, te, ALU.add))
            ve.tensor_copy(gidx[0:BLK, :], tv).then_inc(idx_set, 1)

            def rows_out(s):
                src = ps[:, 0:2, :].rearrange("p b (k c) -> p (b k) c", k=4)[:, :, 0:BLK]
                return ve.tensor_copy(xgt[s], src)

            ve.wait_ge(xgt_ps, 1)
            rows_out(0).then_inc(xgt_sb, 1)
            ve.nop().then_inc(hact_sb, 2)

            def expert(i, s):
                e = SLOTS * i + s
                if not (isinstance(i, int) and e == 0):
                    ve.wait_ge(dn_ps, e)
                for f in range(KF):
                    ve.wait_ge(gact_sb, e * KF + f + 1)
                    ve.tensor_tensor(hact[:, f, :], ps[:, 4 + f % 2, 0:BLK], gact[:, f, :], ALU.mult).then_inc(hact_sb, 1)
                if not (isinstance(i, int) and e == NE - 1):
                    ve.wait_ge(xgt_ps, e + 2)
                    rows_out((s + 1) % SLOTS).then_inc(xgt_sb, 1)

            for s in range(SLOTS):
                expert(0, s)
            with ve.Fori(1, ROUNDS) as i:
                for s in range(SLOTS):
                    expert(i, s)
            for s in range(NE % SLOTS):
                expert(ROUNDS, s)
            count = ve.value_load(over_i[0:1, OVER:OVER + 1], min_val=0, max_val=OVER)
            with ve.If(count > 0):
                with ve.Fori(0, count) as i:
                    ve.wait_ge(ov["tps"], i + 1)
                    rows_out(0).then_inc(ov["tsb"], 1)
                    for f in range(KF):
                        ve.wait_ge(ov["ga"], KF * i + f + 1)
                        ve.tensor_tensor(hact[:, f, :], ps[:, 4, 0:BLK], gact[:, f, :], ALU.mult).then_inc(ov["ha"], 1)

            def scale_row(t):
                n = TILES[t][1]
                ve.wait_ge(hnorm, NTT + t + 1)
                ve.tensor_tensor(fh[t][0:n], fh[t][0:n], g2row[0:n], ALU.mult).then_inc(fmul, 1)

            ve.wait_ge(rows2_loaded, 16 * 7)
            for t, (c0, n) in enumerate(TILES):
                s = t % 2
                ve.wait_ge(fin_loaded[s], 32 * (t // 2 + 1))
                ve.wait_ge(fweigh, t + 1)
                hs, y1, y2 = fh[t][0:n], fy1[s][0:n], fy2[s][0:n]
                link(ve.scalar_tensor_tensor(y1, y2, gw[0:n, 1, t:t + 1], y1, ALU.mult, ALU.add))
                ve.scalar_tensor_tensor(hs, hs, ALPHA, y1, ALU.mult, ALU.add).then_inc(fmix, 1)
                ve.wait_ge(fmix, t + 1)
                statistics(hs, s, n, hvar)
                if t >= 1:
                    scale_row(t - 1)
                ve.wait_ge(hsd, NTT + t + 1)
                scaling(s, n, hscale)
            scale_row(NTT - 1)

        @block.gpsimd
        def _(po):
            po.memset(onesm[:, :], 1.0 / CC)
            po.memset(uext[:, :, 0:PAD], 0.0).then_inc(pads_set, 1)
            po.memset(onesb[:, :], 1.0)
            po.memset(logits[:, :], 0.0)
            po.wait_ge(ci_loaded, 16)
            po.tensor_copy(beforeb[:, :], before).then_inc(pads_set, 1)
            po.wait_ge(tile_mm, 2)
            for b in range(NB):
                for g, dst in enumerate((kv0s, kv1s, kv2s)):
                    w = caches[g].shape[1]
                    keep = dst.shape[2] - NT
                    src = caches[g][b, w - keep:w].rearrange("s two h e -> (s two h e)").rearrange("(c f) -> c f", c=32)
                    po.dma_start(dst[0, b, 0:keep].rearrange("s two h e -> (s two h e)").rearrange("(c f) -> c f", c=32), src).then_inc(copied, 16)
                po.dma_start(conv_s[0, b, 0:PAD - NT].rearrange("s c -> (s c)").rearrange("(c f) -> c f", c=16),
                             a["state_conv"][0, b, NT:PAD].rearrange("s c -> (s c)").rearrange("(c f) -> c f", c=16)).then_inc(copied, 16)

            def load_cache(dst, b, two, done):
                c = caches
                po.dma_start(dst[:, 0, :], c[0][b, :, two].rearrange("s h e -> s (h e)")).then_inc(done, 16)
                po.dma_start(dst[:, 1:5, :], c[1][b, :, two].rearrange("(p t) h e -> p t (h e)", t=4)).then_inc(done, 16)
                po.dma_start(dst[:, 5, :], c[2][b, :, two].rearrange("(a t) h e -> a t (h e)", t=16)[:, 0:4, :]).then_inc(done, 16)

            for b in range(2):
                load_cache(kc[:, b], b, 0, kc_loaded[b])
            po.wait_ge(rotated, 12)
            for b in range(2):
                load_cache(vc[:, b], b, 1, vc_loaded[b])
            po.wait_ge(tile_mm, MT)
            po.memset(eb[:, 4320:4704], 0.0).then_inc(qbd_zero, 1)
            po.wait_ge(k_sb, 6)
            po.wait_ge(v_sb, 6)
            po.dma_start(kv0p[0, 0, :, 0].rearrange("s h e -> s (h e)"), kout0).then_inc(kout_stored, 16)
            po.dma_start(kv0p[0, 0, :, 1].rearrange("s h e -> s (h e)"), vt[:, 3, 0:256]).then_inc(stored, 16)
            for g, dst in ((1, kv1p), (2, kv2p)):
                rows = dst[0, 0].rearrange("(p r) two h e -> p r two (h e)", r=4)
                po.dma_start(rows[:, :, 0, :], kout12[:, :, (g - 1) * 256:g * 256]).then_inc(kout_stored, 16)
                po.dma_start(rows[:, :, 1, :], vt[:, :, g * 256:(g + 1) * 256]).then_inc(stored, 16)
            po.wait_ge(s_sb, 1)
            for g, dst in enumerate((kv0s, kv1s, kv2s)):
                w = dst.shape[2]
                for t in range(NT):
                    po.dma_start(dst[0, :, w - NT + t].rearrange("b two h e -> b (two h e)"),
                                 skv[t:NS:NT, g].rearrange("p two c -> p (two c)")).then_inc(kout_stored, 16)
            po.wait_ge(u_sb, 1)
            po.dma_start(conv_p[0, 0], urow_p[0:PAD, :]).then_inc(stored, 16)
            for t in range(NT):
                po.dma_start(conv_s[0, :, PAD - NT + t], urow_s[t:NS:NT, :]).then_inc(stored, 16)
            for b in range(2, NB):
                po.wait_ge(kt_ps, b - 1)
                load_cache(kc[:, b % 2], b, 0, kc_loaded[b % 2])
            for b in range(2, NB):
                po.wait_ge(vs_used, b - 1)
                load_cache(vc[:, b % 2], b, 1, vc_loaded[b % 2])
            for m in range(KD):
                po.wait_ge(br_used, m + 1)
                po.tensor_tensor(ga[:, m, :], ga[:, m, :], gc[:, m, :], ALU.add).then_inc(merged, 1)
            po.memset(xt_t[:, 0:SLOTS * D], 0.0).then_inc(xg_zero, 1)
            for t, (c0, n) in enumerate(TILES):
                po.wait_ge(hdone, t + 1)
                po.dma_start(h_dram[c0:c0 + n], hrow[0:n, t % 2, :]).then_inc(h_stored[t % 2], 16)
            po.wait_ge(idx_set, 1)
            po.wait_ge(h_stored[0], 48)
            po.wait_ge(h_stored[1], 32)

            def gather(s, col, done, copied_sem, value):
                po.tensor_copy(idx_t[0:BLK, s:s + 1], gidx[0:BLK, col]).then_inc(copied_sem, 1)
                po.wait_ge(copied_sem, value)
                po.sem_inc(pool_steps, 1)
                po.indirect_dma_start(out=xg[s], out_offset=None, in_=h_dram,
                                      in_offset=bass.IndirectOffsetOnAxis(ap=idx_t[0:BLK, s:s + 1], axis=0),
                                      bounds_check=N - 1, oob_is_err=False).then_inc(done, 16)

            def scatter(s, col, done, copied_sem, value):
                po.tensor_copy(idx_t[0:BLK, SLOTS + s:SLOTS + s + 1], sidx[0:BLK, col]).then_inc(copied_sem, 1)
                po.wait_ge(copied_sem, value)
                po.sem_inc(pool_steps, 1)
                po.indirect_dma_start(out=y_dram, out_offset=bass.IndirectOffsetOnAxis(ap=idx_t[0:BLK, SLOTS + s:SLOTS + s + 1], axis=0),
                                      in_=yo[s], in_offset=None, bounds_check=2 * N - 1, oob_is_err=False).then_inc(done, 16)

            po.wait_ge(xg_zero, 1)
            for s in range(SLOTS):
                gather(s, slice(s, s + 1), gathered[s], idx_set_e, s + 1)

            def expert(i, s, ahead):
                e = SLOTS * i + s
                if ahead:
                    po.wait_ge(xgt_ps, e + 1)
                    gather(s, bass.ds(e + SLOTS, 1), gathered[s], idx_set_e, 2 * e + SLOTS + 1)
                po.wait_ge(yo_sb, e + 2)
                scatter(s, bass.ds(e, 1), scattered[s], idx_set_e, 2 * e + SLOTS + 2 if ahead else NE + e + 1)

            with po.Fori(0, ROUNDS - 1) as i:
                for s in range(SLOTS):
                    expert(i, s, True)
            for s in range(SLOTS):
                expert(ROUNDS - 1, s, s < NE % SLOTS)
            for s in range(NE % SLOTS):
                expert(ROUNDS, s, False)
            for s in range(SLOTS):
                blocks = (NE - s + SLOTS - 1) // SLOTS
                po.wait_ge(gathered[s], 16 * blocks)
                po.wait_ge(scattered[s], 16 * blocks)
            po.wait_ge(xgt_ps, NE)
            count = po.value_load(over_i[0:1, OVER:OVER + 1], min_val=0, max_val=OVER)
            with po.If(count > 0):
                with po.Fori(0, count) as i:
                    gather(0, bass.ds(i + NE, 1), ov["gat"], ov["idx"], 2 * i + 1)
                    po.wait_ge(ov["yo"], i + 1)
                    scatter(0, bass.ds(i + NE, 1), ov["sca"], ov["idx"], 2 * i + 2)
                    po.wait_ge(ov["sca"], 16 * i + 16)
                    po.sem_inc(pool_steps, 1)
            po.nop().then_inc(over_done, 1)
            for t, (c0, n) in enumerate(TILES):
                po.wait_ge(fmul, t + 1)
                po.tensor_tensor(fh[t][0:n], fh[t][0:n], b2row[0:n], ALU.add).then_inc(fdone, 1)
            po.wait_ge(copied, 16 * 4 * NB)
            po.wait_ge(stored, 16 * 8)
            po.wait_ge(kout_stored, 16 * 15)


INPUTS = ['x_prompt', 'x_sample', 'cache_kv_w128', 'cache_kv_w512', 'cache_kv_w2048', 'state_conv', 'w_in', 'b_in', 'w_dw',
          'b_dw', 'conv_ln_g', 'conv_ln_b', 'w_conv_out', 'b_conv_out', 'w_attn_out', 'w_o', 'ln1_g', 'ln1_b',
          'w_router_group', 'b_router_group', 'w_router_expert', 'b_router_expert', 'w_expert_gate', 'w_expert_up',
          'w_expert_down', 'ln2_g', 'ln2_b']
OUTPUTS = [(1, SEQ, D), (NB, NT, D), (1, 1, 128, 2, 4, 64), (1, 1, 512, 2, 4, 64), (1, 1, 512, 2, 4, 64), (1, 1, PAD, CC),
           (1, NB, 128, 2, 4, 64), (1, NB, 512, 2, 4, 64), (1, NB, 516, 2, 4, 64), (1, NB, PAD, CC)]


def kernel(**inputs):
    from concourse import bacc
    from concourse.bass_utils import run_bass_kernel_spmd

    nc = bacc.Bacc("TRN2", target_bir_lowering=False, num_devices=1)
    arrays, args = {}, {}
    for name in INPUTS:
        arrays["in_" + name] = np.ascontiguousarray(inputs[name])
        args[name] = nc.dram_tensor("in_" + name, arrays["in_" + name].shape, F32, kind="ExternalInput").ap()
    arrays["in_constants"] = constants()
    args["constants"] = nc.dram_tensor("in_constants", arrays["in_constants"].shape, F32, kind="ExternalInput").ap()
    outs = [nc.dram_tensor(f"out_{i}", shape, F32, kind="ExternalOutput").ap() for i, shape in enumerate(OUTPUTS)]
    build(nc, args, outs)
    r = run_bass_kernel_spmd(nc, [arrays], core_ids=[0])
    return tuple(r.results[0][f"out_{i}"] for i in range(len(OUTPUTS)))
```

```python
from contextlib import ExitStack

import numpy as np

import concourse.bass as bass
from concourse import mybir
from concourse.alu_op_type import AluOpType as ALU

F32 = mybir.dt.float32
F32R = mybir.dt.float32r
BF16 = mybir.dt.bfloat16
I32 = mybir.dt.int32
ACT = mybir.ActivationFunctionType
AX_X = mybir.AxisListType.X

P = 128
D = 1024
KD = D // P
SEQ, NB, NT = 512, 8, 4
NS = NB * NT
N = SEQ + NS
HALF = N // 2
IN_W = 5376
MT = IN_W // P
Q0, K0, V0, UA0, UB0, G0 = 0, 6, 12, 18, 22, 26
CT = 4
CC = CT * P
TAPS = 31
PAD = TAPS - 1
HEADS, HD = 4, 64
WIN = (128, 512, 2048)
PAST = 512
ALPHA = 2 ** 0.25
EPS = 1e-5
SCALE = HD ** -0.5
NEG = -1e30
NGRP, NPER = 4, 8
NE = NGRP * NPER
FE = 512
KF = FE // P
BLK = 96
OVER = (2 * N) // BLK
NBLK = NE + OVER
LEVELS = (N - 1) // BLK
SLOTS = 3
ROUNDS = NE // SLOTS
OOB = 1 << 20
TILES = [(t * P, min(P, N - t * P)) for t in range((N + P - 1) // P)]
NTT = len(TILES)
SKEYS = 3 * P + 3 * NS
PKEYS = SEQ + 2 * P


def constants():
    half = HD // 8
    pos = np.concatenate([np.arange(SEQ), np.tile(PAST + np.arange(NT), NB)]).astype(np.float32)
    inv = (np.float32(500000.0) ** (-np.arange(half, dtype=np.float32) / np.float32(half))).astype(np.float32)
    ang = (pos[None, :] * inv[:, None]).astype(np.float32)
    cos, sin = np.ones((P, N), np.float32), np.zeros((P, N), np.float32)
    rot = np.zeros((P, P), np.float32)
    for h in range(0, P, HD):
        for j in range(half):
            for i in (h + j, h + j + half):
                cos[i], sin[i] = np.cos(ang[j]), np.sin(ang[j])
            rot[h + j + half, h + j] = -1.0
            rot[h + j, h + j + half] = 1.0
    eye = np.eye(P, dtype=np.float32)
    before = np.triu(np.ones((P, P), np.float32), 1)
    rows = np.tile(np.concatenate([np.arange(BLK), np.arange(NBLK), np.arange(NE)]).astype(np.float32), (P, 1))
    p = np.arange(P)
    masks = []
    for r in range(4):
        t, key = 4 * p[:, None] + r, np.arange(SEQ)[None, :]
        masks.append((key <= t) & (key >= t - WIN[0]))
    masks.append(p[None, :] <= p[:, None])
    masks.append((p[None, :] <= p[:, None]) & ((p[:, None] - p[None, :]) % 4 == 0))
    pmask = np.where(np.concatenate(masks, 1), 0.0, NEG).astype(np.float32)
    b, t = (p // 8) % NB, (p // 2) % NT
    col, new = np.arange(P)[None, :], np.arange(NS)[None, :]
    own, nt = new // NT == b[:, None], new % NT
    smask = np.concatenate([col >= t[:, None], col >= 0 * t[:, None], col % 4 == t[:, None],
                            own & (nt <= t[:, None]), own & (nt == t[:, None]), own & (nt == t[:, None])], 1)
    smask = np.where(smask, 0.0, NEG).astype(np.float32)
    token = np.zeros((P, NTT, 2), np.float32)
    for i in range(NTT):
        for k in range(2):
            token[:, i, k] = 1 + k * N + i * P + p
    return np.concatenate([cos, sin, eye, rot, before, rows, token.reshape(P, -1), pmask, smask], 1)


C_COS, C_SIN = 0, N
C_EYE = 2 * N
C_ROWS = C_EYE + 3 * P
NROWS = BLK + NBLK + NE + 2 * NTT
C_PM = C_ROWS + NROWS
C_SM = C_PM + 4 * SEQ + 2 * P
C_END = C_SM + SKEYS


def build(nc, a, o):
    y_prompt, y_sample, kv0p, kv1p, kv2p, conv_p, kv0s, kv1s, kv2s, conv_s = o
    h_dram = nc.dram_tensor("h_rows", [N, D], F32, kind="Internal").ap()
    y_dram = nc.dram_tensor("expert_rows", [2 * N, D], F32, kind="Internal").ap()
    caches = [a["cache_kv_w128"][0], a["cache_kv_w512"][0], a["cache_kv_w2048"][0]]
    const = a["constants"]
    w_in = a["w_in"][0].rearrange("(k p) n -> p k n", p=P)
    wg_d = a["w_expert_gate"][0].rearrange("e (p k) f -> e p (k f)", k=KD)
    wu_d = a["w_expert_up"][0].rearrange("e (p k) f -> e p (k f)", k=KD)
    wd_d = a["w_expert_down"][0].rearrange("e (k p) d -> e p k d", p=P)
    x_p, x_s = a["x_prompt"][0], a["x_sample"].rearrange("b t d -> (b t) d")

    with ExitStack() as ctx:
        def sb(name, cols, dt=F32, parts=P):
            return ctx.enter_context(nc.sbuf_tensor(name, [parts, cols], dt))

        def sem(name):
            return ctx.enter_context(nc.semaphore(name))

        with nc.sbuf_tensor("region_a", [P, 12288], F32) as ea, nc.sbuf_tensor("region_b", [P, 12288], F32) as eb, nc.sbuf_tensor("z_conv_gates", [P, (MT - V0 - 6) * N], F32) as z2:
            pass
        ea_split = sb("region_a_split", 12288, F32R)
        eb_split, z_split = sb("region_b_split", 12288, F32R), sb("z_split", (MT - V0 - 6) * N, F32R)
        xt_t = sb("x_columns", KD * N)
        sc, vt_t = sb("scratch", 3256), sb("value_rows", 3072)
        wa_t, at_t = sb("w_attn", 2048), sb("attn_columns", 2 * N)
        ci = sb("const_small", 3 * P + NROWS)
        colb = sb("column_vectors", 62 + TAPS * CT)
        small = sb("small", 44)
        gidx, sidx = sb("gather_rows", NBLK, I32), sb("scatter_rows", NBLK, I32)
        over_i = sb("further_blocks", OVER + 1, I32)
        over_idx = sb("block_rows", 2 * SLOTS, I32)
        ps = ctx.enter_context(nc.psum_tensor("ps", [P, 8, 512], F32))

        eye, rot, before = ci[:, 0:P], ci[:, P:2 * P], ci[:, 2 * P:3 * P]
        iota_r = ci[:, 3 * P:3 * P + BLK]
        iota_b = ci[:, 3 * P + BLK:3 * P + BLK + NBLK]
        iota_e = ci[:, 3 * P + BLK + NBLK:3 * P + BLK + NBLK + NE]
        token = ci[:, 3 * P + BLK + NBLK + NE:].rearrange("p (t k) -> p t k", k=2)
        bdw_c, clg_c, clb_c, bco_c = (colb[:, i:i + 8] for i in (42, 46, 50, 54))
        wdw_c = colb[:, 62:62 + TAPS * CT]

        zqkv = ea[:, 0:18 * N].rearrange("p (m n) -> p m n", n=N)
        pmask = ea[:, 18 * N:18 * N + 4 * SEQ + 2 * P]
        wring = eb[:, 0:4096].rearrange("p (s k n) -> p s k n", s=2, k=KD)
        skv = eb[:, 4096:5632].rearrange("p (g two c) -> p g two c", g=3, two=2)
        smask = eb[:, 5632:5632 + SKEYS]
        qbd = wa_t[:, 0:384].rearrange("p (m b j) -> p m b j", m=6, j=2)
        st_sb, stn_sb = wa_t[:, 384:768], wa_t[:, 768:1152]
        sp = wa_t[:, 1152:1152 + SKEYS]
        kc = eb[:, 6144:9216].rearrange("p (s t c) -> p s t c", s=2, t=6)
        vc = eb[:, 9216:12288].rearrange("p (s t c) -> p s t c", s=2, t=6)
        trig = eb[:, 12288 - 2 * N:12288]
        cos, sin = trig[:, 0:N], trig[:, N:2 * N]
        w_hi = eb_split[:, 6144:10240].rearrange("p (s k n) -> p s k n", s=2, k=KD)
        w_lo = eb_split[:, 0:4096].rearrange("p (s k n) -> p s k n", s=2, k=KD)
        wo = eb[:, 0:KD * D].rearrange("p (k n) -> p k n", k=KD)

        zr = z2[:, :].rearrange("p (m n) -> p m n", n=N)
        ua, ub = zr[:, 0:CT], zr[:, CT:2 * CT]
        xs = z2[:, 8 * N:8 * N + NTT * D].rearrange("p (t d) -> p t d", d=D)
        ga, gc = zr[:, 8:16], zr[:, 16:24]
        wo_hi = ea_split[:, 0:KD * D].rearrange("p (k n) -> p k n", k=KD)
        wo_lo = eb_split[:, 0:KD * D].rearrange("p (k n) -> p k n", k=KD)
        ga_lo, ga_hi = (z_split[:, c * N:(c + KD) * N].rearrange("p (m n) -> p m n", n=N) for c in (8, 16))
        SPLIT = 26 - 4
        x_hi = z_split[:, 8 * N:16 * N].rearrange("p (k n) -> p k n", k=KD)
        x_lo = z_split[:, 16 * N:24 * N].rearrange("p (k n) -> p k n", k=KD)
        xt = xt_t[:, :].rearrange("p (k n) -> p k n", k=KD)
        wco = xt_t[:, 0:CT * D].rearrange("p (k n) -> p k n", k=CT)
        rows_a, rows_b = vt_t[0:62, 0:P], vt_t[0:TAPS * CT, P:2 * P]
        rtmp = vt_t[:, 2 * P:2 * P + 2 * N].rearrange("p (s n) -> p s n", s=2)
        cst = vt_t[0:4 * PAD, 1408:2432].rearrange("p (j c) -> p j c", j=2)
        vt = vt_t[:, :].rearrange("p (r c) -> p r c", r=4)
        uext = sc[:, 0:CT * (SEQ + PAD)].rearrange("p (c s) -> p c s", c=CT)
        sext = sc[:, CT * (SEQ + PAD):3256].rearrange("p (c b s) -> p c b s", c=CT, b=NB)
        ktr = sc[:, 0:3072].rearrange("p (s m k) -> p s m k", s=2, m=12)
        prob = sc[:, 0:2 * PKEYS].rearrange("p (s k) -> p s k", s=2)
        prt = sc[:, 2 * PKEYS:4 * PKEYS].rearrange("p (s m k) -> p s m k", s=2, m=6)
        wa = wa_t[:, :].rearrange("p (k n) -> p k n", k=2)
        at = at_t[:, :].rearrange("p (k n) -> p k n", k=2)

        acc, cen = ua, ub
        rstd_c = ps[:, 2:4, 0:HALF]
        onesm = sb("ones_mean", P)[:, :]
        onesb = sb("ones_count", P, BF16)[:, :]
        beforeb = sb("before_count", P, BF16)[:, :]
        nmx_p, l_p = small[:, 0:16], small[:, 16:32]
        rinv = small[:, 32:36]
        pmx = small[:, 40:42]
        cst_u = ea[:, 18 * N + 4 * SEQ + 2 * P:18 * N + 4 * SEQ + 3 * P].rearrange("p (c n) -> p c n", c=CT)
        urow_p, urow_s = z2[:, 4 * N:4 * N + CC], z2[:, 4 * N + CC:4 * N + 2 * CC]
        krow = z2[:, 4 * N + 2 * CC:4 * N + 4 * CC].rearrange("p (s r c) -> p s r c", s=2, r=4)
        atk = sb("attn_rows", 256)[:, :]
        nmx_s, l_s, rinv_s = small[:, 36:37], small[:, 37:38], small[:, 38:39]

        wrv = sc[:, 2 * D:2 * D + KD * 36].rearrange("p (k n) -> p k n", k=KD)
        br = sb("b_router", 36)[:, :]
        hrow = z2[:, 0:2048].rearrange("p (s d) -> p s d", s=2)
        xrow = vt_t[:, 0:2 * D].rearrange("p (s d) -> p s d", s=2)
        g1row, b1row = sc[:, 0:D], sc[:, D:2 * D]
        hcol = xt_t[:, 3 * D:4 * D].rearrange("p (k n) -> p k n", k=KD)
        def ln_cols(first, width=1):
            return [small[:, 18 * q + first:18 * q + first + width] for q in range(2)]

        stats, mv, var_e, sd, rs, nmr = ln_cols(0, 12), ln_cols(12, 2), ln_cols(14), ln_cols(15), ln_cols(16), ln_cols(17)
        logits = sb("logits", NTT * 36)
        lg = logits[:, :].rearrange("p (t c) -> p t c", c=36)
        gates = sb("gate_weights", NTT * 2)
        gw = gates[:, :].rearrange("p (k t) -> p k t", k=2)
        mb = sb("choices", NTT * NE, BF16)[:, :].rearrange("p (t e) -> p t e", e=NE)
        at_col = [0]

        def route(*dims):
            n, c = int(np.prod(dims)), at_col[0]
            at_col[0] += n
            names = "abc"[:len(dims)]
            v = vt_t[:, c:c + n]
            return v if len(dims) == 1 else v.rearrange(f"p ({' '.join(names)}) -> p {' '.join(names)}",
                                                        **{names[i]: dims[i] for i in range(1, len(dims))})

        ohr, ohb = route(2 * NTT, BLK), route(2 * NTT, NBLK)
        oh, rank = route(2, NTT, NE), route(NTT, NE)
        emf, rt32, io32 = route(NTT * NE), route(NTT, NE), route(NTT, NE)
        em = emf.rearrange("p (t e) -> p t e", e=NE)
        em4 = emf.rearrange("p (t g e) -> p t g e", g=NGRP, e=NPER)
        rt_a4, rt_b4, rt_c4, rt_g3 = (route(NTT, NGRP) for _ in range(4))
        v12, e12 = route(2, NTT), route(2, NTT)
        m1, i1, rt_d = route(NTT), route(NTT), route(NTT)
        cnt, nov, ovst, tmp32, ovf = route(NE), route(NE), route(NE), route(NE), route(OVER + 1)
        ovend, tabf = route(2, NE), route(2, NBLK)
        rk, ek, ok, qk, q0 = (route(NTT, 2) for _ in range(5))

        wslot = [ea, eb, z2]
        wgv = [w[:, 0:4096].rearrange("p (k f m) -> p k f m", k=KD, f=KF) for w in wslot]
        wuv = [w[:, 4096:8192].rearrange("p (k f m) -> p k f m", k=KD, f=KF) for w in wslot]
        wdv = [w[:, 8192:12288].rearrange("p (k d) -> p k d", k=KF) for w in wslot]
        xg = [xt_t[0:BLK, s * D:(s + 1) * D] for s in range(SLOTS)]
        yo = [vt_t[0:BLK, s * D:(s + 1) * D] for s in range(SLOTS)]
        xgt = [sc[:, s * 768:(s + 1) * 768].rearrange("p (k c) -> p k c", k=KD) for s in range(SLOTS)]
        gact = sc[:, 2304:2688].rearrange("p (f c) -> p f c", f=KF)
        hact = sc[:, 2688:3072].rearrange("p (f c) -> p f c", f=KF)
        idx_t = over_idx

        x_loaded = [sem(f"x_loaded{s}") for s in range(2)]
        over_set = sem("over_set")
        rows_loaded, ci_loaded, trig_loaded = sem("rows_loaded"), sem("ci_loaded"), sem("trig_loaded")
        mask_loaded, state_loaded = sem("mask_loaded"), sem("state_loaded")
        win_loaded = [sem(f"win_loaded{s}") for s in range(2)]
        tile_mm, tile_free = sem("tile_mm"), sem("tile_free")
        pads_set = sem("pads_set")
        xt_ps, xt_sb = sem("xt_ps"), sem("xt_sb")
        colb_ps, colb_sb = sem("colb_ps"), sem("colb_sb")
        rot_ps, rot_used, rotated = sem("rot_ps"), sem("rot_used"), sem("rotated")
        state_ps, state_sb = sem("state_ps"), sem("state_sb")
        dve_chain, pool_steps, sp_steps = sem("dve_chain"), sem("pool_steps"), sem("sp_steps")
        x_high, x_split, w_high, w_split = sem("x_high"), sem("x_split"), sem("w_high"), sem("w_split")
        conv_step, u_set = sem("conv_step"), sem("u_set")
        gate_mm, gate_free, gate_sig = sem("gate_mm"), sem("gate_free"), sem("gate_sig")
        v_ps, v_sb, k_ps, k_sb, s_ps, s_sb = (sem(x) for x in ("v_ps", "v_sb", "k_ps", "k_sb", "s_ps", "s_sb"))
        u_ps, u_sb = sem("u_ps"), sem("u_sb")
        stored, copied = sem("stored"), sem("copied")
        krow_stored = [sem(f"krow_stored{s}") for s in range(2)]
        kc_loaded = [sem(f"kc_loaded{s}") for s in range(2)]
        vc_loaded = [sem(f"vc_loaded{s}") for s in range(2)]
        kt_ps, kt_dve, kt_act, st_ps, st_done = (sem(x) for x in ("kt_ps", "kt_dve", "kt_act", "st_ps", "st_done"))
        qbd_set, sback_ps, sprob, spn, spt_ps, spt_sb, vs_used, so_ps, so_sb = (
            sem(x) for x in ("qbd_set", "sback_ps", "sprob", "spn", "spt_ps", "spt_sb", "vs_used", "so_ps", "so_sb"))
        smax = sem("smax")
        qk_ps, pmax, pexp, pt_ps, pt_dve, pt_act, pv_ps, otok, at_ps, at_sb = (
            sem(x) for x in ("qk_ps", "pmax", "pexp", "pt_ps", "pt_dve", "pt_act", "pv_ps", "otok", "at_ps", "at_sb"))
        mean_ps, cen_sb, sq_sb, var_ps, veps, csd, cnorm, cact = (
            sem(x) for x in ("mean_ps", "cen_sb", "sq_sb", "var_ps", "veps", "csd", "cnorm", "cact"))
        conv_done = sem("conv_done")
        wco_loaded, wa_loaded, wo_loaded = sem("wco_loaded"), sem("wa_loaded"), sem("wo_loaded")
        br_ps, br_used, merged = sem("br_ps"), sem("br_used"), sem("merged")
        xrow_loaded = [sem(f"xrow_loaded{s}") for s in range(2)]
        rows1_loaded, wr_loaded = sem("rows1_loaded"), sem("wr_loaded")
        y_ps, y_used, hvar, hsd, hscale, hnorm, hdone = (
            sem(x) for x in ("y_ps", "y_used", "hvar", "hsd", "hscale", "hnorm", "hdone"))
        h_stored = [sem(f"h_stored{s}") for s in range(2)]
        ht_ps, ht_sb, lg_ps, lg_sb = sem("ht_ps"), sem("ht_sb"), sem("lg_ps"), sem("lg_sb")
        rmax, rexp, mset, cnt_ps, sel_set, idx_ps, idx_set = (
            sem(x) for x in ("rmax", "rexp", "mset", "cnt_ps", "sel_set", "idx_ps", "idx_set"))
        e_loaded = [[sem(f"{n}_loaded{s}") for s in range(SLOTS)] for n in ("wgu", "wd")]
        gathered = [sem(f"gathered{s}") for s in range(SLOTS)]
        scattered = [sem(f"scattered{s}") for s in range(SLOTS)]
        idx_set_e, xgt_ps, xgt_sb, gu_ps, gact_sb, hact_sb, dn_ps, yo_sb = (
            sem(x) for x in ("idx_copied", "xgt_ps", "xgt_sb", "gu_ps", "gact_sb", "hact_sb", "dn_ps", "yo_sb"))
        ov = {x: sem("ov_" + x) for x in ("load", "idx", "gat", "tps", "tsb", "gu", "ga", "ha", "dn", "yo", "sca")}
        over_done = sem("over_done")
        fin_loaded = [sem(f"fin_loaded{s}") for s in range(2)]
        rows2_loaded = sem("rows2_loaded")
        fmix, fmul, fdone = (sem(x) for x in ("fmix", "fmul", "fdone"))
        fweigh, xg_zero, y_stored = sem("fweigh"), sem("xg_zero"), sem("y_stored")
        qbd_zero, br_loaded = sem("qbd_zero"), sem("br_loaded")

        block = ctx.enter_context(nc.Block())
        fh = [z2[:, t * D:(t + 1) * D] for t in range(NTT)]
        fy1 = [z2[:, (NTT + s) * D:(NTT + 1 + s) * D] for s in range(2)]
        fy2 = [z2[:, (NTT + 2 + s) * D:(NTT + 3 + s) * D] for s in range(2)]
        g2row, b2row = z2[:, (NTT + 4) * D:(NTT + 5) * D], z2[:, (NTT + 5) * D:(NTT + 6) * D]

        order = [("conv_rows", 0, 5)] + [("rotate", m, 1) for m in range(12)] + [("values", m, 1) for m in range(6)]
        order.append(("sample_rows", 0, 1))
        for b in range(NB):
            order.append(("cached_keys", b, 2))
            if b < 6:
                order.append(("keys", b, 1))
        order += [(kind, 0, 1) for kind in ("new_keys", "conv_mean", "sample_turn", "conv_var", "sample_probs")]
        order += [("cached_values", b, 2 - b % 2) for b in range(NB)]
        spare = 4 * 16 - sum(step[2] for step in order)
        order += [("attend", i, int(i < spare)) for i in range(16 + 2)]
        starts = np.cumsum([0] + [step[2] for step in order]).tolist()
        steps = [(kind, i, range(q, q + n)) for (kind, i, n), q in zip(order, starts)]
        STORES = 3 + 1 + NT + 3 * NT

        @block.sync
        def _(sp_e):
            def store_rows():
                sp_e.wait_ge(v_sb, 6)
                sp_e.dma_start(kv0p[0, 0, :, 1].rearrange("s h e -> s (h e)"), vt[:, 3, 0:256]).then_inc(stored, 16)
                for g, dst in ((1, kv1p), (2, kv2p)):
                    rows = dst[0, 0].rearrange("(p r) two h e -> p r two (h e)", r=4)
                    sp_e.dma_start(rows[:, :, 1, :], vt[:, :, g * 256:(g + 1) * 256]).then_inc(stored, 16)
                sp_e.wait_ge(u_sb, 1)
                sp_e.dma_start(conv_p[0, 0], urow_p[0:PAD, :]).then_inc(stored, 16)
                for t in range(NT):
                    sp_e.dma_start(conv_s[0, :, PAD - NT + t], urow_s[t:NS:NT, :]).then_inc(stored, 16)
                sp_e.wait_ge(s_sb, 1)
                for g, dst in enumerate((kv0s, kv1s, kv2s)):
                    w = dst.shape[2]
                    for t in range(NT):
                        sp_e.dma_start(dst[0, :, w - NT + t].rearrange("b two h e -> b (two h e)"),
                                       skv[t:NS:NT, g].rearrange("p two c -> p (two c)")).then_inc(stored, 16)

            for s in range(2):
                sp_e.dma_start(xs[:, 2 * s:2 * s + 2, :], x_p[256 * s:256 * s + 256].rearrange("(t p) d -> p t d", p=P)).then_inc(x_loaded[s], 16)
            sp_e.dma_start(xs[0:NS, 4, :], x_s).then_inc(x_loaded[1], 16)

            def load_pair(j, col):
                sp_e.dma_start(wring[:, j % 2], w_in[:, :, col:col + 256]).then_inc(win_loaded[j % 2], 16)

            def copy_batch(b):
                for g, dst in enumerate((kv0s, kv1s, kv2s)):
                    w = caches[g].shape[1]
                    keep = dst.shape[2] - NT
                    src = caches[g][bass.ds(b, 1), w - keep:w].rearrange("o s two h e -> (o s two h e)").rearrange("(c f) -> c f", c=32)
                    sp_e.dma_start(dst[0, bass.ds(b, 1), 0:keep].rearrange("o s two h e -> (o s two h e)").rearrange("(c f) -> c f", c=32), src).then_inc(copied, 16)
                sp_e.dma_start(conv_s[0, bass.ds(b, 1), 0:PAD - NT].rearrange("o s c -> (o s c)").rearrange("(c f) -> c f", c=16),
                               a["state_conv"][0, bass.ds(b, 1), NT:PAD].rearrange("o s c -> (o s c)").rearrange("(c f) -> c f", c=16)).then_inc(copied, 16)

            for j in range(4):
                if j >= 2:
                    sp_e.wait_ge(tile_mm, 2 * (j - 1))
                load_pair(j, UA0 * P + j * 256)
            with sp_e.Fori(0, 4) as i:
                for s in range(2):
                    sp_e.wait_ge(tile_mm, 4 * i + 2 * s + 6)
                    sp_e.dma_start(wring[:, s], w_in[:, :, bass.ds(i * 512 + s * 256, 256)]).then_inc(win_loaded[s], 16)
                    copy_batch(2 * i + s)
            sp_e.wait_ge(tile_mm, 22)
            load_pair(12, 8 * 256)
            for g in range(8):
                if g < 2:
                    sp_e.wait_ge(tile_mm, 24 + 2 * g)
                else:
                    sp_e.wait_ge(gate_mm, 4 * (g - 1))
                load_pair(13 + g, G0 * P + g * 256)
                if g == 3:
                    store_rows()
            sp_e.wait_ge(so_sb, 1)
            sp_e.dma_start(wa, a["w_attn_out"][0].rearrange("(k p) n -> p k n", p=P)).then_inc(wa_loaded, 16)
            sp_e.wait_ge(gate_mm, 32)
            sp_e.wait_ge(stored, 16 * STORES)
            sp_e.dma_start(wco, a["w_conv_out"][0].rearrange("(k p) n -> p k n", p=P)).then_inc(wco_loaded, 16)
            sp_e.dma_start(wo, a["w_o"][0].rearrange("(k p) n -> p k n", p=P)).then_inc(wo_loaded, 16)
            sp_e.dma_start(wdv[1], wd_d[1]).then_inc(e_loaded[1][1], 16)
            sp_e.wait_ge(at_sb, 4)
            for t in range(NTT):
                c0, n = TILES[t]
                if t == 0:
                    sp_e.dma_start(g1row, a["ln1_g"][0].partition_broadcast(P)).then_inc(rows1_loaded, 16)
                    sp_e.dma_start(b1row, a["ln1_b"][0].partition_broadcast(P)).then_inc(rows1_loaded, 16)
                    sp_e.dma_start(wrv[:, :, 0:4], a["w_router_group"][0].rearrange("(k p) n -> p k n", p=P)).then_inc(wr_loaded, 16)
                    sp_e.dma_start(wrv[:, :, 4:36], a["w_router_expert"][0].rearrange("(k p) n -> p k n", p=P)).then_inc(wr_loaded, 16)
                if t >= 2:
                    sp_e.wait_ge(y_used, t - 1)
                src = x_p[c0:c0 + n] if t < 4 else x_s
                sp_e.dma_start(xrow[0:n, t % 2, :], src).then_inc(xrow_loaded[t % 2], 16)
            def load_expert(e, s):
                for n, src in enumerate((wg_d, wu_d)):
                    sp_e.dma_start(wslot[s][:, n * 4096:(n + 1) * 4096],
                                   src[bass.ds(e, 1)].rearrange("o p x -> p (o x)")).then_inc(e_loaded[0][s], 16)

            def load_down(e, s):
                sp_e.dma_start(wdv[s], wd_d[bass.ds(e, 1)].rearrange("o p k d -> p (o k) d")).then_inc(e_loaded[1][s], 16)

            sp_e.wait_ge(y_ps, NTT)
            load_expert(0, 0)
            load_down(0, 0)
            sp_e.wait_ge(lg_ps, NTT)
            sp_e.wait_ge(h_stored[0], 48)
            sp_e.wait_ge(h_stored[1], 32)
            load_expert(1, 1)
            sp_e.wait_ge(xgt_ps, 1)
            load_expert(2, 2)
            load_down(2, 2)

            def reload(i, s):
                e = SLOTS * i + s
                sp_e.wait_ge(gu_ps, KF * (e - SLOTS + 1))
                load_expert(e, s)
                sp_e.wait_ge(dn_ps, e - SLOTS + 1)
                load_down(e, s)

            with sp_e.Fori(1, ROUNDS) as i:
                for s in range(SLOTS):
                    reload(i, s)
            for s in range(NE % SLOTS):
                reload(ROUNDS, s)
            sp_e.wait_ge(dn_ps, NE - NE % SLOTS)
            for t, (c0, n) in enumerate(TILES):
                sp_e.dma_start(fh[t][0:n], h_dram[c0:c0 + n]).then_inc(rows2_loaded, 16)
            sp_e.dma_start(g2row, a["ln2_g"][0].partition_broadcast(P)).then_inc(rows2_loaded, 16)
            sp_e.dma_start(b2row, a["ln2_b"][0].partition_broadcast(P)).then_inc(rows2_loaded, 16)
            sp_e.wait_ge(idx_set, 1)
            sp_e.wait_ge(dn_ps, NE)
            sp_e.wait_ge(over_set, 1)
            count = sp_e.value_load(over_i[0:1, OVER:OVER + 1], min_val=0, max_val=OVER)
            with sp_e.If(count > 0):
                with sp_e.Fori(0, count) as i:
                    e = sp_e.value_load(over_i[0:1, bass.ds(i, 1)], min_val=0, max_val=NE - 1)
                    for n, src in enumerate((wg_d, wu_d)):
                        sp_e.dma_start(ea[:, n * 4096:(n + 1) * 4096],
                                       src[bass.ds(e, 1)].rearrange("o p x -> p (o x)")).then_inc(ov["load"], 16)
                    sp_e.dma_start(wdv[0], wd_d[bass.ds(e, 1)].rearrange("o p k d -> p (o k) d")).then_inc(ov["load"], 16)
                    sp_e.wait_ge(ov["sca"], 16 * i + 16)
                    sp_e.sem_inc(sp_steps, 1)
            sp_e.wait_ge(over_done, 1)

            def load_results(t):
                c0, n = TILES[t]
                s = t % 2
                if t >= 2:
                    sp_e.wait_ge(fmix, t - 1)
                sp_e.dma_start(fy1[s][0:n], y_dram[c0:c0 + n]).then_inc(fin_loaded[s], 16)
                sp_e.dma_start(fy2[s][0:n], y_dram[N + c0:N + c0 + n]).then_inc(fin_loaded[s], 16)

            for t in range(NTT):
                load_results(t)
            for t, (c0, n) in enumerate(TILES):
                sp_e.wait_ge(fdone, t + 1)
                dst = y_prompt[0, c0:c0 + n] if t < 4 else y_sample.rearrange("b t d -> (b t) d")
                sp_e.dma_start(dst, fh[t][0:n]).then_inc(y_stored, 16)
            sp_e.wait_ge(y_stored, 16 * NTT)

        @block.tensor
        def _(pe):
            pe.wait_ge(ci_loaded, 16)
            for t, (c0, n) in enumerate(TILES):
                if t == 0:
                    pe.wait_ge(x_loaded[0], 16)
                if t == 2:
                    pe.wait_ge(x_loaded[1], 32)
                if t >= 2:
                    pe.wait_ge(xt_sb, t - 1)
                for k in range(KD):
                    last = pe.transpose(ps[:, 4 + 2 * (t % 2) + k // 4, (k % 4) * P:(k % 4) * P + n],
                                        xs[0:n, t, k * P:(k + 1) * P], eye[0:n, 0:n])
                last.then_inc(xt_ps, 1)
            pe.wait_ge(xt_sb, NTT)
            def project(n, s, c, whole=True):
                pe.wait_ge(tile_free, n + 1)
                for half in range(2):
                    cols = slice(half * HALF, (half + 1) * HALF)
                    out, tile = ps[:, 2 * c + half, 0:HALF], slice(c * P, (c + 1) * P)
                    for k in range(KD):
                        if whole:
                            last = pe.matmul(out, wring[:, s, k, tile], xt[:, k, cols], start=k == 0, stop=k == KD - 1)
                            continue
                        pe.matmul(out, w_hi[:, s, k, tile], x_hi[:, k, cols], start=k == 0, stop=False)
                        pe.matmul(out, w_hi[:, s, k, tile], x_lo[:, k, cols], start=False, stop=False)
                        last = pe.matmul(out, w_lo[:, s, k, tile], x_hi[:, k, cols], start=False, stop=k == KD - 1)
                last.then_inc(tile_mm, 1)

            def project_split(n, s, c):
                pe.wait_ge(w_split, n - 3)
                project(n, s, c, whole=False)

            def small_turns():
                pe.wait_ge(rows_loaded, 16 * 6)
                pe.transpose(ps[:, 6, 0:62], rows_a, eye[0:62, 0:62])
                pe.transpose(ps[:, 6, 64:64 + TAPS * CT], rows_b, eye[0:TAPS * CT, 0:TAPS * CT]).then_inc(colb_ps, 1)
                pe.wait_ge(state_loaded, 32)
                for j in range(2):
                    for c in range(CT):
                        last = pe.transpose(ps[:, 4 + j, c * P:c * P + 4 * PAD], cst[:, j, c * P:(c + 1) * P], eye[0:4 * PAD, 0:4 * PAD])
                last.then_inc(state_ps, 1)

            for n in range(4):
                if n % 2 == 0:
                    pe.wait_ge(win_loaded[n // 2], 16)
                project(n, n // 2, n % 2)
                if n == 1:
                    small_turns()
            pe.wait_ge(x_split, 1)
            for n in range(4, 8):
                project_split(n, n // 2 % 2, n % 2)
            with pe.Fori(0, 4) as i:
                for s in range(2):
                    for c in range(2):
                        project_split(8 + 4 * i + 2 * s + c, s, c)
            project_split(24, 0, 0)
            project_split(25, 0, 1)

            def gate_quarter(q):
                u = q // 2
                t, half, j = u // 2, u % 2, 13 + u // 4
                if q % 8 == 0:
                    pe.wait_ge(win_loaded[j % 2], 16 * (j // 2 + 1))
                if u < 2 and q % 2 == 0:
                    pe.wait_ge(tile_free, 2 + 25)
                elif q % 2 == 0:
                    pe.wait_ge(gate_free, u - 1)
                for k in range(4 * (q % 2), 4 * (q % 2) + 4):
                    last = pe.matmul(ps[:, half, 0:HALF], wring[:, j % 2, k, (t % 2) * P:(t % 2 + 1) * P],
                                     xt[:, k, half * HALF:(half + 1) * HALF], start=k == 0, stop=k == KD - 1, skip_group_check=True)
                if q % 2 == 1:
                    last.then_inc(gate_mm, 1)

            def conv_rows(_):
                pe.wait_ge(u_set, 1)
                pe.wait_ge(state_sb, 1)
                for c in range(CT):
                    pe.transpose(ps[0:PAD, 6, c * P:(c + 1) * P], uext[:, c, SEQ:SEQ + PAD], eye)
                for c in range(CT):
                    last = pe.transpose(ps[0:NS, 7, c * P:(c + 1) * P], cst_u[:, c, :], eye)
                last.then_inc(u_ps, 1)

            def rotate(m):
                if m == 0:
                    pe.wait_ge(tile_free, 2 + 26)
                if m >= 2:
                    pe.wait_ge(rot_used, m - 1)
                for half in range(2):
                    last = pe.matmul(ps[:, 2 + 2 * (m % 2) + half, 0:HALF], rot, zqkv[:, m, half * HALF:(half + 1) * HALF],
                                     start=True, stop=True)
                last.then_inc(rot_ps, 1)

            def values_rows(m):
                if m == 0:
                    pe.wait_ge(rotated, 12)
                if m >= 3:
                    pe.wait_ge(v_sb, m - 2)
                for r in range(4):
                    src = zqkv[:, V0 + m, r * P:(r + 1) * P] if m < 2 else zqkv[:, V0 + m, r:SEQ:4]
                    last = pe.transpose(ps[:, 2 + m % 3, r * P:(r + 1) * P], src, eye)
                last.then_inc(v_ps, 1)

            def sample_rows(_):
                pe.wait_ge(v_sb, 6)
                for m in range(12):
                    last = pe.transpose(ps[0:NS, 2 + m // 4, (m % 4) * P:(m % 4) * P + P], zqkv[:, K0 + m, SEQ:N], eye)
                last.then_inc(s_ps, 1)

            def key_rows(m):
                if m == 0:
                    pe.wait_ge(u_sb, 1)
                if m >= 2:
                    pe.wait_ge(k_sb, m - 1)
                for r in range(4):
                    if m < 2 and r < 3:
                        continue
                    src = zqkv[:, K0 + m, r * P:(r + 1) * P] if m < 2 else zqkv[:, K0 + m, r:SEQ:4]
                    last = pe.transpose(ps[:, 6 + m % 2, r * P:(r + 1) * P], src, eye)
                last.then_inc(k_ps, 1)

            def cached_scores(b):
                pe.wait_ge(kt_dve, b + 1)
                pe.wait_ge(kt_act, b + 1)
                for hp in range(2):
                    for tile in range(6):
                        g = (0, 1, 1, 1, 1, 2)[tile]
                        q = qbd[:, 2 * g + hp, b * NT:(b + 1) * NT, :].rearrange("p t j -> p (t j)")
                        c0 = g * P + hp * 64 + b * 8
                        if g == 1:
                            t = tile - 1
                            q, c0, w = q[:, 2 * t:2 * t + 2], c0 + 2 * t, 2
                        else:
                            w = 8
                        last = pe.matmul(ps[:, 5, c0:c0 + w], ktr[:, b % 2, tile * 2 + hp, :], q, start=True, stop=True)
                last.then_inc(st_ps, 1)

            def cached_keys(b):
                if b == 0:
                    pe.wait_ge(s_sb, 1)
                    pe.wait_ge(qbd_set, 1)
                else:
                    pe.wait_ge(kt_dve, b)
                    pe.wait_ge(kt_act, b)
                pe.wait_ge(kc_loaded[b % 2], 48 * (b // 2 + 1))
                for tile in range(6):
                    for hp in range(2):
                        m = tile * 2 + hp
                        last = pe.transpose(ps[:, 2 + m // 4, (m % 4) * P:(m % 4 + 1) * P],
                                            kc[:, b % 2, tile, hp * P:(hp + 1) * P], eye)
                last.then_inc(kt_ps, 1)
                if b >= 1:
                    cached_scores(b - 1)

            def new_keys(_):
                cached_scores(NB - 1)
                pe.wait_ge(k_sb, 6)
                for m in range(6):
                    last = pe.matmul(ps[0:NS, 6, m * 64:(m + 1) * 64], zqkv[:, K0 + m, SEQ:N],
                                     qbd[:, m, :, :].rearrange("p b j -> p (b j)"), start=True, stop=True)
                last.then_inc(st_ps, 1)

            def conv_mean(_):
                pe.wait_ge(conv_done, 1)
                for half in range(2):
                    for c in range(CT):
                        last = pe.matmul(ps[:, 2 + half, 0:HALF], onesm, acc[:, c, half * HALF:(half + 1) * HALF],
                                         start=c == 0, stop=c == CT - 1)
                last.then_inc(mean_ps, 1)

            def conv_var(_):
                pe.wait_ge(sq_sb, 1)
                for half in range(2):
                    for c in range(CT):
                        last = pe.matmul(ps[:, 2 + half, 0:HALF], onesm, acc[:, c, half * HALF:(half + 1) * HALF],
                                         start=c == 0, stop=c == CT - 1)
                last.then_inc(var_ps, 1)

            def sample_turn(_):
                pe.wait_ge(st_done, 2)
                for g in range(3):
                    pe.transpose(ps[:, 4, g * P:(g + 1) * P], st_sb[:, g * P:(g + 1) * P], eye)
                for g in range(3):
                    last = pe.transpose(ps[:, 4, 3 * P + g * NS:3 * P + (g + 1) * NS], stn_sb[0:NS, g * P:(g + 1) * P], eye[0:NS, 0:NS])
                last.then_inc(sback_ps, 1)

            def sample_probs(_):
                pe.wait_ge(spn, 1)
                for g in range(3):
                    pe.transpose(ps[:, 5, g * P:(g + 1) * P], sp[:, g * P:(g + 1) * P], eye)
                for g in range(3):
                    last = pe.transpose(ps[0:NS, 4, g * P:(g + 1) * P], sp[:, 3 * P + g * NS:3 * P + (g + 1) * NS], eye)
                last.then_inc(spt_ps, 1)

            def cached_values(b):
                if b == 0:
                    pe.wait_ge(spt_sb, 2)
                    for hp in range(2):
                        for g in range(3):
                            pe.matmul(ps[:, 6 + hp, 0:64], skv[0:NS, g, 1, hp * P:(hp + 1) * P],
                                      stn_sb[0:NS, g * P + hp * 64:g * P + hp * 64 + 64], start=g == 0, stop=False,
                                      skip_group_check=True)
                pe.wait_ge(vc_loaded[b % 2], 48 * (b // 2 + 1))
                for hp in range(2):
                    for tile in range(6):
                        g = (0, 1, 1, 1, 1, 2)[tile]
                        o0, w = (b * 8, 8) if g != 1 else (b * 8 + 2 * (tile - 1), 2)
                        last = pe.matmul(ps[:, 6 + hp, o0:o0 + w], vc[:, b % 2, tile, hp * P:(hp + 1) * P],
                                         st_sb[:, g * P + hp * 64 + o0:g * P + hp * 64 + o0 + w],
                                         start=False, stop=b == NB - 1, skip_group_check=True)
                last.then_inc(vs_used if b < NB - 1 else so_ps, 1)

            def scores(i):
                r, h = divmod(i, HEADS)
                p0, hp = 64 * (h % 2), h // 2
                if i == 0:
                    pe.wait_ge(cnorm, 1)
                else:
                    pe.wait_ge(pmax, i)
                for g in range(3):
                    q = zqkv[p0:p0 + 64, Q0 + 2 * g + hp, r:SEQ:4]
                    if g == 0:
                        pe.matmul(ps[:, 2, :], q, zqkv[p0:p0 + 64, K0 + hp, 0:SEQ], start=True, stop=True)
                    else:
                        last = pe.matmul(ps[:, 3, (g - 1) * P:g * P], q,
                                         zqkv[p0:p0 + 64, K0 + 2 * g + hp, r:SEQ:4], start=True, stop=True)
                last.then_inc(qk_ps, 1)

            def turn(i):
                pe.wait_ge(pexp, i + 1)
                if i >= 1:
                    pe.wait_ge(pt_dve, i)
                    pe.wait_ge(pt_act, i)
                for c in range(6):
                    last = pe.transpose(ps[:, 4 + c // 4, (c % 4) * P:(c % 4 + 1) * P], prob[:, i % 2, c * P:(c + 1) * P], eye)
                last.then_inc(pt_ps, 1)

            def weigh(i):
                r, h = divmod(i, HEADS)
                if i == 0:
                    pe.wait_ge(so_sb, 1)
                pe.wait_ge(pt_dve, i + 1)
                pe.wait_ge(pt_act, i + 1)
                if h == 0 and r >= 2:
                    pe.wait_ge(at_sb, r - 1)
                for c in range(6):
                    kb, col = (c, h * HD) if c < 4 else (r, (c - 3) * 256 + h * HD)
                    last = pe.matmul(ps[:, 6 + r % 2, h * HD:(h + 1) * HD], prt[:, i % 2, c, :], vt[:, kb, col:col + HD],
                                     start=c == 0, stop=c == 5)
                last.then_inc(pv_ps, 1)

            def turn_out(r):
                pe.wait_ge(otok, r + 1)
                for hp in range(2):
                    last = pe.transpose(ps[:, 6 + r % 2, 256 + hp * P:256 + (hp + 1) * P], atk[:, hp * P:(hp + 1) * P], eye)
                last.then_inc(at_ps, 1)

            def attend(i):
                if i < 16:
                    scores(i)
                if 1 <= i <= 16:
                    turn(i - 1)
                if i >= 2:
                    weigh(i - 2)
                    if (i - 2) % 4 == 0 and i - 2 >= 4:
                        turn_out((i - 2) // 4 - 1)

            work = dict(conv_rows=conv_rows, rotate=rotate, values=values_rows, sample_rows=sample_rows, keys=key_rows,
                        cached_keys=cached_keys, new_keys=new_keys, conv_mean=conv_mean, conv_var=conv_var,
                        sample_turn=sample_turn, sample_probs=sample_probs, cached_values=cached_values, attend=attend)
            for kind, i, quarters in steps:
                for q in quarters:
                    gate_quarter(q)
                work[kind](i)
            turn_out(3)

            pe.wait_ge(cact, CT)
            pe.wait_ge(gate_free, 32)
            pe.wait_ge(at_sb, 4)
            pe.wait_ge(wco_loaded, 16)
            pe.wait_ge(wa_loaded, 16)
            for m in range(KD):
                s = 4 * (m % 2)
                if m >= 2:
                    pe.wait_ge(br_used, m - 1)
                for half in range(2):
                    cols = slice(half * HALF, (half + 1) * HALF)
                    for k in range(CT):
                        pe.matmul(ps[:, s + half, 0:HALF], wco[:, k, m * P:(m + 1) * P], acc[:, k, cols], start=k == 0, stop=k == CT - 1)
                    for k in range(2):
                        last = pe.matmul(ps[:, s + 2 + half, 0:HALF], wa[:, k, m * P:(m + 1) * P], at[:, k, cols], start=k == 0, stop=k == 1)
                last.then_inc(br_ps, 1)
            pe.wait_ge(w_split, SPLIT + 4)
            pe.wait_ge(x_split, 1 + KD)
            pe.wait_ge(wr_loaded, 32)

            def router(t):
                c0, n = TILES[t]
                pe.wait_ge(hdone, t + 1)
                if t >= 1:
                    pe.wait_ge(ht_sb, t)
                for k in range(KD):
                    last = pe.transpose(ps[:, 4 + k // 4, (k % 4) * P:(k % 4) * P + n], hrow[0:n, t % 2, k * P:(k + 1) * P], eye[0:n, 0:n])
                last.then_inc(ht_ps, 1)
                pe.wait_ge(ht_sb, t + 1)
                if t >= 2:
                    pe.wait_ge(lg_sb, t - 1)
                for k in range(KD):
                    last = pe.matmul(ps[0:n, 6 + t % 2, 0:36], hcol[:, k, 0:n], wrv[:, k, :], start=k == 0, stop=k == KD - 1)
                last.then_inc(lg_ps, 1)

            for t, (c0, n) in enumerate(TILES):
                if t >= 2:
                    pe.wait_ge(y_used, t - 1)
                for half in range(2):
                    out, cols = ps[0:n, 2 * (t % 2) + half, :], slice(half * 512, (half + 1) * 512)
                    for k in range(KD):
                        pe.matmul(out, ga_hi[:, k, c0:c0 + n], wo_hi[:, k, cols], start=k == 0, stop=False)
                        pe.matmul(out, ga_hi[:, k, c0:c0 + n], wo_lo[:, k, cols], start=False, stop=False)
                        last = pe.matmul(out, ga_lo[:, k, c0:c0 + n], wo_hi[:, k, cols], start=False, stop=k == KD - 1)
                last.then_inc(y_ps, 1)
                if t >= 1:
                    router(t - 1)
            router(NTT - 1)
            pe.wait_ge(mset, 1)
            for t, (c0, n) in enumerate(TILES):
                for u in range(t):
                    pe.matmul(ps[0:n, 0, t * NE:(t + 1) * NE], onesb[0:P, 0:n], mb[:, u, :], start=u == 0, stop=False)
                pe.matmul(ps[0:n, 0, t * NE:(t + 1) * NE], beforeb[0:n, 0:n], mb[0:n, t, :], start=t == 0, stop=True)
            for t, (c0, n) in enumerate(TILES):
                last = pe.matmul(ps[:, 1, 0:NE], onesb[0:n, :], mb[0:n, t, :], start=t == 0, stop=t == NTT - 1)
            last.then_inc(cnt_ps, 1)
            pe.wait_ge(sel_set, 1)
            for i in range(2 * NTT):
                n = TILES[i // 2][1]
                last = pe.matmul(ps[0:BLK, 2, 0:NBLK], ohr[0:n, i, :], ohb[0:n, i, :], start=i == 0, stop=i == 2 * NTT - 1)
            last.then_inc(idx_ps, 1)

            def turn_rows(src):
                for k in range(KD):
                    last = pe.transpose(ps[:, k // 4, (k % 4) * P:(k % 4) * P + BLK], src[:, k:D:KD], eye[0:BLK, 0:BLK])
                return last

            pe.wait_ge(idx_set, 1)
            pe.wait_ge(gathered[0], 16)
            turn_rows(xg[0]).then_inc(xgt_ps, 1)

            def expert(i, s):
                e, nxt = SLOTS * i + s, (s + 1) % SLOTS
                pe.wait_ge(e_loaded[0][s], 32 * i + 32)
                pe.wait_ge(xgt_sb, e + 1)
                for f in range(KF):
                    pe.wait_ge(hact_sb, e * KF + f + 1)
                    for w, bank in ((wgv[s], 2 + f % 2), (wuv[s], 4 + f % 2)):
                        for k in range(KD):
                            last = pe.matmul(ps[:, bank, 0:BLK], w[:, k, f, :], xgt[s][:, k, :], start=k == 0, stop=k == KD - 1)
                    last.then_inc(gu_ps, 1)
                if not (isinstance(i, int) and e == NE - 1):
                    pe.wait_ge(gathered[nxt], 16 * i + 16 + 16 * (nxt == 0))
                    turn_rows(xg[nxt]).then_inc(xgt_ps, 1)
                pe.wait_ge(e_loaded[1][s], 16 * i + 16)
                pe.wait_ge(hact_sb, e * KF + KF + 2)
                pe.wait_ge(yo_sb, e + 1)
                for half in range(2):
                    for k in range(KF):
                        last = pe.matmul(ps[0:BLK, 6 + half, :], hact[:, k, :], wdv[s][:, k, half * 512:(half + 1) * 512],
                                         start=k == 0, stop=k == KF - 1)
                last.then_inc(dn_ps, 1)

            with pe.Fori(0, ROUNDS) as i:
                for s in range(SLOTS):
                    expert(i, s)
            for s in range(NE % SLOTS):
                expert(ROUNDS, s)
            pe.wait_ge(over_set, 1)
            count = pe.value_load(over_i[0:1, OVER:OVER + 1], min_val=0, max_val=OVER)
            with pe.If(count > 0):
                pe.wait_ge(yo_sb, NE + 1)
                pe.wait_ge(xgt_sb, NE)
                with pe.Fori(0, count) as i:
                    pe.wait_ge(ov["gat"], 16 * i + 16)
                    pe.wait_ge(ov["load"], 48 * i + 48)
                    turn_rows(xg[0]).then_inc(ov["tps"], 1)
                    pe.wait_ge(ov["tsb"], i + 1)
                    for f in range(KF):
                        for w, bank in ((wgv[0], 2), (wuv[0], 4)):
                            for k in range(KD):
                                last = pe.matmul(ps[:, bank, 0:BLK], w[:, k, f, :], xgt[0][:, k, :], start=k == 0, stop=k == KD - 1)
                        last.then_inc(ov["gu"], 1)
                        pe.wait_ge(ov["ha"], KF * i + f + 1)
                    for half in range(2):
                        for k in range(KF):
                            last = pe.matmul(ps[0:BLK, 6 + half, :], hact[:, k, :], wdv[0][:, k, half * 512:(half + 1) * 512],
                                             start=k == 0, stop=k == KF - 1)
                    last.then_inc(ov["dn"], 1)

        @block.scalar
        def _(ac):
            ac.dma_start(ci[:, :], const[:, C_EYE:C_PM]).then_inc(ci_loaded, 16)
            ac.dma_start(vt_t[0:42, 0:P], a["b_in"][0].rearrange("(m c) -> m c", c=P)).then_inc(rows_loaded, 16)
            for name, r0, r1 in (("b_dw", 42, 46), ("conv_ln_g", 46, 50), ("conv_ln_b", 50, 54), ("b_conv_out", 54, 62)):
                ac.dma_start(vt_t[r0:r1, 0:P], a[name][0].rearrange("(m c) -> m c", c=P)).then_inc(rows_loaded, 16)
            ac.dma_start(rows_b, a["w_dw"][0].rearrange("t (m c) -> (t m) c", c=P)).then_inc(rows_loaded, 16)
            ac.dma_start(trig, const[:, C_COS:C_COS + 2 * N]).then_inc(trig_loaded, 16)
            for j in range(2):
                ac.dma_start(cst[:, j, :], a["state_conv"][0, 4 * j:4 * j + 4].rearrange("b s c -> (b s) c")).then_inc(state_loaded, 16)
            ac.dma_start(pmask, const[:, C_PM:C_SM]).then_inc(mask_loaded, 16)
            ac.dma_start(smask, const[:, C_SM:C_END]).then_inc(mask_loaded, 16)
            ac.dma_start(br[:, 0:4], a["b_router_group"][0].partition_broadcast(P)).then_inc(br_loaded, 16)
            ac.dma_start(br[:, 4:36], a["b_router_expert"][0].partition_broadcast(P)).then_inc(br_loaded, 16)
            ac.sem_inc(tile_free, 2)
            ac.wait_ge(xt_sb, NTT)
            ac.copy(x_hi, xt).then_inc(x_high, 1)
            ac.wait_ge(colb_sb, 2)

            def evacuate(n, c, dst, bias, func):
                ac.wait_ge(tile_mm, n + 1)
                ac.activation(dst.rearrange("p (h n) -> p h n", h=2), ps[:, 2 * c:2 * c + 2, 0:HALF], func, bias=bias).then_inc(tile_free, 1)

            def high(s, c, first_use):
                if c == 0:
                    ac.wait_ge(win_loaded[s], first_use)
                tile = slice(c * P, (c + 1) * P)
                ac.copy(w_hi[:, s, :, tile], wring[:, s, :, tile]).then_inc(w_high, 1)

            for n in range(8):
                evacuate(n, n % 2, zr[:, n, :], colb[:, UA0 + n:UA0 + n + 1], ACT.Identity if n < CT else ACT.Sigmoid)
                if n % 2 == 0 and n >= 2:
                    j = n // 2 + 1
                    for c in range(2):
                        high(j % 2, c, 16 * (j // 2 + 1))
            with ac.Fori(0, 4) as i:
                for j in range(4):
                    evacuate(8 + 4 * i + j, j % 2, ea[:, bass.ds((4 * i + j) * N, N)], colb[:, bass.ds(4 * i + j, 1)], ACT.Identity)
                    if j % 2 == 0:
                        for c in range(2):
                            high((j // 2 + 1) % 2, c, 16 * i + 16 * (3 + j // 2))
            for n in (24, 25):
                evacuate(n, n % 2, zqkv[:, n - 8, :], colb[:, n - 8:n - 7], ACT.Identity)

            def gate_unit(u):
                t, half = divmod(u, 2)
                ac.wait_ge(gate_mm, u + 1)
                ac.activation(zr[:, 8 + t, half * HALF:(half + 1) * HALF], ps[:, half, 0:HALF], ACT.Identity,
                              bias=colb[:, G0 + t:G0 + t + 1]).then_inc(gate_free, 1)

            def conv_rows(_):
                ac.wait_ge(u_ps, 1)
                ac.copy(urow_p[0:PAD, :], ps[0:PAD, 6, :])
                ac.copy(urow_s[0:NS, :], ps[0:NS, 7, :]).then_inc(u_sb, 1)

            def key_rows(m):
                ac.wait_ge(k_ps, m + 1)
                if m >= 2:
                    ac.wait_ge(krow_stored[m % 2], 16 * (m // 2))
                g, c0 = m // 2, (m % 2) * 2
                if m < 2:
                    ac.copy(krow[:, m % 2, 0, :], ps[:, 6 + m % 2, 3 * P:4 * P]).then_inc(k_sb, 1)
                    dst, src = kv0p[0, 0, :, 0, c0:c0 + 2].rearrange("s h e -> s (h e)"), krow[:, m % 2, 0, :]
                else:
                    ac.copy(krow[:, m % 2], ps[:, 6 + m % 2, :].rearrange("p (r c) -> p r c", r=4)).then_inc(k_sb, 1)
                    dst = (kv1p, kv2p)[g - 1][0, 0].rearrange("(p r) two h e -> p r two (h e)", r=4)[:, :, 0, c0 * HD:c0 * HD + P]
                    src = krow[:, m % 2]
                ac.wait_ge(k_sb, m + 1)
                ac.dma_start(dst, src).then_inc(krow_stored[m % 2], 16)

            def sample_rows(_):
                ac.wait_ge(s_ps, 1)
                for two in range(2):
                    for g in range(3):
                        m = 6 * two + 2 * g
                        last = ac.copy(skv[0:NS, g, two, :], ps[0:NS, 2 + m // 4, (m % 4) * P:(m % 4) * P + 256])
                last.then_inc(s_sb, 1)

            def cached_keys(b):
                ac.wait_ge(kt_ps, b + 1)
                if b == 0:
                    ac.wait_ge(conv_done, 1)
                if b >= 2:
                    ac.wait_ge(st_ps, b - 1)
                ac.copy(ktr[:, b % 2, 8:12, :], ps[:, 4, :].rearrange("p (m k) -> p m k", m=4)).then_inc(kt_act, 1)

            def sample_turn(_):
                ac.wait_ge(smax, 1)
                ac.activation(sp, sp, ACT.Exp, bias=nmx_s, scale=SCALE, accum_out=l_s).then_inc(sprob, 1)

            def conv_mean(_):
                ac.wait_ge(cen_sb, 2)
                ac.activation(acc, cen, ACT.Square).then_inc(sq_sb, 1)

            def conv_var(_):
                ac.wait_ge(veps, 1)
                ac.activation(rstd_c, rstd_c, ACT.Sqrt).then_inc(csd, 1)
                ac.wait_ge(cnorm, 1)
                for c in range(CT):
                    ac.activation(acc[:, c, :], cen[:, c, :], ACT.Silu, bias=clb_c[:, c:c + 1], scale=clg_c[:, c:c + 1]).then_inc(cact, 1)

            def attend(i):
                if i < 16:
                    ac.wait_ge(pmax, i + 1)
                    ac.activation(prob[:, i % 2, :], prob[:, i % 2, :], ACT.Exp, bias=nmx_p[:, i:i + 1], scale=SCALE,
                                  accum_out=l_p[:, i:i + 1]).then_inc(pexp, 1)
                if 1 <= i <= 16:
                    j = i - 1
                    ac.wait_ge(pt_ps, j + 1)
                    if j >= 2:
                        ac.wait_ge(pv_ps, j - 1)
                    ac.copy(prt[:, j % 2, 4:6, :], ps[:, 5, 0:256].rearrange("p (m k) -> p m k", m=2)).then_inc(pt_act, 1)

            work = dict(conv_rows=conv_rows, sample_rows=sample_rows, keys=key_rows, cached_keys=cached_keys,
                        sample_turn=sample_turn, conv_mean=conv_mean, conv_var=conv_var, attend=attend)
            for kind, i, quarters in steps:
                for q in quarters:
                    if q % 2 == 1:
                        gate_unit(q // 2)
                if kind in work:
                    work[kind](i)
            ac.wait_ge(gate_free, 32)
            for m in range(KD):
                ac.activation(zr[:, 8 + m:24:8, :], zr[:, 8 + m:24:8, :], ACT.Sigmoid).then_inc(gate_sig, 1)
            ac.wait_ge(at_sb, 4)
            ac.wait_ge(wo_loaded, 16)
            for j in range(4):
                ac.copy(wo_hi[:, 2 * j:2 * j + 2, :], wo[:, 2 * j:2 * j + 2, :]).then_inc(w_high, 1)
            for m in range(KD):
                ac.wait_ge(merged, m + 1)
                ac.copy(ga_hi[:, m, :], ga[:, m, :]).then_inc(x_high, 1)
            def columns_out(t):
                c1, n1 = TILES[t]
                ac.wait_ge(ht_ps, t + 1)
                if t >= 1:
                    ac.wait_ge(lg_ps, t)
                ac.copy(hcol[:, :, 0:n1], ps[:, 4:6, :].rearrange("p b (k c) -> p (b k) c", k=4)[:, :, 0:n1]).then_inc(ht_sb, 1)

            for t, (c0, n) in enumerate(TILES):
                s = t % 2
                ac.wait_ge(hvar, t + 1)
                ac.activation(sd[s][0:n], var_e[s][0:n], ACT.Sqrt).then_inc(hsd, 1)
                ac.wait_ge(hscale, t + 1)
                ac.activation(hrow[0:n, s, :], hrow[0:n, s, :], ACT.Identity, bias=nmr[s][0:n], scale=rs[s][0:n]).then_inc(hnorm, 1)
                columns_out(t)
            ac.wait_ge(rmax, 1)
            ac.activation(rt_g3, rt_g3, ACT.Exp).then_inc(rexp, 1)
            ac.wait_ge(rmax, 2)
            ac.activation(rt_d, rt_d, ACT.Exp).then_inc(rexp, 1)
            ac.sem_inc(yo_sb, 1)

            def expert(i, s):
                e = SLOTS * i + s
                for f in range(KF):
                    ac.wait_ge(gu_ps, e * KF + f + 1)
                    ac.wait_ge(hact_sb, e * KF + f + 1)
                    ac.activation(gact[:, f, :], ps[:, 2 + f % 2, 0:BLK], ACT.Silu).then_inc(gact_sb, 1)
                ac.wait_ge(dn_ps, e + 1)
                if not isinstance(i, int) or i > 0:
                    ac.wait_ge(scattered[s], 16 * i)
                ac.copy(yo[s].rearrange("p (h n) -> p h n", h=2), ps[0:BLK, 6:8, :]).then_inc(yo_sb, 1)

            for s in range(SLOTS):
                expert(0, s)
            with ac.Fori(1, ROUNDS) as i:
                for s in range(SLOTS):
                    expert(i, s)
            for s in range(NE % SLOTS):
                expert(ROUNDS, s)
            ac.wait_ge(idx_set, 1)
            ac.wait_ge(over_set, 1)
            count = ac.value_load(over_i[0:1, OVER:OVER + 1], min_val=0, max_val=OVER)
            with ac.If(count > 0):
                with ac.Fori(0, count) as i:
                    for f in range(KF):
                        ac.wait_ge(ov["gu"], KF * i + f + 1)
                        ac.activation(gact[:, f, :], ps[:, 2, 0:BLK], ACT.Silu).then_inc(ov["ga"], 1)
                    ac.wait_ge(ov["dn"], i + 1)
                    ac.copy(yo[0].rearrange("p (h n) -> p h n", h=2), ps[0:BLK, 6:8, :]).then_inc(ov["yo"], 1)
            def weigh(t):
                n = TILES[t][1]
                ac.wait_ge(fin_loaded[t % 2], 32 * (t // 2 + 1))
                ac.activation(fy1[t % 2][0:n], fy1[t % 2][0:n], ACT.Identity, scale=gw[0:n, 0, t:t + 1]).then_inc(fweigh, 1)

            weigh(0)
            for t, (c0, n) in enumerate(TILES):
                s = t % 2
                if t + 1 < NTT:
                    weigh(t + 1)
                if t == 0:
                    ac.wait_ge(rows2_loaded, 16 * 7)
                ac.wait_ge(hvar, NTT + t + 1)
                ac.activation(sd[s][0:n], var_e[s][0:n], ACT.Sqrt).then_inc(hsd, 1)
                ac.wait_ge(hscale, NTT + t + 1)
                ac.activation(fh[t][0:n], fh[t][0:n], ACT.Identity, bias=nmr[s][0:n], scale=rs[s][0:n]).then_inc(hnorm, 1)

        @block.vector
        def _(ve):
            chain = [0]

            def link(ins):
                chain[0] += 1
                ins.then_inc(dve_chain, 1)
                ve.wait_ge(dve_chain, chain[0])

            for t, (c0, n) in enumerate(TILES):
                ve.wait_ge(xt_ps, t + 1)
                src = ps[:, 4 + 2 * (t % 2):6 + 2 * (t % 2), :].rearrange("p b (k c) -> p (b k) c", k=4)
                ve.tensor_copy(xt[:, :, c0:c0 + n], src[:, :, 0:n]).then_inc(xt_sb, 1)
            ve.wait_ge(colb_ps, 1)
            ve.tensor_copy(colb[:, 0:62], ps[:, 6, 0:62]).then_inc(colb_sb, 1)
            ve.tensor_copy(wdw_c, ps[:, 6, 64:64 + TAPS * CT]).then_inc(colb_sb, 1)
            ve.wait_ge(state_ps, 1)
            for j in range(2):
                for c in range(CT):
                    last = ve.tensor_copy(sext[:, c, 4 * j:4 * j + 4, 0:PAD],
                                          ps[:, 4 + j, c * P:c * P + 4 * PAD].rearrange("p (b s) -> p b s", b=4))
            last.then_inc(state_sb, 1)
            ve.wait_ge(x_high, 1)
            ve.tensor_tensor(x_lo, xt, x_hi.bitcast(F32), ALU.subtract).then_inc(x_split, 1)
            ve.wait_ge(pads_set, 1)
            ve.wait_ge(tile_free, 2 + 8)
            ve.tensor_tensor(uext[:, :, PAD:PAD + SEQ], ua[:, :, 0:SEQ], ub[:, :, 0:SEQ], ALU.mult)
            for c in range(CT):
                ve.tensor_tensor(sext[:, c, :, PAD:PAD + NT], ua[:, c, SEQ:N].rearrange("p (b t) -> p b t", t=NT),
                                 ub[:, c, SEQ:N].rearrange("p (b t) -> p b t", t=NT), ALU.mult)
            link(ve.tensor_tensor(cst_u, ua[:, :, SEQ:N], ub[:, :, SEQ:N], ALU.mult))
            ve.nop().then_inc(u_set, 1)

            def conv_parts():
                for c in range(CT):
                    yield c, acc[:, c, 0:SEQ], lambda k, c=c: uext[:, c, bass.ds(k, SEQ)] if not isinstance(k, int) else uext[:, c, k:k + SEQ]
                for c in range(CT):
                    yield (c, acc[:, c, SEQ:N].rearrange("p (b t) -> p b t", t=NT),
                           lambda k, c=c: sext[:, c, :, bass.ds(k, NT)] if not isinstance(k, int) else sext[:, c, :, k:k + NT])

            for c, dst, win in conv_parts():
                ve.tensor_scalar(dst, win(0), wdw_c[:, c:c + 1], bdw_c[:, c:c + 1], ALU.mult, ALU.add).then_inc(conv_step, 1)
            with ve.Fori(1, TAPS) as k:
                for j, (c, dst, win) in enumerate(conv_parts()):
                    ve.wait_ge(conv_step, 8 * k + j - 7)
                    ve.scalar_tensor_tensor(dst, win(k), wdw_c[:, bass.ds(k * CT + c, 1)], dst, ALU.mult, ALU.add).then_inc(conv_step, 1)
            ve.wait_ge(conv_step, 8 * TAPS)
            ve.nop().then_inc(conv_done, 1)
            v2 = lambda t: t.rearrange("p (h n) -> p h n", h=2)

            def rotate(m):
                if m == 0:
                    ve.wait_ge(trig_loaded, 16)
                ve.wait_ge(rot_ps, m + 1)
                ve.tensor_tensor(v2(rtmp[:, m % 2, :]), ps[:, 2 + 2 * (m % 2):4 + 2 * (m % 2), 0:HALF], v2(sin), ALU.mult).then_inc(rot_used, 1)
                link(ve.tensor_tensor(zqkv[:, m, :], zqkv[:, m, :], cos, ALU.mult))
                ve.wait_ge(rot_used, m + 1)
                ve.tensor_tensor(zqkv[:, m, :], zqkv[:, m, :], rtmp[:, m % 2, :], ALU.add).then_inc(rotated, 1)

            def value_rows(m):
                ve.wait_ge(v_ps, m + 1)
                ve.tensor_copy(vt[:, :, m * P:(m + 1) * P], ps[:, 2 + m % 3, :].rearrange("p (r c) -> p r c", r=4)).then_inc(v_sb, 1)

            def sample_queries(_):
                ve.wait_ge(qbd_zero, 1)
                for hh in range(2):
                    rows = slice(64 * hh, 64 * hh + 64)
                    last = ve.tensor_copy(qbd[rows, :, :, hh], zqkv[rows, Q0:Q0 + 6, SEQ:N])
                last.then_inc(qbd_set, 1)

            def cached_keys(b):
                if b == 0:
                    ve.wait_ge(u_ps, 1)
                ve.wait_ge(kt_ps, b + 1)
                if b >= 2:
                    ve.wait_ge(st_ps, b - 1)
                ve.tensor_copy(ktr[:, b % 2, 0:8, :], ps[:, 2:4, :].rearrange("p b (m k) -> p (b m) k", m=4)).then_inc(kt_dve, 1)

            def new_keys(_):
                ve.wait_ge(st_ps, NB + 1)
                ve.tensor_copy(st_sb, ps[:, 5, 0:3 * P]).then_inc(st_done, 1)
                ve.tensor_copy(stn_sb[0:NS, :], ps[0:NS, 6, 0:3 * P]).then_inc(st_done, 1)

            def sample_turn(_):
                ve.wait_ge(sback_ps, 1)
                ve.wait_ge(mask_loaded, 32)
                link(ve.tensor_tensor_reduce(sp, ps[:, 4, 0:SKEYS], smask, 1.0, -3e38, ALU.add, ALU.max, nmx_s))
                ve.tensor_scalar(nmx_s, nmx_s, -SCALE, None, ALU.mult).then_inc(smax, 1)
                ve.wait_ge(sprob, 1)
                link(ve.reciprocal(rinv_s, l_s))
                ve.tensor_scalar(sp, sp, rinv_s, None, ALU.mult).then_inc(spn, 1)

            def sample_probs(_):
                ve.wait_ge(spt_ps, 1)
                ve.tensor_copy(st_sb, ps[:, 5, 0:3 * P]).then_inc(spt_sb, 1)
                ve.tensor_copy(stn_sb[0:NS, :], ps[0:NS, 4, 0:3 * P]).then_inc(spt_sb, 1)

            def cached_values(b):
                if b < NB - 1:
                    return
                ve.wait_ge(so_ps, 1)
                for hh in range(2):
                    rows = slice(64 * hh, 64 * hh + 64)
                    last = ve.tensor_copy(at[rows, :, SEQ:N], ps[rows, 6:8, 0:64].rearrange("p h (b j) -> p h b j", j=2)[:, :, :, hh])
                last.then_inc(so_sb, 1)

            def conv_mean(_):
                ve.wait_ge(mean_ps, 1)
                ve.wait_ge(stored, 16 * STORES)
                for s in range(2):
                    ve.wait_ge(krow_stored[s], 16 * 3)
                for half in range(2):
                    cols = slice(half * HALF, (half + 1) * HALF)
                    ve.tensor_tensor(cen[:, :, cols], acc[:, :, cols], ps[:, 2 + half, 0:HALF].unsqueeze(1).broadcast_to([P, CT, HALF]),
                                     ALU.subtract).then_inc(cen_sb, 1)

            def conv_var(_):
                ve.wait_ge(var_ps, 1)
                ve.tensor_scalar(rstd_c, rstd_c, EPS, None, ALU.add).then_inc(veps, 1)
                ve.wait_ge(csd, 1)
                link(ve.reciprocal(rstd_c, rstd_c))
                ve.wait_ge(cen_sb, 2)
                ve.tensor_tensor(cen.rearrange("p c (h n) -> p c h n", h=2), cen.rearrange("p c (h n) -> p c h n", h=2),
                                 rstd_c.unsqueeze(1).broadcast_to([P, CT, 2, HALF]), ALU.mult).then_inc(cnorm, 1)

            def mask_max(i):
                r, s = i // 4, i % 2
                ve.wait_ge(qk_ps, i + 1)
                if i >= 2:
                    ve.wait_ge(pt_ps, i - 1)
                sv = ps[:, 2:4, :].rearrange("p b k -> p (b k)")
                link(ve.tensor_tensor_reduce(prob[:, s, 0:SEQ], sv[:, 0:SEQ], pmask[:, r * SEQ:(r + 1) * SEQ], 1.0, -3e38,
                                             ALU.add, ALU.max, pmx[:, 0:1]))
                link(ve.tensor_tensor_reduce(prob[:, s, SEQ:PKEYS], sv[:, SEQ:PKEYS], pmask[:, 4 * SEQ:4 * SEQ + 2 * P], 1.0, pmx[:, 0:1],
                                             ALU.add, ALU.max, pmx[:, 1:2]))
                ve.tensor_scalar(nmx_p[:, i:i + 1], pmx[:, 1:2], -SCALE, None, ALU.mult).then_inc(pmax, 1)

            def divide(q):
                ve.wait_ge(pv_ps, 4 * q + 4)
                link(ve.reciprocal(rinv, l_p[:, 4 * q:4 * q + 4]))
                ve.tensor_tensor(atk.rearrange("p (h e) -> p h e", h=4), ps[:, 6 + q % 2, 0:256].rearrange("p (h e) -> p h e", h=4),
                                 rinv.unsqueeze(2).to_broadcast([P, 4, HD]), ALU.mult).then_inc(otok, 1)

            def columns(q):
                ve.wait_ge(at_ps, q + 1)
                ve.tensor_copy(at[:, :, q:SEQ:4], ps[:, 6 + q % 2, 256:512].rearrange("p (m k) -> p m k", m=2)).then_inc(at_sb, 1)

            def attend(i):
                if i < 16:
                    mask_max(i)
                if 1 <= i <= 16:
                    j = i - 1
                    ve.wait_ge(pt_ps, j + 1)
                    if j >= 2:
                        ve.wait_ge(pv_ps, j - 1)
                    ve.tensor_copy(prt[:, j % 2, 0:4, :], ps[:, 4, :].rearrange("p (m k) -> p m k", m=4)).then_inc(pt_dve, 1)
                if i in (6, 10, 14):
                    divide((i - 6) // 4)
                if i in (8, 12):
                    columns(i // 4 - 2)

            work = dict(rotate=rotate, values=value_rows, sample_rows=sample_queries, cached_keys=cached_keys, new_keys=new_keys,
                        sample_turn=sample_turn, sample_probs=sample_probs, cached_values=cached_values,
                        conv_mean=conv_mean, conv_var=conv_var, attend=attend)
            for kind, i, _ in steps:
                if kind in work:
                    work[kind](i)
            columns(2)
            divide(3)
            columns(3)
            for m in range(KD):
                s = 4 * (m % 2)
                ve.wait_ge(gate_sig, m + 1)
                ve.wait_ge(br_ps, m + 1)
                ve.scalar_tensor_tensor(v2(gc[:, m, :]), ps[:, s:s + 2, 0:HALF], bco_c[:, m:m + 1], v2(gc[:, m, :]), ALU.add, ALU.mult)
                ve.tensor_tensor(v2(ga[:, m, :]), ps[:, s + 2:s + 4, 0:HALF], v2(ga[:, m, :]), ALU.mult).then_inc(br_used, 1)
                if m >= 3 and m < 7:
                    j = m - 3
                    ve.wait_ge(w_high, SPLIT + j + 1)
                    two = slice(2 * j, 2 * j + 2)
                    ve.tensor_tensor(wo_lo[:, two, :], wo[:, two, :], wo_hi[:, two, :].bitcast(F32), ALU.subtract).then_inc(w_split, 1)
            for m in range(KD):
                ve.wait_ge(x_high, 1 + m + 1)
                ve.tensor_tensor(ga_lo[:, m, :], ga[:, m, :], ga_hi[:, m, :].bitcast(F32), ALU.subtract).then_inc(x_split, 1)
            def statistics(rows, s, n, done):
                for half in range(2):
                    st = ve.bn_stats(stats[s][0:n, 6 * half:6 * half + 6], rows[:, half * 512:(half + 1) * 512])
                link(st)
                link(ve.bn_aggr(mv[s][0:n], stats[s][0:n, :]))
                ve.tensor_scalar(var_e[s][0:n], mv[s][0:n, 1:2], EPS, None, ALU.add).then_inc(done, 1)

            def scaling(s, n, done):
                link(ve.reciprocal(rs[s][0:n], sd[s][0:n]))
                ve.scalar_tensor_tensor(nmr[s][0:n], mv[s][0:n, 0:1], -1.0, rs[s][0:n], ALU.mult, ALU.mult).then_inc(done, 1)

            ve.wait_ge(rows1_loaded, 32)
            ve.wait_ge(br_loaded, 32)
            for t, (c0, n) in enumerate(TILES):
                s = t % 2
                ve.wait_ge(y_ps, t + 1)
                ve.wait_ge(xrow_loaded[s], 16 * (t // 2 + 1))
                if t >= 2:
                    ve.wait_ge(h_stored[s], 16 * (t // 2))
                    ve.wait_ge(ht_ps, t - 1)
                hs = hrow[0:n, s, :]
                ve.scalar_tensor_tensor(hs.rearrange("p (h n) -> p h n", h=2), xrow[0:n, s, :].rearrange("p (h n) -> p h n", h=2), ALPHA,
                                        ps[0:n, 2 * s:2 * s + 2, :], ALU.mult, ALU.add).then_inc(y_used, 1)
                ve.wait_ge(y_used, t + 1)
                statistics(hrow[0:n, s, :], s, n, hvar)
                ve.wait_ge(hsd, t + 1)
                scaling(s, n, hscale)
                ve.wait_ge(hnorm, t + 1)
                link(ve.tensor_tensor(hs, hs, g1row[0:n], ALU.mult))
                ve.tensor_tensor(hs, hs, b1row[0:n], ALU.add).then_inc(hdone, 1)
                if t >= 1:
                    c1, n1 = TILES[t - 1]
                    ve.wait_ge(lg_ps, t)
                    ve.tensor_tensor(lg[0:n1, t - 1, :], ps[0:n1, 6 + (t - 1) % 2, 0:36], br[0:n1], ALU.add).then_inc(lg_sb, 1)
            ve.wait_ge(lg_ps, NTT)
            ve.tensor_tensor(lg[0:NS, 4, :], ps[0:NS, 6, 0:36], br[0:NS], ALU.add).then_inc(lg_sb, 1)
            ve.wait_ge(lg_sb, NTT)

            def bc(x, shape):
                return x.to_broadcast(shape)

            S4, S32 = [P, NTT, NGRP], [P, NTT, NE]
            L4, L32 = lg[:, :, 0:4], lg[:, :, 4:36]
            link(ve.memset(rank, 0.0))
            link(ve.tensor_reduce(m1, L4, AX_X, ALU.max))
            link(ve.tensor_tensor(rt_a4, L4, bc(m1.unsqueeze(2), S4), ALU.is_equal))
            link(ve.tensor_scalar(rt_b4, iota_e[:, 0:4].unsqueeze(1).broadcast_to(S4), -64.0, None, ALU.add))
            link(ve.tensor_tensor(rt_c4, rt_b4, rt_a4, ALU.mult))
            link(ve.tensor_reduce(i1, rt_c4, AX_X, ALU.min))
            link(ve.tensor_tensor(rt_a4, rt_b4, bc(i1.unsqueeze(2), S4), ALU.is_equal))
            ve.tensor_tensor(rt_g3, L4, bc(m1.unsqueeze(2), S4), ALU.subtract).then_inc(rmax, 1)
            link(ve.tensor_scalar(rt_b4, rt_a4, -1.0, 1e30, ALU.add, ALU.mult))
            link(ve.tensor_tensor(em4, L32.rearrange("p t (g e) -> p t g e", g=NGRP),
                                  bc(rt_b4.unsqueeze(3), [P, NTT, NGRP, NPER]), ALU.add))
            link(ve.tensor_scalar(io32, iota_e.unsqueeze(1).broadcast_to(S32), -64.0, None, ALU.add))
            for k in range(2):
                link(ve.tensor_reduce(v12[:, k, :], em, AX_X, ALU.max))
                link(ve.tensor_tensor(rt32, em, bc(v12[:, k, :].unsqueeze(2), S32), ALU.is_equal))
                link(ve.tensor_tensor(rt32, rt32, io32, ALU.mult))
                link(ve.tensor_reduce(e12[:, k, :], rt32, AX_X, ALU.min))
                link(ve.tensor_tensor(oh[:, k], io32, bc(e12[:, k, :].unsqueeze(2), S32), ALU.is_equal))
                if k == 0:
                    link(ve.scalar_tensor_tensor(em, oh[:, 0], -3e38, em, ALU.mult, ALU.add))
            link(ve.tensor_tensor(mb, oh[:, 0], oh[:, 1], ALU.add))
            ve.nop().then_inc(mset, 1)
            ve.tensor_tensor(rt_d, v12[:, 1, :], v12[:, 0, :], ALU.subtract).then_inc(rmax, 1)
            for k in range(2):
                link(ve.tensor_tensor(rt32, oh[:, k], iota_e.unsqueeze(1).broadcast_to(S32), ALU.mult))
                link(ve.tensor_reduce(ek[:, :, k], rt32, AX_X, ALU.add))
            ve.wait_ge(rexp, 1)
            link(ve.tensor_reduce(i1, rt_g3, AX_X, ALU.add))
            ve.wait_ge(rexp, 2)
            link(ve.scalar_tensor_tensor(m1, rt_d, 1.0, i1, ALU.add, ALU.mult))
            link(ve.reciprocal(gw[:, 0, :], m1))
            link(ve.tensor_tensor(gw[:, 1, :], gw[:, 0, :], rt_d, ALU.mult))
            ve.wait_ge(cnt_ps, 1)
            link(ve.tensor_copy(cnt, ps[:, 1, 0:NE]))
            link(ve.tensor_scalar(nov, cnt, float(BLK), None, ALU.is_gt))
            for j in range(2, LEVELS + 1):
                link(ve.scalar_tensor_tensor(nov, cnt, float(j * BLK), nov, ALU.is_gt, ALU.add))
            link(ve.tensor_copy(ovend[:, 0, :], nov))
            cur = 0
            for sh in (1, 2, 4, 8, 16):
                ve.tensor_copy(ovend[:, 1 - cur, 0:sh], ovend[:, cur, 0:sh])
                link(ve.tensor_tensor(ovend[:, 1 - cur, sh:NE], ovend[:, cur, sh:NE], ovend[:, cur, 0:NE - sh], ALU.add))
                cur = 1 - cur
            oe = ovend[:, cur, :]
            link(ve.tensor_tensor(ovst, oe, nov, ALU.subtract))
            link(ve.tensor_copy(rank[:, 0:4, :], ps[:, 0, 0:4 * NE].rearrange("p (t e) -> p t e", e=NE)))
            link(ve.tensor_copy(rank[0:NS, 4, :], ps[0:NS, 0, 4 * NE:5 * NE]))
            for k in range(2):
                link(ve.tensor_tensor(rt32, oh[:, k], rank, ALU.mult))
                link(ve.tensor_reduce(rk[:, :, k], rt32, AX_X, ALU.add))
                link(ve.tensor_tensor(rt32, oh[:, k], ovst.unsqueeze(1).broadcast_to(S32), ALU.mult))
                link(ve.tensor_reduce(ok[:, :, k], rt32, AX_X, ALU.add))
            link(ve.tensor_scalar(qk, rk, float(BLK), None, ALU.is_ge))
            link(ve.tensor_copy(q0, qk))
            for j in range(2, LEVELS + 1):
                link(ve.scalar_tensor_tensor(qk, rk, float(j * BLK), qk, ALU.is_ge, ALU.add))
            link(ve.scalar_tensor_tensor(ok, qk, float(NE - 1), ok, ALU.add, ALU.add))
            link(ve.tensor_tensor(ok, ok, ek, ALU.subtract))
            link(ve.tensor_tensor(ok, ok, q0, ALU.mult))
            link(ve.tensor_tensor(ok, ok, ek, ALU.add))
            link(ve.scalar_tensor_tensor(rk, qk, -float(BLK), rk, ALU.mult, ALU.add))
            fl = lambda x: x.rearrange("p t k -> p (t k)")
            R3, B3 = [P, 2 * NTT, BLK], [P, 2 * NTT, NBLK]
            link(ve.tensor_tensor(ohr, iota_r.unsqueeze(1).broadcast_to(R3), fl(rk).unsqueeze(2).to_broadcast(R3), ALU.is_equal))
            link(ve.tensor_tensor(ohb, iota_b.unsqueeze(1).broadcast_to(B3), fl(ok).unsqueeze(2).to_broadcast(B3), ALU.is_equal))
            link(ve.tensor_tensor(ohb, ohb, fl(token).unsqueeze(2).to_broadcast(B3), ALU.mult))
            ve.nop().then_inc(sel_set, 1)
            ve.wait_ge(idx_ps, 1)
            tv, te = tabf[0:BLK, 0, :], tabf[0:BLK, 1, :]
            link(ve.tensor_scalar(tv, ps[0:BLK, 2, 0:NBLK], -1.0, None, ALU.add))
            link(ve.tensor_scalar(te, tv, 0.0, float(OOB), ALU.is_lt, ALU.mult))
            link(ve.tensor_tensor(te, te, tv, ALU.add))
            ve.tensor_copy(sidx[0:BLK, :], te)
            link(ve.tensor_scalar(tv, tv, float(N), -float(N), ALU.is_ge, ALU.mult))
            link(ve.tensor_tensor(tv, tv, te, ALU.add))
            ve.tensor_copy(gidx[0:BLK, :], tv).then_inc(idx_set, 1)
            for b in range(OVER):
                link(ve.tensor_scalar(tmp32, oe, float(b), None, ALU.is_le))
                link(ve.tensor_reduce(ovf[:, b:b + 1], tmp32, AX_X, ALU.add))
            link(ve.tensor_scalar(ovf[:, 0:OVER], ovf[:, 0:OVER], float(NE - 1), None, ALU.min))
            link(ve.tensor_copy(ovf[:, OVER:OVER + 1], oe[:, NE - 1:NE]))
            ve.tensor_copy(over_i[:, :], ovf).then_inc(over_set, 1)

            def rows_out(s):
                src = ps[:, 0:2, :].rearrange("p b (k c) -> p (b k) c", k=4)[:, :, 0:BLK]
                return ve.tensor_copy(xgt[s], src)

            ve.wait_ge(xgt_ps, 1)
            rows_out(0).then_inc(xgt_sb, 1)
            ve.nop().then_inc(hact_sb, 2)

            def expert(i, s):
                e = SLOTS * i + s
                if not (isinstance(i, int) and e == 0):
                    ve.wait_ge(dn_ps, e)
                for f in range(KF):
                    ve.wait_ge(gact_sb, e * KF + f + 1)
                    ve.tensor_tensor(hact[:, f, :], ps[:, 4 + f % 2, 0:BLK], gact[:, f, :], ALU.mult).then_inc(hact_sb, 1)
                if not (isinstance(i, int) and e == NE - 1):
                    ve.wait_ge(xgt_ps, e + 2)
                    rows_out((s + 1) % SLOTS).then_inc(xgt_sb, 1)

            for s in range(SLOTS):
                expert(0, s)
            with ve.Fori(1, ROUNDS) as i:
                for s in range(SLOTS):
                    expert(i, s)
            for s in range(NE % SLOTS):
                expert(ROUNDS, s)
            ve.wait_ge(over_set, 1)
            count = ve.value_load(over_i[0:1, OVER:OVER + 1], min_val=0, max_val=OVER)
            with ve.If(count > 0):
                with ve.Fori(0, count) as i:
                    ve.wait_ge(ov["tps"], i + 1)
                    rows_out(0).then_inc(ov["tsb"], 1)
                    for f in range(KF):
                        ve.wait_ge(ov["ga"], KF * i + f + 1)
                        ve.tensor_tensor(hact[:, f, :], ps[:, 4, 0:BLK], gact[:, f, :], ALU.mult).then_inc(ov["ha"], 1)

            def scale_row(t):
                n = TILES[t][1]
                ve.wait_ge(hnorm, NTT + t + 1)
                ve.tensor_tensor(fh[t][0:n], fh[t][0:n], g2row[0:n], ALU.mult).then_inc(fmul, 1)

            ve.wait_ge(rows2_loaded, 16 * 7)
            for t, (c0, n) in enumerate(TILES):
                s = t % 2
                ve.wait_ge(fin_loaded[s], 32 * (t // 2 + 1))
                ve.wait_ge(fweigh, t + 1)
                hs, y1, y2 = fh[t][0:n], fy1[s][0:n], fy2[s][0:n]
                link(ve.scalar_tensor_tensor(y1, y2, gw[0:n, 1, t:t + 1], y1, ALU.mult, ALU.add))
                ve.scalar_tensor_tensor(hs, hs, ALPHA, y1, ALU.mult, ALU.add).then_inc(fmix, 1)
                ve.wait_ge(fmix, t + 1)
                statistics(hs, s, n, hvar)
                if t >= 1:
                    scale_row(t - 1)
                ve.wait_ge(hsd, NTT + t + 1)
                scaling(s, n, hscale)
            scale_row(NTT - 1)

        @block.gpsimd
        def _(po):
            po.memset(onesm[:, :], 1.0 / CC)
            po.memset(uext[:, :, 0:PAD], 0.0).then_inc(pads_set, 1)
            po.memset(onesb[:, :], 1.0)
            po.memset(wa_t[:, 0:384], 0.0).then_inc(qbd_zero, 1)
            po.memset(logits[:, :], 0.0)
            po.wait_ge(ci_loaded, 16)
            po.tensor_copy(beforeb[:, :], before).then_inc(pads_set, 1)
            def low(n, s, c):
                po.wait_ge(w_high, n - 3)
                po.sem_inc(pool_steps, 1)
                tile = slice(c * P, (c + 1) * P)
                po.tensor_tensor(w_lo[:, s, :, tile], wring[:, s, :, tile], w_hi[:, s, :, tile].bitcast(F32), ALU.subtract).then_inc(w_split, 1)

            for n in range(4, 8):
                low(n, n // 2 % 2, n % 2)
            with po.Fori(0, 4) as i:
                for s in range(2):
                    for c in range(2):
                        low(8 + 4 * i + 2 * s + c, s, c)
            low(24, 0, 0)
            low(25, 0, 1)

            def load_cache(dst, b, two, done):
                c = caches
                po.dma_start(dst[:, 0, :], c[0][b, :, two].rearrange("s h e -> s (h e)")).then_inc(done, 16)
                po.dma_start(dst[:, 1:5, :], c[1][b, :, two].rearrange("(p t) h e -> p t (h e)", t=4)).then_inc(done, 16)
                po.dma_start(dst[:, 5, :], c[2][b, :, two].rearrange("(a t) h e -> a t (h e)", t=16)[:, 0:4, :]).then_inc(done, 16)

            po.wait_ge(tile_mm, 26)
            for b in range(2):
                load_cache(kc[:, b], b, 0, kc_loaded[b])
            po.wait_ge(rotated, 12)
            for b in range(2):
                load_cache(vc[:, b], b, 1, vc_loaded[b])
            for b in range(2, NB):
                po.wait_ge(kt_ps, b - 1)
                load_cache(kc[:, b % 2], b, 0, kc_loaded[b % 2])
            for b in range(2, NB):
                po.wait_ge(vs_used, b - 1)
                load_cache(vc[:, b % 2], b, 1, vc_loaded[b % 2])
            for m in range(KD):
                po.wait_ge(br_used, m + 1)
                po.tensor_tensor(ga[:, m, :], ga[:, m, :], gc[:, m, :], ALU.add).then_inc(merged, 1)
            po.memset(xt_t[:, 0:SLOTS * D], 0.0).then_inc(xg_zero, 1)
            for t, (c0, n) in enumerate(TILES):
                po.wait_ge(hdone, t + 1)
                po.dma_start(h_dram[c0:c0 + n], hrow[0:n, t % 2, :]).then_inc(h_stored[t % 2], 16)
            po.wait_ge(idx_set, 1)
            po.wait_ge(h_stored[0], 48)
            po.wait_ge(h_stored[1], 32)

            def gather(s, col, done, copied_sem, value):
                po.tensor_copy(idx_t[0:BLK, s:s + 1], gidx[0:BLK, col]).then_inc(copied_sem, 1)
                po.wait_ge(copied_sem, value)
                po.sem_inc(pool_steps, 1)
                po.indirect_dma_start(out=xg[s], out_offset=None, in_=h_dram,
                                      in_offset=bass.IndirectOffsetOnAxis(ap=idx_t[0:BLK, s:s + 1], axis=0),
                                      bounds_check=N - 1, oob_is_err=False).then_inc(done, 16)

            def scatter(s, col, done, copied_sem, value):
                po.tensor_copy(idx_t[0:BLK, SLOTS + s:SLOTS + s + 1], sidx[0:BLK, col]).then_inc(copied_sem, 1)
                po.wait_ge(copied_sem, value)
                po.sem_inc(pool_steps, 1)
                po.indirect_dma_start(out=y_dram, out_offset=bass.IndirectOffsetOnAxis(ap=idx_t[0:BLK, SLOTS + s:SLOTS + s + 1], axis=0),
                                      in_=yo[s], in_offset=None, bounds_check=2 * N - 1, oob_is_err=False).then_inc(done, 16)

            po.wait_ge(xg_zero, 1)
            for s in range(SLOTS):
                gather(s, slice(s, s + 1), gathered[s], idx_set_e, s + 1)

            def expert(i, s, ahead):
                e = SLOTS * i + s
                if ahead:
                    po.wait_ge(xgt_ps, e + 1)
                    gather(s, bass.ds(e + SLOTS, 1), gathered[s], idx_set_e, 2 * e + SLOTS + 1)
                po.wait_ge(yo_sb, e + 2)
                scatter(s, bass.ds(e, 1), scattered[s], idx_set_e, 2 * e + SLOTS + 2 if ahead else NE + e + 1)

            with po.Fori(0, ROUNDS - 1) as i:
                for s in range(SLOTS):
                    expert(i, s, True)
            for s in range(SLOTS):
                expert(ROUNDS - 1, s, s < NE % SLOTS)
            for s in range(NE % SLOTS):
                expert(ROUNDS, s, False)
            for s in range(SLOTS):
                blocks = (NE - s + SLOTS - 1) // SLOTS
                po.wait_ge(gathered[s], 16 * blocks)
                po.wait_ge(scattered[s], 16 * blocks)
            po.wait_ge(xgt_ps, NE)
            po.wait_ge(over_set, 1)
            count = po.value_load(over_i[0:1, OVER:OVER + 1], min_val=0, max_val=OVER)
            with po.If(count > 0):
                with po.Fori(0, count) as i:
                    gather(0, bass.ds(i + NE, 1), ov["gat"], ov["idx"], 2 * i + 1)
                    po.wait_ge(ov["yo"], i + 1)
                    scatter(0, bass.ds(i + NE, 1), ov["sca"], ov["idx"], 2 * i + 2)
                    po.wait_ge(ov["sca"], 16 * i + 16)
                    po.sem_inc(pool_steps, 1)
            po.nop().then_inc(over_done, 1)
            for t, (c0, n) in enumerate(TILES):
                po.wait_ge(fmul, t + 1)
                po.tensor_tensor(fh[t][0:n], fh[t][0:n], b2row[0:n], ALU.add).then_inc(fdone, 1)
            po.wait_ge(copied, 16 * 4 * NB)
            po.wait_ge(stored, 16 * STORES)
            for s in range(2):
                po.wait_ge(krow_stored[s], 16 * 3)


INPUTS = ['x_prompt', 'x_sample', 'cache_kv_w128', 'cache_kv_w512', 'cache_kv_w2048', 'state_conv', 'w_in', 'b_in', 'w_dw',
          'b_dw', 'conv_ln_g', 'conv_ln_b', 'w_conv_out', 'b_conv_out', 'w_attn_out', 'w_o', 'ln1_g', 'ln1_b',
          'w_router_group', 'b_router_group', 'w_router_expert', 'b_router_expert', 'w_expert_gate', 'w_expert_up',
          'w_expert_down', 'ln2_g', 'ln2_b']
OUTPUTS = [(1, SEQ, D), (NB, NT, D), (1, 1, 128, 2, 4, 64), (1, 1, 512, 2, 4, 64), (1, 1, 512, 2, 4, 64), (1, 1, PAD, CC),
           (1, NB, 128, 2, 4, 64), (1, NB, 512, 2, 4, 64), (1, NB, 516, 2, 4, 64), (1, NB, PAD, CC)]


def kernel(**inputs):
    from concourse import bacc
    from concourse.bass_utils import run_bass_kernel_spmd

    nc = bacc.Bacc("TRN2", target_bir_lowering=False, num_devices=1)
    arrays, args = {}, {}
    for name in INPUTS:
        arrays["in_" + name] = np.ascontiguousarray(inputs[name])
        args[name] = nc.dram_tensor("in_" + name, arrays["in_" + name].shape, F32, kind="ExternalInput").ap()
    arrays["in_constants"] = constants()
    args["constants"] = nc.dram_tensor("in_constants", arrays["in_constants"].shape, F32, kind="ExternalInput").ap()
    outs = [nc.dram_tensor(f"out_{i}", shape, F32, kind="ExternalOutput").ap() for i, shape in enumerate(OUTPUTS)]
    build(nc, args, outs)
    r = run_bass_kernel_spmd(nc, [arrays], core_ids=[0])
    return tuple(r.results[0][f"out_{i}"] for i in range(len(OUTPUTS)))
```
